# Optimizing a Trainium2 kernel written in Bass

```python
import jax, jax.numpy as jnp
from jax import lax
import numpy as np

D_MODEL = 1024
BATCH = 1
SEQ = 256
DEPTH = 1

GRID_W = 64
CTX_LEN = 256

MLA_HEADS = 8
MLA_Q_RANK = 256
MLA_KV_RANK = 256
MLA_NOPE = 64
MLA_ROPE = 32
MLA_V = 64
MLA_SCALE = (MLA_NOPE + MLA_ROPE) ** -0.5
Q_BLOCK = 128

RET_HEADS = 4
RET_DK = 128
RET_DV = 128
RET_CHUNK = 128

D_FF = 2816
CONV_WIDTH = 3

ROPE_BASE = 10000.0
EPS = 1e-6

MLA_WIDTH = MLA_HEADS * MLA_V
RET_WIDTH = RET_HEADS * RET_DV
MIX_WIDTH = MLA_WIDTH + RET_WIDTH
IN_SIZES = (MLA_Q_RANK, MLA_KV_RANK, MLA_ROPE, RET_HEADS * RET_DK, RET_HEADS * RET_DK, RET_WIDTH, RET_WIDTH)
IN_SPLITS = tuple(int(v) for v in np.cumsum(IN_SIZES)[:-1])
IN_COLS = int(sum(IN_SIZES))


def rmsnorm(x, g):
    xf = x.astype(jnp.float32)
    y = xf * lax.rsqrt(jnp.mean(xf * xf, axis=-1, keepdims=True) + EPS)
    return (y * g.astype(jnp.float32)).astype(x.dtype)

def modulate(h, shift, scale):
    return h * (1.0 + scale) + shift

def rope_angles(pos, dim):
    inv = ROPE_BASE ** (-jnp.arange(0, dim, 2, dtype=jnp.float32) / dim)
    return pos.astype(jnp.float32)[:, None] * inv[None, :]

def apply_rope(x, ang):
    x1, x2 = jnp.split(x, 2, axis=-1)
    cos = jnp.cos(ang)[None, :, None, :].astype(x.dtype)
    sin = jnp.sin(ang)[None, :, None, :].astype(x.dtype)
    return jnp.concatenate([x1 * cos - x2 * sin, x1 * sin + x2 * cos], axis=-1)

def axial_rope(x, pos):
    pos_row, pos_col = pos
    half = x.shape[-1] // 2
    xr = apply_rope(x[..., :half], rope_angles(pos_row, half))
    xc = apply_rope(x[..., half:], rope_angles(pos_col, half))
    return jnp.concatenate([xr, xc], axis=-1)

def split_proj(p):
    return jnp.split(p, IN_SPLITS, axis=-1)

def mla_queries(c_q, g_q, w_uq, pos):
    B, S, _ = c_q.shape
    q = (rmsnorm(c_q, g_q) @ w_uq).reshape(B, S, MLA_HEADS, MLA_NOPE + MLA_ROPE)
    q_nope, q_pe = q[..., :MLA_NOPE], q[..., MLA_NOPE:]
    if pos is not None:
        q_pe = axial_rope(q_pe, pos)
    return jnp.concatenate([q_nope, q_pe], axis=-1)

def mla_keys(c_kv, k_pe, g_kv, w_ukv, pos):
    B, S, _ = c_kv.shape
    kv = (rmsnorm(c_kv, g_kv) @ w_ukv).reshape(B, S, MLA_HEADS, MLA_NOPE + MLA_V)
    k_nope, v = kv[..., :MLA_NOPE], kv[..., MLA_NOPE:]
    k_pe = k_pe[:, :, None, :]
    if pos is not None:
        k_pe = axial_rope(k_pe, pos)
    k_pe = jnp.broadcast_to(k_pe, (B, S, MLA_HEADS, MLA_ROPE))
    return jnp.concatenate([k_nope, k_pe], axis=-1), v

def softmax_attention(q, k, v):
    s = jnp.einsum('bqhd,bkhd->bhqk', q, k).astype(jnp.float32) * MLA_SCALE
    p = jax.nn.softmax(s, axis=-1).astype(v.dtype)
    return jnp.einsum('bhqk,bkhd->bqhd', p, v)

def latent_attention(q, k_lat, v_lat, k_ctx, v_ctx):
    k = jnp.concatenate([k_lat, k_ctx], axis=1)
    v = jnp.concatenate([v_lat, v_ctx], axis=1)
    B, S, H, dq = q.shape
    qb = q.reshape(B, S // Q_BLOCK, Q_BLOCK, H, dq).swapaxes(0, 1)
    o = lax.map(lambda qi: softmax_attention(qi, k, v), qb)
    return o.swapaxes(0, 1).reshape(B, S, H * MLA_V)

def retention_inputs(rq, rk, rv, pos):
    B, S, _ = rq.shape
    q = rq.reshape(B, S, RET_HEADS, RET_DK)
    k = rk.reshape(B, S, RET_HEADS, RET_DK) * (RET_DK ** -0.5)
    v = rv.reshape(B, S, RET_HEADS, RET_DV)
    if pos is not None:
        ang = rope_angles(pos, RET_DK)
        q = apply_rope(q, ang)
        k = apply_rope(k, ang)
    return q, k, v

def retention_final_state(k, v, log_gamma, reverse):
    L = k.shape[1]
    j = jnp.arange(L, dtype=jnp.float32)
    expo = j if reverse else (L - 1.0 - j)
    w = jnp.exp(log_gamma[:, None] * expo[None, :])
    return jnp.einsum('bjhd,hj,bjhe->bhde', k.astype(jnp.float32), w, v.astype(jnp.float32))

def retention_chunkwise(q, k, v, log_gamma, init_state, strict):
    B, S, H, dk = q.shape
    dv = v.shape[-1]
    C = RET_CHUNK
    n = S // C
    idx = jnp.arange(C, dtype=jnp.float32)
    diff = idx[:, None] - idx[None, :]
    mask = (diff > 0) if strict else (diff >= 0)
    expo = jnp.where(mask, diff, 0.0)
    lg = log_gamma.astype(jnp.float32)
    decay_in = jnp.where(mask[None], jnp.exp(lg[:, None, None] * expo[None]), 0.0)
    xi = jnp.exp(lg[:, None] * (idx + 1.0)[None, :])[None, :, :, None]
    zeta = jnp.exp(lg[:, None] * (C - 1.0 - idx)[None, :])[None, :, :, None]
    g_chunk = jnp.exp(lg * C)[None, :, None, None]

    def to_chunks(a):
        return a.astype(jnp.float32).reshape(B, n, C, H, a.shape[-1]).transpose(1, 0, 3, 2, 4)

    def step(state, inp):
        qi, ki, vi = inp
        att = jnp.einsum('bhqd,bhkd->bhqk', qi, ki) * decay_in[None]
        inner = jnp.einsum('bhqk,bhke->bhqe', att, vi)
        cross = jnp.einsum('bhqd,bhde->bhqe', qi, state) * xi
        new_state = state * g_chunk + jnp.einsum('bhkd,bhke->bhde', ki * zeta, vi)
        return new_state, inner + cross

    _, out = lax.scan(step, init_state.astype(jnp.float32), (to_chunks(q), to_chunks(k), to_chunks(v)))
    return out.transpose(1, 0, 3, 2, 4).reshape(B, S, H, dv)

def head_groupnorm(y, g):
    B, S, H, dv = y.shape
    mu = jnp.mean(y, axis=-1, keepdims=True)
    var = jnp.mean(jnp.square(y - mu), axis=-1, keepdims=True)
    yn = ((y - mu) * lax.rsqrt(var + EPS)).reshape(B, S, H * dv)
    return yn * g.astype(jnp.float32)

def retention_bidir(q, k, v, gate, log_gamma, state_f, state_b, g_ret):
    flip = lambda a: jnp.flip(a, axis=1)
    y_f = retention_chunkwise(q, k, v, log_gamma[0], state_f, False)
    y_b = flip(retention_chunkwise(flip(q), flip(k), flip(v), log_gamma[1], state_b, True))
    y = head_groupnorm(y_f + y_b, g_ret)
    return (jax.nn.silu(gate.astype(jnp.float32)) * y).astype(v.dtype)

def conv_ffn(h, w_up, conv_w, conv_b, w_down):
    u = h @ w_up
    u = lax.conv_general_dilated(u, conv_w[:, None, :].astype(u.dtype), window_strides=(1,),
                                 padding=((CONV_WIDTH // 2, CONV_WIDTH // 2),),
                                 dimension_numbers=('NWC', 'WIO', 'NWC'),
                                 feature_group_count=u.shape[-1]) + conv_b
    a, g = jnp.split(u, 2, axis=-1)
    return (jax.nn.silu(g) * a) @ w_down

def first_inputs(seed: int = 0) -> dict:
    key = jax.random.key(seed)
    ks = jax.random.split(key, 21)
    nrm = lambda k, shape, scale: jax.random.normal(k, shape, jnp.float32) * scale
    h = jnp.arange(RET_HEADS, dtype=jnp.float32)
    decay_init = jnp.log(-jnp.log(1.0 - 2.0 ** (-5.0 - h)))
    return {
        'x': nrm(ks[0], (BATCH, SEQ, D_MODEL), 1.0),
        'c': nrm(ks[1], (BATCH, D_MODEL), 1.0),
        'ctx': nrm(ks[2], (BATCH, CTX_LEN, D_MODEL), 1.0),
        'c_ctx': nrm(ks[3], (D_MODEL,), 1.0),
        'w_ada': nrm(ks[4], (DEPTH, D_MODEL, 6 * D_MODEL), 0.5 * D_MODEL ** -0.5),
        'b_ada': nrm(ks[5], (DEPTH, 6 * D_MODEL), 0.02),
        'g_norm1': 1.0 + nrm(ks[6], (DEPTH, D_MODEL), 0.02),
        'w_in': nrm(ks[7], (DEPTH, D_MODEL, IN_COLS), D_MODEL ** -0.5),
        'g_q': 1.0 + nrm(ks[8], (DEPTH, MLA_Q_RANK), 0.02),
        'w_uq': nrm(ks[9], (DEPTH, MLA_Q_RANK, MLA_HEADS * (MLA_NOPE + MLA_ROPE)), MLA_Q_RANK ** -0.5),
        'g_kv': 1.0 + nrm(ks[10], (DEPTH, MLA_KV_RANK), 0.02),
        'w_ukv': nrm(ks[11], (DEPTH, MLA_KV_RANK, MLA_HEADS * (MLA_NOPE + MLA_V)), MLA_KV_RANK ** -0.5),
        'ret_decay': decay_init[None, None, :] + nrm(ks[12], (DEPTH, 2, RET_HEADS), 0.05),
        'g_ret': 1.0 + nrm(ks[13], (DEPTH, RET_WIDTH), 0.02),
        'w_out': nrm(ks[14], (DEPTH, MIX_WIDTH, D_MODEL), MIX_WIDTH ** -0.5),
        'g_norm2': 1.0 + nrm(ks[15], (DEPTH, D_MODEL), 0.02),
        'w_up': nrm(ks[16], (DEPTH, D_MODEL, 2 * D_FF), D_MODEL ** -0.5),
        'conv_w': nrm(ks[17], (DEPTH, CONV_WIDTH, 2 * D_FF), CONV_WIDTH ** -0.5),
        'conv_b': nrm(ks[18], (DEPTH, 2 * D_FF), 0.02),
        'w_down': nrm(ks[19], (DEPTH, D_FF, D_MODEL), D_FF ** -0.5),
        'g_final': 1.0 + nrm(ks[20], (D_MODEL,), 0.02),
    }

def first_block(x, c, ctx, c_ctx, w_ada, b_ada, g_norm1, w_in, g_q, w_uq, g_kv, w_ukv,
              ret_decay, g_ret, w_out, g_norm2, w_up, conv_w, conv_b, w_down, g_final):
    B, S, _ = x.shape
    rows = S // GRID_W
    pos_row = jnp.repeat(jnp.arange(rows, dtype=jnp.int32), GRID_W)
    pos_col = jnp.tile(jnp.arange(GRID_W, dtype=jnp.int32), rows)
    pos_grid = (pos_row, pos_col)
    pos_seq = jnp.arange(S, dtype=jnp.int32)

    for l in range(DEPTH):
        last = l == DEPTH - 1
        mod = jax.nn.silu(c) @ w_ada[l] + b_ada[l]
        sh1, sc1, gt1, sh2, sc2, gt2 = jnp.split(mod[:, None, :], 6, axis=-1)
        mod_c = jax.nn.silu(c_ctx) @ w_ada[l] + b_ada[l]
        shc1, scc1, gtc1, shc2, scc2, gtc2 = jnp.split(mod_c, 6)
        log_gamma = -jnp.exp(ret_decay[l].astype(jnp.float32))

        h = modulate(rmsnorm(x, g_norm1[l]), sh1, sc1)
        hc = modulate(rmsnorm(ctx, g_norm1[l]), shc1, scc1)
        cq, ckv, kpe, rq, rk, rv, rg = split_proj(h @ w_in[l])
        cq_c, ckv_c, kpe_c, rq_c, rk_c, rv_c, rg_c = split_proj(hc @ w_in[l])

        k_c, v_c = mla_keys(ckv_c, kpe_c, g_kv[l], w_ukv[l], None)
        qr_c, kr_c, vr_c = retention_inputs(rq_c, rk_c, rv_c, None)
        st_f = retention_final_state(kr_c, vr_c, log_gamma[0], False)
        st_b = retention_final_state(kr_c, vr_c, log_gamma[1], True)

        q = mla_queries(cq, g_q[l], w_uq[l], pos_grid)
        k, v = mla_keys(ckv, kpe, g_kv[l], w_ukv[l], pos_grid)
        o_mla = latent_attention(q, k, v, k_c, v_c)
        qr, kr, vr = retention_inputs(rq, rk, rv, pos_seq)
        o_ret = retention_bidir(qr, kr, vr, rg, log_gamma, st_f, st_b, g_ret[l])
        o = jnp.concatenate([o_mla, o_ret.astype(o_mla.dtype)], axis=-1) @ w_out[l]
        x_new = x + gt1 * o
        x_new = x_new + gt2 * conv_ffn(modulate(rmsnorm(x_new, g_norm2[l]), sh2, sc2),
                                       w_up[l], conv_w[l], conv_b[l], w_down[l])

        if not last:
            q_c = mla_queries(cq_c, g_q[l], w_uq[l], None)
            o_mla_c = softmax_attention(q_c, k_c, v_c).reshape(B, ctx.shape[1], MLA_WIDTH)
            zero_state = jnp.zeros_like(st_f)
            o_ret_c = retention_bidir(qr_c, kr_c, vr_c, rg_c, log_gamma, zero_state, zero_state, g_ret[l])
            o_c = jnp.concatenate([o_mla_c, o_ret_c.astype(o_mla_c.dtype)], axis=-1) @ w_out[l]
            ctx = ctx + gtc1 * o_c
            ctx = ctx + gtc2 * conv_ffn(modulate(rmsnorm(ctx, g_norm2[l]), shc2, scc2),
                                        w_up[l], conv_w[l], conv_b[l], w_down[l])
        x = x_new

    return rmsnorm(x, g_final)


CHUNK = 64
D_MIX = D_MODEL
SWA_HEAD_DIM = 64
SWA_HEADS = (D_MIX // 2) // SWA_HEAD_DIM
SWA_KV_HEADS = 2
SWA_WIDTH = SWA_HEADS * SWA_HEAD_DIM
SWA_KV_WIDTH = SWA_KV_HEADS * SWA_HEAD_DIM
WINDOW = 128
WINDOW_CHUNKS = WINDOW // CHUNK
HGRN_HEAD_DIM = 128
HGRN_WIDTH = D_MIX - SWA_WIDTH
HGRN_HEADS = HGRN_WIDTH // HGRN_HEAD_DIM
IN_SIZES_2 = (SWA_WIDTH, SWA_KV_WIDTH, SWA_KV_WIDTH,
            HGRN_WIDTH, HGRN_WIDTH, HGRN_WIDTH, HGRN_WIDTH)
D_IN = sum(IN_SIZES_2)
IN_SPLITS_2 = [int(v) for v in np.cumsum(IN_SIZES_2)[:-1]]
MEM_LEN = 256
XATTN_HEADS = 4
XATTN_HEAD_DIM = D_MODEL // XATTN_HEADS
D_FF_2 = ((8 * D_MODEL // 3 + 255) // 256) * 256
RMS_EPS = 1e-6
NEG_INF = -1e30


def rms_norm(x, g):
    xf = x.astype(jnp.float32)
    y = xf * lax.rsqrt(jnp.mean(xf * xf, axis=-1, keepdims=True) + RMS_EPS)
    return (y * g.astype(jnp.float32)).astype(x.dtype)

def swa_with_sinks(q, k, v, sinks):
    B, T, Hq, Dh = q.shape
    Hkv = k.shape[2]
    G = Hq // Hkv
    NC = T // CHUNK
    WC = WINDOW_CHUNKS
    L = (WC + 1) * CHUNK
    qc = q.reshape(B, NC, CHUNK, Hkv, G, Dh)
    pad = ((0, 0), (WC * CHUNK, 0), (0, 0), (0, 0))
    kc = jnp.pad(k, pad).reshape(B, NC + WC, CHUNK, Hkv, Dh)
    vc = jnp.pad(v, pad).reshape(B, NC + WC, CHUNK, Hkv, Dh)
    kband = jnp.concatenate([kc[:, j:j + NC] for j in range(WC + 1)], axis=2)
    vband = jnp.concatenate([vc[:, j:j + NC] for j in range(WC + 1)], axis=2)
    band_chunk = jnp.arange(NC)[:, None] - WC + jnp.arange(WC + 1)[None, :]
    valid = jnp.repeat(band_chunk >= 0, CHUNK, axis=1)
    s = jnp.einsum('bnqhgd,bnkhd->bnhgqk', qc, kband).astype(jnp.float32) * (Dh ** -0.5)
    s = jnp.where(valid[None, :, None, None, None, :], s, NEG_INF)
    sink = jnp.broadcast_to(sinks.astype(jnp.float32).reshape(1, 1, Hkv, G, 1, 1),
                            (B, NC, Hkv, G, CHUNK, 1))
    p = jax.nn.softmax(jnp.concatenate([s, sink], axis=-1), axis=-1)[..., :L]
    o = jnp.einsum('bnhgqk,bnkhd->bnqhgd', p.astype(v.dtype), vband)
    return o.reshape(B, T, Hq * Dh)

def hgrn2(q, f_logit, i, g, lb, onorm_g):
    B, T, H, Dk = q.shape
    Dv = i.shape[-1]
    NC = T // CHUNK
    f32 = jnp.float32
    qf = jax.nn.silu(q.astype(f32)) * (Dk ** -0.5)
    lbf = lb.astype(f32)
    f = lbf + (1.0 - lbf) * jax.nn.sigmoid(f_logit.astype(f32))
    kf = 1.0 - f
    logf = jnp.log(f)

    def chunks(a):
        return a.reshape(B, NC, CHUNK, H, a.shape[-1]).transpose(0, 3, 1, 2, 4)

    qc, kc, vc, lc = chunks(qf), chunks(kf), chunks(i.astype(f32)), chunks(logf)
    b = jnp.cumsum(lc, axis=3)
    b_mid = b[:, :, :, CHUNK // 2 - 1:CHUNK // 2]
    b_last = b[:, :, :, CHUNK - 1:CHUNK]
    A = jnp.einsum('bhnqd,bhnkd->bhnqk', qc * jnp.exp(b - b_mid), kc * jnp.exp(b_mid - b))
    causal = jnp.tril(jnp.ones((CHUNK, CHUNK), dtype=bool))
    A = jnp.where(causal, A, 0.0)
    o_intra = jnp.einsum('bhnqk,bhnkv->bhnqv', A, vc)
    kv = jnp.einsum('bhnkd,bhnkv->bhndv', kc * jnp.exp(b_last - b), vc)
    decay = jnp.exp(b_last[:, :, :, 0, :])

    def step(S, inp):
        d, u = inp
        return d[..., None] * S + u, S

    S0 = jnp.zeros((B, H, Dk, Dv), f32)
    _, S_prev = lax.scan(step, S0, (jnp.moveaxis(decay, 2, 0), jnp.moveaxis(kv, 2, 0)))
    S_prev = jnp.moveaxis(S_prev, 0, 2)
    o_inter = jnp.einsum('bhnqd,bhndv->bhnqv', qc * jnp.exp(b), S_prev)
    o = (o_intra + o_inter).transpose(0, 2, 3, 1, 4).reshape(B, T, H, Dv)
    o = rms_norm(o, onorm_g) * jax.nn.silu(g.astype(f32))
    return o.reshape(B, T, H * Dv).astype(q.dtype)

def cross_attention(u, m, wq, wk, wv, wo):
    B, T, _ = u.shape
    M = m.shape[1]
    q = (u @ wq).reshape(B, T, XATTN_HEADS, XATTN_HEAD_DIM)
    k = (m @ wk).reshape(B, M, XATTN_HEADS, XATTN_HEAD_DIM)
    v = (m @ wv).reshape(B, M, XATTN_HEADS, XATTN_HEAD_DIM)
    s = jnp.einsum('bthd,bmhd->bhtm', q, k).astype(jnp.float32) * (XATTN_HEAD_DIM ** -0.5)
    p = jax.nn.softmax(s, axis=-1).astype(v.dtype)
    o = jnp.einsum('bhtm,bmhd->bthd', p, v).reshape(B, T, D_MODEL)
    return o @ wo

def second_inputs(seed: int = 0) -> dict:
    key = jax.random.key(seed)
    ks = jax.random.split(key, 24)
    f32 = jnp.float32

    def nrm(k, shape, scale):
        return jax.random.normal(k, shape, f32) * scale

    def gain(k, shape):
        return 1.0 + 0.05 * jax.random.normal(k, shape, f32)

    return {
        "x": nrm(ks[0], (BATCH, SEQ, D_MODEL), 1.0),
        "mem": nrm(ks[1], (BATCH, MEM_LEN, D_MODEL), 1.0),
        "w_in": nrm(ks[2], (DEPTH, D_MODEL, D_IN), D_MODEL ** -0.5),
        "sinks": nrm(ks[3], (DEPTH, SWA_HEADS), 0.5),
        "hgrn_lb": nrm(ks[4], (DEPTH + 1, HGRN_WIDTH), 0.1),
        "hgrn_onorm": gain(ks[5], (DEPTH, HGRN_HEAD_DIM)),
        "w_out": nrm(ks[6], (DEPTH, D_MIX, D_MODEL), D_MIX ** -0.5),
        "g_mix_pre": gain(ks[7], (DEPTH, D_MODEL)),
        "g_mix_post": gain(ks[8], (DEPTH, D_MODEL)),
        "g_mem": gain(ks[9], (DEPTH, D_MODEL)),
        "g_x_pre": gain(ks[10], (DEPTH, D_MODEL)),
        "g_x_post": gain(ks[11], (DEPTH, D_MODEL)),
        "wq_x": nrm(ks[12], (DEPTH, D_MODEL, D_MODEL), D_MODEL ** -0.5),
        "wk_x": nrm(ks[13], (DEPTH, D_MODEL, D_MODEL), D_MODEL ** -0.5),
        "wv_x": nrm(ks[14], (DEPTH, D_MODEL, D_MODEL), D_MODEL ** -0.5),
        "wo_x": nrm(ks[15], (DEPTH, D_MODEL, D_MODEL), D_MODEL ** -0.5),
        "g_ffn_pre": gain(ks[16], (DEPTH, D_MODEL)),
        "g_ffn_post": gain(ks[17], (DEPTH, D_MODEL)),
        "w_gate": nrm(ks[18], (DEPTH, D_MODEL, D_FF_2), D_MODEL ** -0.5),
        "w_up": nrm(ks[19], (DEPTH, D_MODEL, D_FF_2), D_MODEL ** -0.5),
        "w_down": nrm(ks[20], (DEPTH, D_FF_2, D_MODEL), D_FF_2 ** -0.5),
    }

def second_block(x, mem, w_in, sinks, hgrn_lb, hgrn_onorm, w_out, g_mix_pre, g_mix_post,
              g_mem, g_x_pre, g_x_post, wq_x, wk_x, wv_x, wo_x, g_ffn_pre, g_ffn_post,
              w_gate, w_up, w_down):
    B, T, _ = x.shape
    lb_all = jnp.cumsum(jax.nn.softmax(hgrn_lb.astype(jnp.float32), axis=0), axis=0)
    h = x
    for l in range(DEPTH):
        u = rms_norm(h, g_mix_pre[l])
        z = u @ w_in[l]
        qa, ka, va, qh, fh, ih, gh = jnp.split(z, IN_SPLITS_2, axis=-1)
        ya = swa_with_sinks(qa.reshape(B, T, SWA_HEADS, SWA_HEAD_DIM),
                            ka.reshape(B, T, SWA_KV_HEADS, SWA_HEAD_DIM),
                            va.reshape(B, T, SWA_KV_HEADS, SWA_HEAD_DIM),
                            sinks[l])
        hv = HGRN_WIDTH // HGRN_HEADS
        yh = hgrn2(qh.reshape(B, T, HGRN_HEADS, HGRN_HEAD_DIM),
                   fh.reshape(B, T, HGRN_HEADS, HGRN_HEAD_DIM),
                   ih.reshape(B, T, HGRN_HEADS, hv),
                   gh.reshape(B, T, HGRN_HEADS, hv),
                   lb_all[l].reshape(HGRN_HEADS, HGRN_HEAD_DIM),
                   hgrn_onorm[l])
        y = jnp.concatenate([ya, yh.astype(ya.dtype)], axis=-1) @ w_out[l]
        h = h + rms_norm(y, g_mix_post[l])
        u = rms_norm(h, g_x_pre[l])
        m = rms_norm(mem, g_mem[l])
        y = cross_attention(u, m, wq_x[l], wk_x[l], wv_x[l], wo_x[l])
        h = h + rms_norm(y, g_x_post[l])
        u = rms_norm(h, g_ffn_pre[l])
        y = (jax.nn.silu(u @ w_gate[l]) * (u @ w_up[l])) @ w_down[l]
        h = h + rms_norm(y, g_ffn_post[l])
    return h


def setup_inputs(seed=0):
    out = dict(first_inputs(seed))
    for name, value in second_inputs(seed + 1).items():
        if name != "x":
            out[name + "_2"] = value
    return out


def reference(
    x, c, ctx, c_ctx, w_ada, b_ada, g_norm1, w_in, g_q, w_uq, g_kv, w_ukv, ret_decay, g_ret,
    w_out, g_norm2, w_up, conv_w, conv_b, w_down, g_final, mem_2, w_in_2, sinks_2, hgrn_lb_2,
    hgrn_onorm_2, w_out_2, g_mix_pre_2, g_mix_post_2, g_mem_2, g_x_pre_2, g_x_post_2, wq_x_2,
    wk_x_2, wv_x_2, wo_x_2, g_ffn_pre_2, g_ffn_post_2, w_gate_2, w_up_2, w_down_2,
):
    x = first_block(
        x, c, ctx, c_ctx, w_ada, b_ada, g_norm1, w_in, g_q, w_uq, g_kv, w_ukv, ret_decay, g_ret,
        w_out, g_norm2, w_up, conv_w, conv_b, w_down, g_final,
    )
    return second_block(
        x, mem_2, w_in_2, sinks_2, hgrn_lb_2, hgrn_onorm_2, w_out_2, g_mix_pre_2, g_mix_post_2,
        g_mem_2, g_x_pre_2, g_x_post_2, wq_x_2, wk_x_2, wv_x_2, wo_x_2, g_ffn_pre_2,
        g_ffn_post_2, w_gate_2, w_up_2, w_down_2,
    )


_drawn_inputs = setup_inputs


def setup_inputs(seed=0):
    import zlib

    import numpy as np

    out = dict(_drawn_inputs(seed))
    spreads = {}
    factors = {'g_norm1': 7.161,
     'g_q': 8.0,
     'g_kv': 8.0,
     'g_ret': 8.0,
     'g_norm2': 6.408,
     'conv_b': 6.005,
     'sinks_2': 64.0,
     'hgrn_lb_2': 5.966}
    for name, (base, spread) in spreads.items():
        noise = np.random.default_rng([zlib.crc32(name.encode()), seed]).standard_normal(out[name].shape)
        drawn = base * np.exp(spread * noise) if base else spread * noise
        out[name] = __import__('jax').numpy.asarray(drawn.astype(out[name].dtype))
    for name, factor in factors.items():
        out[name] = (out[name] * factor).astype(out[name].dtype)
    return out
```

```python
import math
from contextlib import ExitStack

import concourse.bass as bass
import numpy as np
from concourse import mybir

F32 = mybir.dt.float32
F32R = mybir.dt.float32r
U32 = mybir.dt.uint32
ALU = mybir.AluOpType
ACT = mybir.ActivationFunctionType
AX_X = mybir.AxisListType.X

P = 128
D = 1024
KD = D // P
T = 2
TOK = T * P
FF = 2816
KF = FF // P
NFF = KF // 2
EPS = 1e-6
MLA_H, NOPE, ROPE = 8, 64, 32
DQ = NOPE + ROPE
MLA_SCALE = DQ ** -0.5
RH, RD = 4, 128
RET_SCALE = RD ** -0.5
CH = 64
HH = 4
HG_SCALE = 128 ** -0.5
SWA_H = 8
SWA_SCALE = 64 ** -0.5
XH = 4
XD = 256
X_SCALE = XD ** -0.5

UNIT = 1024
NRAW = 6
NSPLIT = 3

C_ID = 0
C_RCOS = 128
C_RSIN = C_RCOS + T * 64
C_MCOS = C_RSIN + T * 64
C_MSIN = C_MCOS + T * ROPE
C_WEXP = C_MSIN + T * ROPE
C_PF = C_WEXP + 4
C_PB = C_PF + 512
C_XF = C_PB + 512
C_XB = C_XF + 256
C_E1 = C_XB + 256
C_SWA = C_E1
C_SCAN = C_SWA + 384
C_CAUS = C_SCAN + 256
C_END = C_CAUS + 512


def constants():
    c = np.zeros((P, C_END), np.float32)
    c[:, C_ID:C_ID + P] = np.eye(P)
    pos = np.arange(TOK)
    f32 = np.float32

    def angles(p, dim):
        inv = f32(10000.0) ** (-np.arange(0, dim, 2, dtype=f32) / f32(dim))
        return p.astype(f32)[:, None] * inv[None, :]

    a = angles(pos, RD)
    c[:, C_RCOS:C_RSIN] = np.cos(a).reshape(T, P, 64).transpose(1, 0, 2).reshape(P, -1)
    c[:, C_RSIN:C_MCOS] = np.sin(a).reshape(T, P, 64).transpose(1, 0, 2).reshape(P, -1)
    r, q = angles(pos // 64, 16), angles(pos % 64, 16)
    full = np.concatenate([r, r, q, q], axis=1)
    c[:, C_MCOS:C_MSIN] = np.cos(full).reshape(T, P, ROPE).transpose(1, 0, 2).reshape(P, -1)
    c[:, C_MSIN:C_WEXP] = np.sin(full).reshape(T, P, ROPE).transpose(1, 0, 2).reshape(P, -1)
    row = np.arange(P)
    for t in range(T):
        c[:, C_WEXP + t] = TOK - 1 - (t * P + row)
        c[:, C_WEXP + 2 + t] = t * P + row
        diff = pos[None, :] - (t * P + row)[:, None]
        c[:, C_PF + t * TOK:C_PF + (t + 1) * TOK] = np.maximum(diff, 0)
        c[:, C_PB + t * TOK:C_PB + (t + 1) * TOK] = np.maximum(-diff, 0)
    c[:, C_XF:C_XF + TOK] = pos + 1
    c[:, C_XB:C_XB + TOK] = TOK - pos
    chunk = row // CH
    for t in range(T):
        q_chunk = chunk + 2 * t
        k_chunk = np.arange((t + 1) * P) // CH
        seen = (k_chunk[None, :] <= q_chunk[:, None]) & (k_chunk[None, :] >= q_chunk[:, None] - 2)
        at = C_SWA + t * P
        c[:, at:at + (t + 1) * P] = np.where(seen, 0.0, -1e30)
    c[:, C_SCAN:C_SCAN + TOK] = (pos % CH != 0)
    causal = (row[None, :] >= row[:, None]) & (chunk[None, :] == chunk[:, None])
    c[:, C_CAUS:C_END] = np.tile(causal, (1, 4))
    return c


VEC = {}
VEC_GROUPS = (
    [("g_norm1", 8), ("g_norm2", 8), ("g_mix_pre_2", 8), ("g_mem_2", 8), ("g_x_pre_2", 8),
     ("g_ffn_pre_2", 8), ("g_q", 2), ("g_kv", 2), ("hgrn_lb_2", 8), ("c", 8), ("c_ctx", 8), ("b_ada", 48)],
    [("conv_b", 44), ("conv_w0", 44)],
    [("conv_w1", 44), ("conv_w2", 44)],
)
for _g, _vs in enumerate(VEC_GROUPS):
    _at = 0
    for _name, _n in _vs:
        VEC[_name] = (_g, _at, _n)
        _at += _n


def plan_panels(a):
    out = []

    def add(name, kind, matrix, c0, cols, kt=KD, nk=2):
        out.append((name, kind, kt, nk, cols, [(0, cols, matrix, c0)]))

    for p in range(2):
        add(f"wk{p}", "cols", a["wk_x_2"], 512 * p, 512)
    for p in range(2):
        add(f"wv{p}", "rows", a["wv_x_2"], 512 * p, 512)
    for p in range(4):
        add(f"ada{p}", "ada", a["w_ada"], 512 * p, 512)
    add("cqkv", "rows", a["w_in"], 0, 512)
    add("kpe", "rows", a["w_in"], 512, 32, nk=8)
    add("rk", "rows", a["w_in"], 544 + 512, 512)
    add("rv", "rows", a["w_in"], 544 + 1024, 512)
    add("rq", "rows", a["w_in"], 544, 512)
    add("rg", "rows", a["w_in"], 544 + 1536, 512)
    for p in range(4, 12):
        add(f"ada{p}", "ada", a["w_ada"], 512 * p, 512)
    for p in range(2):
        add(f"uq{p}", "rows", a["w_uq"], 384 * p, 384, kt=2)
    for p in range(2):
        add(f"ukv{p}", "rows", a["w_ukv"], 512 * p, 512, kt=2)
    for p in range(2):
        add(f"wout{p}", "rows", a["w_out"], 512 * p, 512)
    for p in range(NFF):
        w = a["w_up"]
        out.append((f"up{p}", "cols", KD, 2, 512, [(0, 256, w, 256 * p), (256, 256, w, FF + 256 * p)]))
    for p in range(2):
        add(f"down{p}", "rows", a["w_down"], 512 * p, 512, kt=KF)
    w = a["w_in_2"]
    add("qh", "cols", w, 768, 512)
    add("fh", "cols", w, 1280, 512)
    add("ih", "rows", w, 1792, 512)
    add("gh", "rows", w, 2304, 512)
    add("qa", "cols", w, 0, 512)
    add("kva", "kva", w, 512, 256, nk=4)
    for p in range(2):
        add(f"wout2_{p}", "rows", a["w_out_2"], 512 * p, 512)
    for p in range(2):
        add(f"wq{p}", "cols", a["wq_x_2"], 512 * p, 512)
    for p in range(2):
        add(f"wo{p}", "rows", a["wo_x_2"], 512 * p, 512)
    for p in range(NFF):
        out.append((f"gu{p}", "cols", KD, 2, 512,
                    [(0, 256, a["w_gate_2"], 256 * p), (256, 256, a["w_up_2"], 256 * p)]))
    for p in range(2):
        add(f"dn{p}", "rows", a["w_down_2"], 512 * p, 512, kt=KF)
    return out


NORMS = [("mem", D), ("ctx", D), ("x1", D), ("cq", 256), ("ckv", 256), ("ckvc", 256), ("x2", D),
         ("final", D), ("mix", D), ("mixpost", D), ("xpre", D), ("xpost", D), ("ffnpre", D), ("ffnpost", D)]
NORM = {name: n for n, (name, _) in enumerate(NORMS)}
POWS = ["mem", "ctx", "x1", "cq", "ckv", "ckvc", "ret", "x2", "final", "mix", "hgrn",
        "mixpost", "xpre", "xpost", "ffnpre", "ffnpost"]
POW = {name: n for n, name in enumerate(POWS)}

ROUNDS = ([("mla", t, h) for t in range(T) for h in range(MLA_H)]
          + [("swa", t, h) for t in range(T) for h in range(SWA_H)]
          + [("x", t, h) for t in range(T) for h in range(XH)])
ROUND = {r: n for n, r in enumerate(ROUNDS)}


def key_tiles(kind, t):
    return {"mla": 4, "swa": t + 1, "x": 2}[kind]


def group_of(r):
    kind, t, h = r
    per = 2 if kind == "x" else 8
    return (kind, t, h // per), h % per, h % per == per - 1


def build(nc, a, const, out):
    panels = plan_panels(a)
    units = []
    first_unit, last_unit = {}, {}
    for n, (name, kind, kt, nk, cols, sources) in enumerate(panels):
        first_unit[name] = len(units)
        for k0 in range(0, kt, nk):
            units.append((name, k0, nk, cols, sources))
        last_unit[name] = len(units) - 1
    ends = set(last_unit.values())
    inner = np.cumsum([u not in ends for u in range(len(units))]).tolist()

    with ExitStack() as ctx:
        base = (nc.sbuf_base + 63) // 64 * 64
        at = [base]
        top = [0]

        def sb(name, shape, dt=F32):
            nbytes = (int(np.prod(shape[1:])) * 4 + 31) // 32 * 32
            t = nc.alloc_sbuf_tensor_at(name, shape, dt, offset=at[0])
            at[0] += nbytes
            top[0] = max(top[0], at[0])
            return t

        raw = [sb(f"raw{i}", [P, UNIT]) for i in range(NRAW)]
        w_hi = [sb(f"w_hi{i}", [P, UNIT], F32R) for i in range(NSPLIT)]
        w_lo = [sb(f"w_lo{i}", [P, UNIT], F32R) for i in range(NSPLIT)]
        res = sb("res", [P, T, D])
        row = sb("row", [P, T, D])
        hT_hi = sb("hT_hi", [P, KD, TOK], F32R)
        hT_lo = sb("hT_lo", [P, KD, TOK], F32R)
        KxT = sb("KxT", [P, KD, TOK])
        Vx = sb("Vx", [P, T, D])
        junk = sb("junk", [P, D])
        fbuf = sb("fbuf", [P, 2, 2, TOK])
        ident = sb("ident", [P, P])
        vcol = [sb(f"vcol{g}", [P, sum(n for _, n in vs)]) for g, vs in enumerate(VEC_GROUPS)]
        NPOW = 8
        ssq = sb("ssq", [P, len(NORMS) * 2])
        var = sb("var", [P, len(POWS), NPOW])
        rstd = sb("rstd", [P, len(POWS), NPOW])
        mhalf = sb("mhalf", [P, NPOW])
        ones = sb("ones", [P, P])
        modc = sb("modc", [P, 6 * 8])
        modx = sb("modx", [P, 2 * 8])
        acol = sb("acol", [P, 3, 8])
        lbc = sb("lbc", [P, 6, HH])
        rowsum = sb("rowsum", [P, len(ROUNDS)])
        expsink = sb("expsink", [P, len(ROUNDS)])
        nmax = sb("nmax", [P, len(ROUNDS), 2])
        denom = sb("denom", [P, len(ROUNDS)])
        rinv = sb("rinv", [P, len(ROUNDS)])
        prob_at = at[0]
        prob = sb("prob", [P, 2, 512])
        probT = sb("probT", [P, 2, 512])
        epoch = at[0]
        at[0] = prob_at
        rstate = sb("rstate", [P, 2, 512])
        rtmp = sb("rtmp", [P, 2, 512])
        at[0] = epoch

        gate = sb("gate", [P, 2, D])
        gate_end = at[0]
        c_hi = sb("c_hi", [P, KD, P], F32R)
        c_lo = sb("c_lo", [P, KD, P], F32R)
        after_c = at[0]
        at[0] = gate_end
        q_row = sb("q_row", [P, T, MLA_H, DQ])
        at[0] = after_c
        csilu = sb("csilu", [P, 2, KD])
        modrow = sb("modrow", [P, 2, 512])
        k1 = sb("k1", [P, C_E1 - C_RCOS])
        g_ret = sb("g_ret", [P, 512])
        lgam = sb("lgam", [P, 8])
        wctx = sb("wctx", [P, 2, RH, T])
        cq_row = sb("cq_row", [P, T, 256])
        ckv_row = sb("ckv_row", [P, 2 * T, 256])
        kpe_row = sb("kpe_row", [P, 2 * T, ROPE])
        shared = at[0]
        hcT_hi = sb("hcT_hi", [P, KD, TOK], F32R)
        hcT_lo = sb("hcT_lo", [P, KD, TOK], F32R)
        after_hc = at[0]
        vrow = [sb(f"vrow{g}", [P, P]) for g in range(3)]
        in_mem = sb("in_mem", [P, T, D])
        in_ctx = sb("in_ctx", [P, T, D])
        at[0] = after_hc
        rk_row = sb("rk_row", [P, T, 512])
        rkf = sb("rkf", [P, T, 512])
        rkb = sb("rkb", [P, T, 512])
        rv_row = sb("rv_row", [P, T, 512])
        rvc_row = sb("rvc_row", [P, T, 512])
        rq_row = sb("rq_row", [P, T, 512])
        sgate = sb("sgate", [P, T, 512])
        decay = sb("decay", [P, RH, T, TOK])
        bn = sb("bn", [P, T, RH, 6])
        mv = sb("mv", [P, T, RH, 2])
        at[0] = shared
        rqT = sb("rqT", [P, RH, TOK])
        rkT = sb("rkT", [P, RH, TOK])
        xi = sb("xi", [P, RH, 2, TOK])
        at[0] = shared
        cqT_hi = sb("cqT_hi", [P, 2, TOK], F32R)
        cqT_lo = sb("cqT_lo", [P, 2, TOK], F32R)
        ckvT_hi = sb("ckvT_hi", [P, 2, 2 * TOK], F32R)
        ckvT_lo = sb("ckvT_lo", [P, 2, 2 * TOK], F32R)
        k_row = sb("k_row", [P, 2 * T, MLA_H // 2, DQ])
        V = sb("V", [P, 2 * T, MLA_H, 64])
        qT = sb("qT", [P, MLA_H, TOK])
        kT = sb("kT", [P, MLA_H, 2 * TOK])

        at[0] = gate_end
        act_hi = sb("act_hi", [P, KF, TOK], F32R)
        act_lo = sb("act_lo", [P, KF, TOK], F32R)
        conv = sb("conv", [P, 2, 2, 2, TOK])
        sg = sb("sg", [P, 2, 2, TOK])
        prod = sb("prod", [P, 2, 2, TOK])
        g_final = sb("g_final", [P, D])
        ffn_end = at[0]
        at[0] = ffn_end
        g_post = sb("g_post", [P, 3, D])
        hsq = sb("hsq", [P, T, HH])
        sinks = sb("sinks", [P, SWA_H])
        at[0] = epoch
        k3 = sb("k3", [P, C_END - C_E1])
        onorm = sb("onorm", [P, P])
        aqT = sb("aqT", [P, 4, TOK])
        akT = sb("akT", [P, 2, TOK])
        av = sb("av", [P, T, P])
        qs = sb("qs", [P, HH, TOK])
        kk_ = sb("kk_", [P, HH, TOK])
        logf = sb("logf", [P, HH, TOK])
        cum = sb("cum", [P, HH, TOK])
        bmid = sb("bmid", [P, HH, TOK])
        e_b = sb("e_b", [P, HH, TOK])
        qd = sb("qd", [P, HH, TOK])
        kz_row = sb("kz_row", [P, T, 512])
        hi_row = sb("hi_row", [P, T, 512])
        hg = sb("hg", [P, T, 512])
        AT = sb("AT", [P, T, 512])
        state = sb("state", [P, 3, 512])
        sxqT = sb("sxqT", [P, KD, TOK])
        assert at[0] <= ffn_end, (at[0], ffn_end)
        assert top[0] <= nc.sbuf_usable_end, (top[0], nc.sbuf_usable_end)

        bank = [ctx.enter_context(nc.psum_tensor(f"bank{i}", [P, 512], F32)) for i in range(8)]

        def sem(name):
            return ctx.enter_context(nc.semaphore(name))

        raw_landed = [sem(f"raw_landed{i}") for i in range(NRAW)]
        w_hi_ready = sem("w_hi_ready")
        w_lo_ready = sem("w_lo_ready")
        w_used = sem("w_used")
        filled = [sem(f"filled{i}") for i in range(8)]
        freed = [sem(f"freed{i}") for i in range(8)]
        act_step = sem("act_step")
        dve_step = sem("dve_step")
        in_vec = sem("in_vec")
        in_conv = sem("in_conv")
        in_ident = sem("in_ident")
        in_k1 = sem("in_k1")
        in_decay = sem("in_decay")
        in_memx = sem("in_memx")
        in_ctxx = sem("in_ctxx")
        in_x = sem("in_x")
        in_gate = sem("in_gate")
        in_gains = sem("in_gains")
        in_k3 = sem("in_k3")
        ones_ready = sem("ones_ready")
        csilu_ready = sem("csilu_ready")
        c_hi_ready = sem("c_hi_ready")
        c_lo_ready = sem("c_lo_ready")
        lb_in_ready = sem("lb_in_ready")
        lb_exp_ready = sem("lb_exp_ready")
        ssq_ready = sem("ssq_ready")
        var_ready = sem("var_ready")
        rstd_ready = sem("rstd_ready")
        row_ready = sem("row_ready")
        turn_hi = sem("turn_hi")
        turn_lo = sem("turn_lo")
        ret_row_ready = sem("ret_row_ready")
        wctx_ready = sem("wctx_ready")
        decay_ready = sem("decay_ready")
        decay_exp_ready = sem("decay_exp_ready")
        xi_ready = sem("xi_ready")
        qx_ready = sem("qx_ready")
        ret_out_ready = sem("ret_out_ready")
        q_row_ready = sem("q_row_ready")
        kpe_ready = sem("kpe_ready")
        nmax_ready = sem("nmax_ready")
        exp_ready = sem("exp_ready")
        pv_done = sem("pv_done")
        res_ready = sem("res_ready")
        conv_ready = sem("conv_ready")
        sg_ready = sem("sg_ready")
        prod_ready = sem("prod_ready")
        act_hi_ready = sem("act_hi_ready")
        act_lo_ready = sem("act_lo_ready")
        sig_ready = sem("sig_ready")
        f_ready = sem("f_ready")
        log_ready = sem("log_ready")
        cum_ready = sem("cum_ready")
        hexp_ready = sem("hexp_ready")
        hd_ready = sem("hd_ready")
        hsq_ready = sem("hsq_ready")
        hgrn_out_ready = sem("hgrn_out_ready")
        stored = sem("stored")

        place, uses = {}, [0] * 8

        def ready(eng, name):
            b, n = place[name]
            eng.wait_ge(filled[b], n + 1)

        def emptied(eng, name):
            b, n = place[name]
            eng.wait_ge(freed[b], n + 1)

        def ps(name):
            return bank[place[name][0]]

        def free(ins, name):
            ins.then_inc(freed[place[name][0]], 1)

        def vec(name, k=None):
            g, c, n = VEC[name]
            return vcol[g][:, c:c + n] if k is None else vcol[g][:, c + k:c + k + 1]

        def multiplied(eng, i):
            group, _, last = group_of(ROUNDS[i])
            if last:
                ready(eng, ("o",) + group)
            else:
                eng.wait_ge(pv_done, sum(not group_of(r)[2] for r in ROUNDS[:i + 1]))

        vec_src = {}
        for vs in VEC_GROUPS:
            for name, n in vs:
                if name.startswith("conv_w"):
                    v = a["conv_w"][int(name[-1]), :]
                elif name == "hgrn_lb_2":
                    v = a[name].rearrange("l n -> (l n)")
                else:
                    v = a[name]
                vec_src[name] = v.rearrange("(r p) -> r p", p=P)

        def unit_view(t, u):
            _, _, nk, cols, _ = units[u]
            return t[:, 0:nk * cols]

        def released(eng, u):
            if u in ends:
                ready(eng, ("end", units[u][0]))
            else:
                eng.wait_ge(w_used, inner[u])

        TURNS = [("mem", KD, True), ("ctx", KD, True), ("x1", KD, True), ("cq", 2, True), ("ckv", 2, True),
                 ("ckvc", 2, True), ("o", KD, False), ("x2", KD, True), ("mix", KD, True),
                 ("o2", KD, False), ("xpre", KD, True), ("xo", KD, False), ("ffnpre", KD, True)]
        turn_hi_at, turn_lo_at = {}, {}
        nh = nl = 0
        for name, kt, scaled in TURNS:
            for p in range(kt // 2):
                nh += 1
                turn_hi_at[name, p] = nh
                nl += scaled
                turn_lo_at[name, p] = nl if scaled else None

        def turned(eng, name, p):
            if turn_lo_at[name, p] is None:
                emptied(eng, ("turn", name, p))
            else:
                eng.wait_ge(turn_lo, turn_lo_at[name, p])

        TURN_SRC = {"cq": lambda t, k: cq_row[:, t, k * P:(k + 1) * P],
                    "ckv": lambda t, k: ckv_row[:, t, k * P:(k + 1) * P],
                    "ckvc": lambda t, k: ckv_row[:, T + t, k * P:(k + 1) * P]}

        def turn_src(name):
            return TURN_SRC.get(name, lambda t, k: row[:, t, k * P:(k + 1) * P])

        def turn_dst(name):
            if name in ("mem", "ctx"):
                return hcT_hi, hcT_lo, 0
            if name == "cq":
                return cqT_hi, cqT_lo, 0
            if name in ("ckv", "ckvc"):
                return ckvT_hi, ckvT_lo, TOK * (name == "ckvc")
            return hT_hi, hT_lo, 0

        def turn_gain(name, k):
            if name in ("x1", "x2", "ctx"):
                n = {"x1": 0, "x2": 1, "ctx": 2}[name]
                shift = modx[:, k:k + 1] if name == "ctx" else modc[:, 24 * n + k:24 * n + k + 1]
                return acol[:, n, k:k + 1], shift
            gain = {"mem": "g_mem_2", "cq": "g_q", "ckv": "g_kv", "ckvc": "g_kv", "mix": "g_mix_pre_2",
                    "xpre": "g_x_pre_2", "ffnpre": "g_ffn_pre_2"}[name]
            return vec(gain, k), None

        NORM_ROWS = ["mem", "ctx", "x1", "cq", "ckv", "ckvc", "x2", "mix", "xpre", "ffnpre"]
        RES = {"wout": 4, "down": 8, "final": 10, "mixpost": 12, "xpost": 14, "ffnpost": 16}
        landed = {}

        block = ctx.enter_context(nc.Block())

        @block.tensor
        def _(pe):
            def claim(name, b):
                if uses[b]:
                    pe.wait_ge(freed[b], uses[b])
                place[name] = (b, uses[b])
                uses[b] += 1
                return bank[b]

            def fill(ins, name):
                ins.then_inc(filled[place[name][0]], 1)

            small = [0]

            def next_small():
                small[0] += 1
                return 4 + small[0] % 4

            side = [0]

            def next_side():
                side[0] ^= 1
                return 2 * side[0]

            def three(o, xh, xl, yh, yl, first, last, skip=False):
                pe.matmul(o, xh, yh, start=first, stop=False, skip_group_check=skip)
                pe.matmul(o, xh, yl, start=False, stop=False, skip_group_check=skip)
                return pe.matmul(o, xl, yh, start=False, stop=last, skip_group_check=skip)

            def panel(name, outs, step, before=None):
                _, kind, kt, nk, cols, _ = next(x for x in panels if x[0] == name)
                place[("end", name)] = place[outs[-1]]
                for u in range(first_unit[name], last_unit[name] + 1):
                    k0 = units[u][1]
                    if before is not None:
                        for k in range(k0, k0 + nk):
                            before(k)
                    pe.wait_ge(w_lo_ready, u + 1)
                    hi = unit_view(w_hi[u % NSPLIT], u).rearrange("p (k n) -> p k n", k=nk)
                    lo = unit_view(w_lo[u % NSPLIT], u).rearrange("p (k n) -> p k n", k=nk)
                    final = u == last_unit[name]
                    for use in outs:
                        for kk in range(nk):
                            k = k0 + kk
                            ins = step(k, use, hi[:, kk, :], lo[:, kk, :], k == 0, k == kt - 1)
                        if final:
                            fill(ins, use)
                    if not final:
                        ins.then_inc(w_used, 1)

            def rows_panel(name, xh, xl, before=None, ctxT=None, ctx_from=0):
                outs = []
                b = next_side() if ctxT is None else 0
                for t in range(T):
                    outs.append((name, t))
                    claim(outs[-1], b + t)
                if ctxT is not None:
                    side[0] = 1
                    for t in range(T):
                        outs.append((name, T + t))
                        claim(outs[-1], 2 + t)

                def step(k, use, hi, lo, first, last):
                    t = use[1]
                    sh, sl, c = (xh, xl, 0) if t < T else (ctxT[0], ctxT[1], ctx_from)
                    s = slice((t % T) * P, (t % T + 1) * P)
                    o = ps(use)[:, c:hi.shape[1]] if c else ps(use)[:, 0:hi.shape[1]]
                    return three(o, sh[:, k, s], sl[:, k, s], hi[:, c:], lo[:, c:], first, last)

                panel(name, outs, step, before)

            def cols_panel(name, xh, xl, before=None):
                outs = [(name, 0), (name, 1)]
                b = next_side()
                for j in range(2):
                    claim(outs[j], b + j)

                def step(k, use, hi, lo, first, last):
                    for n in range(2):
                        c = (2 * use[1] + n) * P
                        o = ps(use)[:, n * TOK:(n + 1) * TOK]
                        f = first and n == 0
                        pe.matmul(o, hi[:, c:c + P], xh[:, k, :], start=f, stop=False, skip_group_check=True)
                        pe.matmul(o, lo[:, c:c + P], xh[:, k, :], start=False, stop=False, skip_group_check=True)
                        ins = pe.matmul(o, hi[:, c:c + P], xl[:, k, :], start=False, stop=last,
                                        skip_group_check=True)
                    return ins

                panel(name, outs, step, before)

            def turn(name, wait_src):
                src = turn_src(name)
                kt = next(x[1] for x in TURNS if x[0] == name)
                wait_src()
                for p in range(kt // 2):
                    use = ("turn", name, p)
                    o = claim(use, next_small())
                    for kk in range(2):
                        for t in range(T):
                            c = (kk * T + t) * P
                            ins = pe.transpose(o[:, c:c + P], src(t, 2 * p + kk), ident[:, :])
                    fill(ins, use)

            def turn_before(name):
                done = set()

                def before(k):
                    if k // 2 not in done:
                        done.add(k // 2)
                        turned(pe, name, k // 2)
                return before

            def rows_scaled(name):
                return lambda: pe.wait_ge(row_ready, T * (NORM_ROWS.index(name) + 1))

            pe.wait_ge(in_ident, 16)
            for g, vs in enumerate(VEC_GROUPS):
                n = sum(m for _, m in vs)
                o = claim(("vec", g), next_small())
                pe.wait_ge(in_conv if g else in_vec, 16 * (4 if g else 12))
                fill(pe.transpose(o[:, 0:n], vrow[g][0:n, :], ident[0:n, 0:n]), ("vec", g))

            turn("mem", rows_scaled("mem"))
            for p in range(2):
                cols_panel(f"wk{p}", hcT_hi, hcT_lo, turn_before("mem"))
            for p in range(2):
                rows_panel(f"wv{p}", hcT_hi, hcT_lo)

            def ada(p):
                name = f"ada{p}"
                use = (name, 0)
                claim(use, (0, 2, 1, 3)[p % 4])

                def step(k, use, hi, lo, first, last):
                    return three(ps(use)[:, :], c_hi[:, k, :], c_lo[:, k, :], hi, lo, first, last)

                pe.wait_ge(c_lo_ready, 2)
                panel(name, [use], step)

            def ada_spread(p):
                emptied(pe, (f"ada{p}", 0))
                use = ("spread", p)
                o = claim(use, next_small())
                m = modrow[:, p % 2, :]
                if p in (4, 5, 10, 11):
                    fill(pe.matmul(o[:, :], ones[0:1, :], m[0:1, :], start=True, stop=True), use)
                    return
                for j in range(4):
                    ins = pe.matmul(o[:, j:j + 1], m[0:1, j * P:(j + 1) * P], ones[0:1, 0:1],
                                    start=True, stop=True)
                fill(ins, use)
                if p < 4:
                    use = ("spread_ctx", p)
                    o = claim(use, next_small())
                    for j in range(4):
                        ins = pe.matmul(o[:, j:j + 1], m[64:65, j * P:(j + 1) * P], ones[64:65, 0:1],
                                        start=True, stop=True)
                    fill(ins, use)

            pe.wait_ge(ones_ready, 2)
            for p in range(4):
                ada(p)
                if p:
                    ada_spread(p - 1)
            ada_spread(3)
            turn("ctx", rows_scaled("ctx"))
            turn("x1", rows_scaled("x1"))

            cT = (hcT_hi, hcT_lo)
            before_x, before_c = turn_before("x1"), turn_before("ctx")

            def before_both(k):
                before_x(k)
                before_c(k)

            rows_panel("cqkv", hT_hi, hT_lo, before_both, cT, 256)
            rows_panel("kpe", hT_hi, hT_lo, None, cT)
            rows_panel("rk", hT_hi, hT_lo, None, cT)
            rows_panel("rv", hT_hi, hT_lo, None, cT)
            rows_panel("rq", hT_hi, hT_lo)
            rows_panel("rg", hT_hi, hT_lo)
            for p in range(4, 12):
                ada(p)
                if p > 4:
                    ada_spread(p - 1)
            ada_spread(11)

            for what, src in (("rk", rk_row), ("rq", rq_row)):
                for t in range(T):
                    use = ("rT", what, t)
                    o = claim(use, next_small())
                    pe.wait_ge(ret_row_ready, 2 * (what == "rq") + t + 1)
                    for h in range(RH):
                        ins = pe.transpose(o[:, h * P:(h + 1) * P], src[:, t, h * P:(h + 1) * P], ident[:, :])
                    fill(ins, use)
            for d, kd in enumerate((rkf, rkb)):
                use = ("rstate", d)
                o = claim(use, next_small())
                for t in range(T):
                    emptied(pe, ("rk", T + t))
                    emptied(pe, ("rv", T + t))
                for h in range(RH):
                    for j in range(T):
                        ins = pe.matmul(o[:, h * P:(h + 1) * P], kd[:, j, h * P:(h + 1) * P],
                                        rvc_row[:, j, h * P:(h + 1) * P], start=j == 0, stop=j == T - 1)
                fill(ins, use)
            for what in ("rk", "rq"):
                for t in range(T):
                    emptied(pe, ("rT", what, t))
            for h in range(RH):
                use = ("ratt", h)
                o = claim(use, next_small())
                for j in range(T):
                    ins = pe.matmul(o[:, j * TOK:(j + 1) * TOK], rkT[:, h, j * P:(j + 1) * P], rqT[:, h, :],
                                    start=True, stop=True)
                fill(ins, use)
            for t in range(T):
                use = ("ret", t)
                o = claim(use, next_small())
                for h in range(RH):
                    emptied(pe, ("ratt", h))
                for d in range(2):
                    emptied(pe, ("rstate", d))
                    emptied(pe, ("rv", d))
                pe.wait_ge(qx_ready, 2)
                s = slice(t * P, (t + 1) * P)
                for h in range(RH):
                    c = slice(h * P, (h + 1) * P)
                    pe.matmul(o[:, c], decay[:, h, 0, s], rv_row[:, 0, c], start=True, stop=False)
                    pe.matmul(o[:, c], decay[:, h, 1, s], rv_row[:, 1, c], start=False, stop=False)
                    pe.matmul(o[:, c], xi[:, h, 0, s], rstate[:, 0, c], start=False, stop=False)
                    ins = pe.matmul(o[:, c], xi[:, h, 1, s], rstate[:, 1, c], start=False, stop=True)
                fill(ins, use)

            for name in ("cq", "ckv", "ckvc"):
                turn(name, rows_scaled(name))
            for p in range(2):
                rows_panel(f"uq{p}", cqT_hi, cqT_lo, turn_before("cq"))
            for t in range(T):
                for p in range(2):
                    use = ("qT", t, p)
                    o = claim(use, next_small())
                    pe.wait_ge(q_row_ready, t + 1)
                    for h in range(4):
                        ins = pe.transpose(o[0:DQ, h * P:(h + 1) * P], q_row[:, t, 4 * p + h, :], ident[:, :])
                    fill(ins, use)
            for p in range(2):
                name = f"ukv{p}"
                b4 = turn_before("ckv")
                c4 = turn_before("ckvc")

                def both(k, b4=b4, c4=c4):
                    b4(k)
                    c4(k)
                rows_panel(name, ckvT_hi[:, :, 0:TOK], ckvT_lo[:, :, 0:TOK], both,
                           (ckvT_hi[:, :, TOK:], ckvT_lo[:, :, TOK:]))
                for t in range(2 * T):
                    use = ("kT", p, t)
                    o = claim(use, next_small())
                    emptied(pe, (name, t))
                    pe.wait_ge(kpe_ready, 2 * T)
                    for h in range(4):
                        ins = pe.transpose(o[0:DQ, h * P:(h + 1) * P], k_row[:, t, h, :], ident[:, :])
                    fill(ins, use)

            def attend(kind):
                rounds = [r for r in ROUNDS if r[0] == kind]

                def score(r):
                    i = ROUND[r]
                    _, t, h = r
                    use = ("score",) + r
                    o = claim(use, 4 + i % 2)
                    s = slice(t * P, (t + 1) * P)
                    if kind == "mla":
                        ins = pe.matmul(o[:, :], qT[0:DQ, h, s], kT[0:DQ, h, :], start=True, stop=True)
                    elif kind == "swa":
                        b = slice(64 * (h % 2), 64 * (h % 2) + 64)
                        ins = pe.matmul(o[:, 0:(t + 1) * P], aqT[b, h // 2, s], akT[b, h // 4, 0:(t + 1) * P],
                                        start=True, stop=True)
                    else:
                        pe.matmul(o[:, 0:TOK], sxqT[:, 2 * h, s], KxT[:, 2 * h, :], start=True, stop=False)
                        ins = pe.matmul(o[:, 0:TOK], sxqT[:, 2 * h + 1, s], KxT[:, 2 * h + 1, :],
                                        start=False, stop=True)
                    fill(ins, use)

                score(rounds[0])
                for n, r in enumerate(rounds):
                    if n + 1 < len(rounds):
                        score(rounds[n + 1])
                    i = ROUND[r]
                    _, t, h = r
                    nk = key_tiles(kind, t)
                    use = ("probT",) + r
                    o = claim(use, 6)
                    if kind == "swa":
                        pe.wait_ge(exp_ready, i - ROUND[rounds[0]] + 1)
                    else:
                        emptied(pe, ("score",) + r)
                    for j in range(nk):
                        ins = pe.transpose(o[:, j * P:(j + 1) * P], prob[:, i % 2, j * P:(j + 1) * P], ident[:, :])
                    fill(ins, use)
                    group, at_, last = group_of(r)
                    if at_ == 0:
                        claim(("o",) + group, 7)
                    o = ps(("o",) + group)
                    w = XD if kind == "x" else 64
                    emptied(pe, use)
                    for j in range(nk):
                        v = {"mla": lambda: V[:, j, h, :], "swa": lambda: av[:, j, 64 * (h // 4):64 * (h // 4) + 64],
                             "x": lambda: Vx[:, j, h * XD:(h + 1) * XD]}[kind]()
                        ins = pe.matmul(o[:, at_ * w:(at_ + 1) * w], probT[:, i % 2, j * P:(j + 1) * P], v,
                                        start=j == 0, stop=j == nk - 1)
                    if last:
                        fill(ins, ("o",) + group)
                    else:
                        ins.then_inc(pv_done, 1)

            for t in range(T):
                for p in range(2):
                    emptied(pe, ("qT", t, p))
            for p in range(2):
                for t in range(2 * T):
                    emptied(pe, ("kT", p, t))
            attend("mla")

            def mixed(kind, sem_):
                for t in range(T):
                    emptied(pe, ("o", kind, t, 0))
                pe.wait_ge(sem_, T)

            turn("o", lambda: mixed("mla", ret_out_ready))
            for p in range(2):
                rows_panel(f"wout{p}", hT_hi, hT_lo, turn_before("o"))

            def ffn(up, down, pre, gen):
                turn(pre, rows_scaled(pre))
                for p in range(NFF):
                    cols_panel(f"{up}{p}", hT_hi, hT_lo, turn_before(pre) if p == 0 else None)

                def before(k):
                    if k % 2 == 0:
                        pe.wait_ge(act_lo_ready, NFF * gen + k // 2 + 1)
                rows_panel(f"{down}0", act_hi, act_lo, before)
                rows_panel(f"{down}1", act_hi, act_lo)

            ffn("up", "down", "x2", 0)

            turn("mix", rows_scaled("mix"))
            cols_panel("qh", hT_hi, hT_lo, turn_before("mix"))
            cols_panel("fh", hT_hi, hT_lo)
            rows_panel("ih", hT_hi, hT_lo)
            rows_panel("gh", hT_hi, hT_lo)
            cols_panel("qa", hT_hi, hT_lo)
            b = next_side()
            claim(("kva", 0), b)
            claim(("kva", 1), b + 1)

            def step(k, use, hi, lo, first, last):
                if use[1] == 0:
                    o = ps(use)[:, 0:TOK]
                    pe.matmul(o, hi[:, 0:P], hT_hi[:, k, :], start=first, stop=False)
                    pe.matmul(o, lo[:, 0:P], hT_hi[:, k, :], start=False, stop=False)
                    return pe.matmul(o, hi[:, 0:P], hT_lo[:, k, :], start=False, stop=last)
                for t in range(T):
                    s = slice(t * P, (t + 1) * P)
                    ins = three(ps(use)[:, s], hT_hi[:, k, s], hT_lo[:, k, s], hi[:, P:], lo[:, P:],
                                first and t == 0, last, skip=True)
                return ins

            panel("kva", [("kva", 0), ("kva", 1)], step)
            for j in range(2):
                emptied(pe, ("qa", j))
                emptied(pe, ("kva", j))
            attend("swa")

            for t in range(T):
                use = ("kz", t)
                o = claim(use, next_small())
                pe.wait_ge(hd_ready, 3)
                for h in range(HH):
                    ins = pe.transpose(o[:, h * P:(h + 1) * P], kk_[:, h, t * P:(t + 1) * P], ident[:, :])
                fill(ins, use)
                use = ("A", t)
                o = claim(use, next_small())
                for h in range(HH):
                    s = slice(t * P, (t + 1) * P)
                    ins = pe.matmul(o[:, h * P:(h + 1) * P], bmid[:, h, s], qd[:, h, s], start=True, stop=True)
                fill(ins, use)
            for c in range(3):
                use = ("kv", c)
                o = claim(use, next_small())
                emptied(pe, ("kz", c // 2))
                emptied(pe, ("ih", c // 2))
                b = slice((c % 2) * CH, (c % 2 + 1) * CH)
                for h in range(HH):
                    f = slice(h * P, (h + 1) * P)
                    ins = pe.matmul(o[:, f], kz_row[b, c // 2, f], hi_row[b, c // 2, f], start=True, stop=True)
                fill(ins, use)
            for t in range(T):
                use = ("ho", t)
                o = claim(use, next_small())
                emptied(pe, ("A", t))
                emptied(pe, ("ih", t))
                for c in range(2 * t + 1):
                    emptied(pe, ("kv", c))
                pe.wait_ge(hd_ready, 4)
                for h in range(HH):
                    f = slice(h * P, (h + 1) * P)
                    ins = pe.matmul(o[:, f], AT[:, t, f], hi_row[:, t, f], start=True, stop=False,
                                    skip_group_check=True)
                    for half in range(2):
                        c = 2 * t + half
                        if c:
                            b = slice(half * CH, (half + 1) * CH)
                            ins = pe.matmul(o[b, f], logf[:, h, c * CH:(c + 1) * CH], state[:, c - 1, f],
                                            start=False, stop=True, skip_group_check=True)
                fill(ins, use)
            turn("o2", lambda: mixed("swa", hgrn_out_ready))
            for p in range(2):
                rows_panel(f"wout2_{p}", hT_hi, hT_lo, turn_before("o2"))
            turn("xpre", rows_scaled("xpre"))
            for p in range(2):
                cols_panel(f"wq{p}", hT_hi, hT_lo, turn_before("xpre"))
            for p in range(2):
                for j in range(2):
                    emptied(pe, (f"wk{p}", j))
                    emptied(pe, (f"wv{p}", j))
                    emptied(pe, (f"wq{p}", j))
            attend("x")

            def crossed():
                for t in range(T):
                    for g in range(2):
                        emptied(pe, ("o", "x", t, g))

            turn("xo", crossed)
            for p in range(2):
                rows_panel(f"wo{p}", hT_hi, hT_lo, turn_before("xo"))
            ffn("gu", "dn", "ffnpre", 1)

        @block.sync
        def _(sp):
            count = [0] * NRAW
            for u, (name, k0, nk, cols, sources) in enumerate(units):
                slot = u % NRAW
                if u >= NRAW:
                    sp.wait_ge(w_lo_ready, u - NRAW + 1)
                dst = unit_view(raw[slot], u).rearrange("p (k n) -> p k n", k=nk)
                for c0, width, matrix, m0 in sources:
                    src = matrix[k0 * P:(k0 + nk) * P, m0:m0 + width].rearrange("(k p) n -> p k n", p=P)
                    sp.dma_start(dst[:, :, c0:c0 + width], src).then_inc(raw_landed[slot], 16)
                    count[slot] += 16
                landed[u] = count[slot]
            sp.wait_ge(res_ready, RES["ffnpost"])
            sp.dma_start(out.rearrange("a (t p) d -> p (a t) d", p=P), res[:, :, :]).then_inc(stored, 16)
            sp.wait_ge(stored, 16)

        @block.gpsimd
        def _(pool):
            pool.memset(ones[:, :], 1.0).then_inc(ones_ready, 1)
            pool.memset(mhalf[:, :], -0.5).then_inc(ones_ready, 1)
            pool.wait_ge(ones_ready, 2)
            for n, name in enumerate(POWS):
                w = 8 if name in ("ret", "hgrn") else 2
                pool.wait_ge(var_ready, n + 1)
                pool.tensor_tensor(rstd[:, n, 0:w], var[:, n, 0:w], mhalf[:, 0:w], ALU.pow).then_inc(rstd_ready, 1)

        @block.scalar
        def _(act):
            steps = [0]

            def step(ins):
                steps[0] += 1
                ins.then_inc(act_step, 1)

            def settle():
                act.wait_ge(act_step, steps[0])

            fed = [0]

            def feed(name):
                stop = min(len(units), last_unit[name] + 1 + NSPLIT) if name else NSPLIT
                while fed[0] < stop:
                    u = fed[0]
                    act.wait_ge(raw_landed[u % NRAW], landed[u])
                    if u >= NSPLIT:
                        released(act, u - NSPLIT)
                    act.activation(unit_view(w_hi[u % NSPLIT], u), unit_view(raw[u % NRAW], u),
                                   ACT.Copy).then_inc(w_hi_ready, 1)
                    fed[0] += 1

            act.dma_start(ident[:, :], const[:, C_ID:C_ID + P]).then_inc(in_ident, 16)
            for name, _ in VEC_GROUPS[0]:
                g, r, n = VEC[name]
                act.dma_start(vrow[g][r:r + n, :], vec_src[name]).then_inc(in_vec, 16)
            act.dma_start(in_mem[:, :, :], a["mem_2"].rearrange("(t p) d -> p t d", p=P)).then_inc(in_memx, 16)
            act.dma_start(in_ctx[:, :, :], a["ctx"].rearrange("(t p) d -> p t d", p=P)).then_inc(in_ctxx, 16)
            act.dma_start(res[:, :, :], a["x"].rearrange("(t p) d -> p t d", p=P)).then_inc(in_x, 16)
            for vs in VEC_GROUPS[1:]:
                for name, _ in vs:
                    g, r, n = VEC[name]
                    act.dma_start(vrow[g][r:r + n, :], vec_src[name]).then_inc(in_conv, 16)
            act.dma_start(k1[:, :], const[:, C_RCOS:C_E1]).then_inc(in_k1, 16)
            act.dma_start(lgam[:, :], a["ret_decay"].partition_broadcast(P)).then_inc(in_decay, 16)
            act.dma_start(g_ret[:, :], a["g_ret"].partition_broadcast(P)).then_inc(in_gains, 16)
            act.dma_start(gate[:, 0, :], a["b_ada"][2 * D:3 * D].partition_broadcast(P)).then_inc(in_gate, 16)
            act.dma_start(gate[:, 1, :], a["b_ada"][5 * D:6 * D].partition_broadcast(P)).then_inc(in_gate, 16)

            def square_res(name, after):
                n = NORM[name]
                for t in range(T):
                    act.wait_ge(res_ready, RES[after] - T + t + 1)
                    act.wait_ge(ssq_ready, T * n + t)
                    act.activation(junk[:, :], res[:, t, :], ACT.Square,
                                   accum_out=ssq[:, 2 * n + t:2 * n + t + 1]).then_inc(ssq_ready, 1)

            def square(name, srcs):
                for t in range(T):
                    n = NORM[name]
                    if T * n + t:
                        act.wait_ge(ssq_ready, T * n + t)
                    act.activation(junk[:, 0:srcs[t].shape[1]], srcs[t], ACT.Square,
                                   accum_out=ssq[:, 2 * n + t:2 * n + t + 1]).then_inc(ssq_ready, 1)

            def turn(name):
                kt, scaled = next(x[1:] for x in TURNS if x[0] == name)
                hi, _, c = turn_dst(name)
                for p in range(kt // 2):
                    use = ("turn", name, p)
                    dst = hi[:, 2 * p:2 * p + 2, c:c + TOK]
                    if scaled:
                        emptied(act, use)
                        act.activation(dst, fbuf[:, p % 2, :, :], ACT.Copy).then_inc(turn_hi, 1)
                    else:
                        ready(act, use)
                        act.activation(dst, ps(use)[:, :].rearrange("p (k t) -> p k t", k=2),
                                       ACT.Copy).then_inc(turn_hi, 1)

            act.wait_ge(in_memx, 16)
            square("mem", [in_mem[:, t, :] for t in range(T)])
            act.wait_ge(in_ctxx, 16)
            square("ctx", [in_ctx[:, t, :] for t in range(T)])
            act.wait_ge(in_x, 16)
            square("x1", [res[:, t, :] for t in range(T)])
            emptied(act, ("vec", 0))
            act.activation(csilu[:, 0, :], vec("c"), ACT.Silu).then_inc(csilu_ready, 1)
            act.activation(csilu[:, 1, :], vec("c_ctx"), ACT.Silu).then_inc(csilu_ready, 1)
            act.wait_ge(csilu_ready, 2)
            for i in range(2):
                act.activation(c_hi[:, :, 64 * i:64 * i + 64],
                               csilu[:, i, :].unsqueeze(2).broadcast_to([P, KD, 64]), ACT.Copy).then_inc(c_hi_ready, 1)
            act.wait_ge(lb_in_ready, 2)
            act.activation(lbc[:, 1:3, :], lbc[:, 1:3, :], ACT.Exp).then_inc(lb_exp_ready, 1)
            feed(None)
            turn("mem")
            for p in range(2):
                feed(f"wk{p}")
                for j in range(2):
                    use = (f"wk{p}", j)
                    ready(act, use)
                    ins = act.activation(KxT[:, 4 * p + 2 * j:4 * p + 2 * j + 2, :],
                                         ps(use)[:, :].rearrange("p (k t) -> p k t", k=2), ACT.Copy)
                    free(ins, use)
            for p in range(2):
                feed(f"wv{p}")
                for t in range(T):
                    use = (f"wv{p}", t)
                    ready(act, use)
                    free(act.activation(Vx[:, t, 512 * p:512 * p + 512], ps(use)[:, :], ACT.Copy), use)

            def ada(p):
                feed(f"ada{p}")
                use = (f"ada{p}", 0)
                ready(act, use)
                if p >= 2:
                    ready(act, ("spread", p - 2))
                    if p - 2 < 4:
                        ready(act, ("spread_ctx", p - 2))
                free(act.activation(modrow[:, p % 2, :], ps(use)[:, :], ACT.Copy), use)

            for p in range(4):
                ada(p)
            turn("ctx")
            turn("x1")

            feed("cqkv")
            for t in range(T):
                use = ("cqkv", t)
                ready(act, use)
                act.activation(cq_row[:, t, :], ps(use)[:, 0:256], ACT.Copy)
                ins = act.activation(ckv_row[:, t, :], ps(use)[:, 256:512], ACT.Copy)
                free(ins, use)
            for t in range(T):
                use = ("cqkv", T + t)
                ready(act, use)
                ins = act.activation(ckv_row[:, T + t, :], ps(use)[:, 256:512], ACT.Copy)
                free(ins, use)
            for t in range(2 * T):
                emptied(act, ("cqkv", t))
            square("cq", [cq_row[:, t, :] for t in range(T)])
            square("ckv", [ckv_row[:, t, :] for t in range(T)])
            square("ckvc", [ckv_row[:, T + t, :] for t in range(T)])
            feed("kpe")
            for t in range(2 * T):
                use = ("kpe", t)
                ready(act, use)
                free(act.activation(kpe_row[:, t, :], ps(use)[:, 0:ROPE], ACT.Copy), use)
            act.wait_ge(in_decay, 16)
            step(act.activation(lgam[:, :], lgam[:, :], ACT.Exp))
            settle()
            step(act.activation(lgam[:, :], lgam[:, :], ACT.Copy, scale=-1.0))
            settle()
            act.wait_ge(in_k1, 16)
            for d in range(2):
                for h in range(RH):
                    act.activation(wctx[:, d, h, :], k1[:, C_WEXP - C_RCOS + 2 * d:C_WEXP - C_RCOS + 2 * d + 2],
                                   ACT.Exp, scale=lgam[:, 4 * d + h:4 * d + h + 1]).then_inc(wctx_ready, 1)
            feed("rk")
            feed("rv")
            for t in range(2 * T):
                use = ("rv", t)
                ready(act, use)
                dst = rv_row if t < T else rvc_row
                free(act.activation(dst[:, t % T, :], ps(use)[:, :], ACT.Copy), use)
            feed("rq")
            feed("rg")
            for t in range(T):
                use = ("rg", t)
                ready(act, use)
                free(act.activation(sgate[:, t, :], ps(use)[:, :], ACT.Silu), use)
            for p in range(4, 12):
                ada(p)
            for h in range(RH):
                act.wait_ge(decay_ready, h + 1)
                act.activation(decay[:, h, :, :], decay[:, h, :, :], ACT.Exp).then_inc(decay_exp_ready, 1)
            for what, dst in (("rk", rkT), ("rq", rqT)):
                for t in range(T):
                    use = ("rT", what, t)
                    ready(act, use)
                    ins = act.activation(dst[:, :, t * P:(t + 1) * P],
                                         ps(use)[:, :].rearrange("p (h t) -> p h t", h=RH), ACT.Copy)
                    free(ins, use)
            for h in range(RH):
                for d in range(2):
                    c = (C_XF, C_XB)[d] - C_RCOS
                    act.activation(xi[:, h, d, :], k1[:, c:c + TOK], ACT.Exp,
                                   scale=lgam[:, 4 * d + h:4 * d + h + 1]).then_inc(xi_ready, 1)
            for name in ("cq", "ckv", "ckvc"):
                turn(name)
            for p in range(2):
                feed(f"uq{p}")
                for t in range(T):
                    use = (f"uq{p}", t)
                    ready(act, use)
                    ins = act.activation(q_row[:, t, 4 * p:4 * p + 4, :],
                                         ps(use)[:, 0:384].rearrange("p (h d) -> p h d", h=4), ACT.Copy)
                    free(ins, use)
            for t in range(T):
                for p in range(2):
                    use = ("qT", t, p)
                    ready(act, use)
                    ins = act.activation(qT[0:DQ, 4 * p:4 * p + 4, t * P:(t + 1) * P],
                                         ps(use)[0:DQ, :].rearrange("p (h t) -> p h t", h=4), ACT.Copy)
                    free(ins, use)
            for p in range(2):
                feed(f"ukv{p}")
                for t in range(2 * T):
                    use = (f"ukv{p}", t)
                    ready(act, use)
                    v = ps(use)[:, :].rearrange("p (h d) -> p h d", h=4)
                    if p:
                        ready(act, ("kT", 0, t))
                    act.activation(V[:, t, 4 * p:4 * p + 4, :], v[:, :, NOPE:], ACT.Copy)
                    free(act.activation(k_row[:, t, :, 0:NOPE], v[:, :, 0:NOPE], ACT.Copy), use)
                for t in range(2 * T):
                    use = ("kT", p, t)
                    ready(act, use)
                    ins = act.activation(kT[0:DQ, 4 * p:4 * p + 4, t * P:(t + 1) * P],
                                         ps(use)[0:DQ, :].rearrange("p (h t) -> p h t", h=4), ACT.Copy)
                    free(ins, use)

            def attend(kind):
                scale = {"mla": MLA_SCALE, "swa": 1.0, "x": X_SCALE}[kind]
                for r in [r for r in ROUNDS if r[0] == kind]:
                    i = ROUND[r]
                    _, t, h = r
                    n = key_tiles(kind, t) * P
                    src = fbuf[:, i % 2, 0, 0:n] if kind == "swa" else ps(("score",) + r)[:, 0:n]
                    act.wait_ge(nmax_ready, i + 1)
                    if i >= 2:
                        ready(act, ("probT",) + ROUNDS[i - 2])
                    if kind == "swa":
                        act.activation(expsink[:, i:i + 1], sinks[:, h:h + 1], ACT.Exp, bias=nmax[:, i, 1:2])
                    ins = act.activation(prob[:, i % 2, 0:n], src, ACT.Exp, bias=nmax[:, i, 1:2], scale=scale,
                                         accum_out=rowsum[:, i:i + 1])
                    if kind == "swa":
                        ins.then_inc(exp_ready, 1)
                    else:
                        free(ins, ("score",) + r)
                    use = ("probT",) + r
                    ready(act, use)
                    if i >= 2:
                        multiplied(act, i - 2)
                    free(act.activation(probT[:, i % 2, 0:n], ps(use)[:, 0:n], ACT.Copy), use)

            attend("mla")
            turn("o")
            feed("wout0")
            feed("wout1")
            square_res("x2", "wout")
            turn("x2")

            act.dma_start(g_final[:, :], a["g_final"].partition_broadcast(P)).then_inc(in_gains, 16)
            for p in range(NFF):
                feed(f"up{p}")
                for s in range(2):
                    use = (f"up{p}", s)
                    ready(act, use)
                    if p >= 2:
                        act.wait_ge(prod_ready, p - 1)
                    for j in range(2):
                        ch = KF * s + 2 * p + j
                        act.activation(conv[:, p % 2, s, j, :], ps(use)[:, j * TOK:(j + 1) * TOK], ACT.Identity,
                                       scale=vec("conv_w1", ch), bias=vec("conv_b", ch)).then_inc(conv_ready, 1)
                emptied(act, (f"up{p}", 1))
                act.activation(sg[:, p % 2, :, :], conv[:, p % 2, 1, :, :], ACT.Silu).then_inc(sg_ready, 1)
                act.wait_ge(prod_ready, p + 1)
                act.activation(act_hi[:, 2 * p:2 * p + 2, :], prod[:, p % 2, :, :], ACT.Copy).then_inc(act_hi_ready, 1)
            feed("down0")
            feed("down1")
            square_res("final", "down")
            act.wait_ge(res_ready, RES["down"])
            act.dma_start(k3[:, :], const[:, C_E1:C_END]).then_inc(in_k3, 16)
            act.dma_start(onorm[:, :], a["hgrn_onorm_2"].partition_broadcast(P)).then_inc(in_k3, 16)
            act.dma_start(sinks[:, :], a["sinks_2"].partition_broadcast(P)).then_inc(in_k3, 16)
            for n, g in enumerate(("g_mix_post_2", "g_x_post_2", "g_ffn_post_2")):
                act.dma_start(g_post[:, n, :], a[g].partition_broadcast(P)).then_inc(in_k3, 16)
            square_res("mix", "final")
            turn("mix")

            feed("qh")
            for j in range(2):
                use = ("qh", j)
                ready(act, use)
                free(act.activation(qs[:, 2 * j:2 * j + 2, :], ps(use)[:, :].rearrange("p (h t) -> p h t", h=2),
                                    ACT.Silu), use)
            feed("fh")
            for j in range(2):
                use = ("fh", j)
                ready(act, use)
                free(act.activation(kk_[:, 2 * j:2 * j + 2, :], ps(use)[:, :].rearrange("p (h t) -> p h t", h=2),
                                    ACT.Sigmoid), use)
            act.wait_ge(f_ready, 1)
            act.activation(logf[:, :, :], logf[:, :, :], ACT.Ln).then_inc(log_ready, 1)
            feed("ih")
            for t in range(T):
                use = ("ih", t)
                ready(act, use)
                free(act.activation(hi_row[:, t, :], ps(use)[:, :], ACT.Copy), use)
            act.wait_ge(cum_ready, 1)
            act.activation(qd[:, :, :], bmid[:, :, :], ACT.Exp).then_inc(hexp_ready, 1)
            act.activation(e_b[:, :, :], bmid[:, :, :], ACT.Exp, scale=-1.0).then_inc(hexp_ready, 1)
            act.wait_ge(cum_ready, 2)
            act.activation(logf[:, :, :], logf[:, :, :], ACT.Exp).then_inc(hexp_ready, 1)
            act.wait_ge(hd_ready, 2)
            act.activation(e_b[:, :, :], cum[:, :, :], ACT.Exp).then_inc(hexp_ready, 1)
            feed("gh")
            for t in range(T):
                use = ("gh", t)
                ready(act, use)
                free(act.activation(hg[:, t, :], ps(use)[:, :], ACT.Silu), use)
            feed("qa")
            for j in range(2):
                use = ("qa", j)
                ready(act, use)
                free(act.activation(aqT[:, 2 * j:2 * j + 2, :], ps(use)[:, :].rearrange("p (h t) -> p h t", h=2),
                                    ACT.Copy), use)
            feed("kva")
            use = ("kva", 0)
            ready(act, use)
            for g in range(2):
                for half in range(2):
                    ins = act.activation(akT[64 * half:64 * half + 64, g, :], ps(use)[64 * g:64 * g + 64, 0:TOK],
                                         ACT.Copy)
            free(ins, use)
            use = ("kva", 1)
            ready(act, use)
            free(act.activation(av[:, :, :], ps(use)[:, 0:TOK].rearrange("p (t d) -> p t d", t=T), ACT.Copy), use)
            act.wait_ge(in_k3, 16 * 6)
            attend("swa")
            for t in range(T):
                use = ("kz", t)
                ready(act, use)
                free(act.activation(kz_row[:, t, :], ps(use)[:, :], ACT.Copy), use)
            for t in range(T):
                use = ("ho", t)
                ready(act, use)
                for h in range(HH):
                    if HH * t + h:
                        act.wait_ge(hsq_ready, HH * t + h)
                    else:
                        act.wait_ge(ssq_ready, T * NORM["mix"] + T)
                    act.activation(junk[:, 0:P], ps(use)[:, h * P:(h + 1) * P], ACT.Square,
                                   accum_out=hsq[:, t, h:h + 1]).then_inc(hsq_ready, 1)
            turn("o2")

            act.wait_ge(hsq_ready, T * HH)

            def rows_out(name, norm):
                for p in range(2):
                    feed(f"{name}{p}")
                    for t in range(T):
                        use = (f"{name}{p}", t)
                        ready(act, use)
                        free(act.activation(row[:, t, 512 * p:512 * p + 512], ps(use)[:, :], ACT.Copy), use)
                for t in range(T):
                    emptied(act, (f"{name}1", t))
                square(norm, [row[:, t, :] for t in range(T)])

            rows_out("wout2_", "mixpost")
            square_res("xpre", "mixpost")
            turn("xpre")
            for p in range(2):
                feed(f"wq{p}")
                for j in range(2):
                    use = (f"wq{p}", j)
                    ready(act, use)
                    free(act.activation(sxqT[:, 4 * p + 2 * j:4 * p + 2 * j + 2, :],
                                        ps(use)[:, :].rearrange("p (k t) -> p k t", k=2), ACT.Copy), use)
            attend("x")
            turn("xo")
            rows_out("wo", "xpost")
            square_res("ffnpre", "xpost")
            turn("ffnpre")
            for p in range(NFF):
                feed(f"gu{p}")
                use = (f"gu{p}", 0)
                ready(act, use)
                if p >= 2:
                    emptied(act, (f"gu{p - 2}", 1))
                free(act.activation(sg[:, p % 2, :, :], ps(use)[:, :].rearrange("p (k t) -> p k t", k=2),
                                    ACT.Silu), use)
                emptied(act, (f"gu{p}", 1))
                act.activation(act_hi[:, 2 * p:2 * p + 2, :], prod[:, p % 2, :, :], ACT.Copy).then_inc(act_hi_ready, 1)
            rows_out("dn", "ffnpost")

        @block.vector
        def _(dve):
            steps = [0]

            def step(ins):
                steps[0] += 1
                ins.then_inc(dve_step, 1)

            def settle():
                dve.wait_ge(dve_step, steps[0])

            fed = [0]

            def feed(name):
                stop = min(len(units), last_unit[name] + 1 + NSPLIT) if name else NSPLIT
                while fed[0] < stop:
                    u = fed[0]
                    dve.wait_ge(w_hi_ready, u + 1)
                    dve.tensor_tensor(unit_view(w_lo[u % NSPLIT], u), unit_view(raw[u % NRAW], u),
                                      unit_view(w_hi[u % NSPLIT], u).bitcast(F32), ALU.subtract).then_inc(w_lo_ready, 1)
                    fed[0] += 1

            def variance(name):
                n = NORM[name]
                dve.wait_ge(ssq_ready, T * (n + 1))
                dve.tensor_scalar(var[:, POW[name], 0:T], ssq[:, T * n:T * n + T], 1.0 / NORMS[n][1], EPS,
                                  ALU.mult, ALU.add).then_inc(var_ready, 1)

            def scale_rows(name, srcs, dsts):
                dve.wait_ge(rstd_ready, POW[name] + 1)
                for t in range(T):
                    dve.tensor_scalar(dsts[t], srcs[t], rstd[:, POW[name], t:t + 1], None, ALU.mult).then_inc(row_ready, 1)

            def turn(name):
                kt, scaled = next(x[1:] for x in TURNS if x[0] == name)
                hi, lo, c = turn_dst(name)

                def full(p):
                    use = ("turn", name, p)
                    ready(dve, use)
                    before = turn_lo_at[name, p] - 2 if p >= 2 else turn_lo_at[name, 0] - 1
                    if before:
                        dve.wait_ge(turn_lo, before)
                    for kk in range(2):
                        gain, shift = turn_gain(name, 2 * p + kk)
                        src = ps(use)[:, kk * TOK:(kk + 1) * TOK]
                        if shift is None:
                            ins = dve.tensor_scalar(fbuf[:, p % 2, kk, :], src, gain, None, ALU.mult)
                        else:
                            ins = dve.tensor_scalar(fbuf[:, p % 2, kk, :], src, gain, shift, ALU.mult, ALU.add)
                    free(ins, use)

                def rest(p):
                    use = ("turn", name, p)
                    h, l = hi[:, 2 * p:2 * p + 2, c:c + TOK], lo[:, 2 * p:2 * p + 2, c:c + TOK]
                    dve.wait_ge(turn_hi, turn_hi_at[name, p])
                    if scaled:
                        dve.tensor_tensor(l, fbuf[:, p % 2, :, :], h.bitcast(F32), ALU.subtract).then_inc(turn_lo, 1)
                    else:
                        free(dve.tensor_tensor(l, ps(use)[:, :].rearrange("p (k t) -> p k t", k=2), h.bitcast(F32),
                                               ALU.subtract), use)

                n = kt // 2
                if scaled:
                    full(0)
                for p in range(n):
                    if scaled and p + 1 < n:
                        full(p + 1)
                    rest(p)

            def columns(g):
                ready(dve, ("vec", g))
                n = vcol[g].shape[1]
                free(dve.tensor_copy(vcol[g][:, :], ps(("vec", g))[:, 0:n]), ("vec", g))

            columns(0)
            emptied(dve, ("vec", 0))
            lb = vec("hgrn_lb_2")
            step(dve.tensor_tensor(lbc[:, 0, :], lb[:, 0:HH], lb[:, HH:2 * HH], ALU.max))
            settle()
            for i in range(2):
                dve.tensor_tensor(lbc[:, 1 + i, :], lb[:, i * HH:(i + 1) * HH], lbc[:, 0, :],
                                  ALU.subtract).then_inc(lb_in_ready, 1)
            variance("mem")
            variance("ctx")
            variance("x1")
            scale_rows("mem", [in_mem[:, t, :] for t in range(T)], [row[:, t, :] for t in range(T)])
            dve.wait_ge(c_hi_ready, 2)
            for i in range(2):
                s = slice(64 * i, 64 * i + 64)
                dve.tensor_tensor(c_lo[:, :, s], csilu[:, i, :].unsqueeze(2).broadcast_to([P, KD, 64]),
                                  c_hi[:, :, s].bitcast(F32), ALU.subtract).then_inc(c_lo_ready, 1)
            columns(1)
            columns(2)
            dve.wait_ge(lb_exp_ready, 1)
            step(dve.tensor_tensor(lbc[:, 3, :], lbc[:, 1, :], lbc[:, 2, :], ALU.add))
            settle()
            step(dve.reciprocal(lbc[:, 3, :], lbc[:, 3, :]))
            settle()
            step(dve.tensor_tensor(lbc[:, 4, :], lbc[:, 1, :], lbc[:, 3, :], ALU.mult))
            settle()
            step(dve.tensor_scalar(lbc[:, 5, :], lbc[:, 4, :], -1.0, 1.0, ALU.mult, ALU.add))
            feed(None)
            turn("mem")
            ready(dve, ("turn", "mem", 3))
            scale_rows("ctx", [in_ctx[:, t, :] for t in range(T)], [row[:, t, :] for t in range(T)])
            for name in ("wk0", "wk1", "wv0", "wv1"):
                feed(name)

            def spread(p):
                use = ("spread", p)
                ready(dve, use)
                b = vec("b_ada")
                if p in (4, 5, 10, 11):
                    g = gate[:, p // 8, 512 * (p % 2):512 * (p % 2) + 512]
                    if p == 4:
                        dve.wait_ge(in_gate, 32)
                    free(dve.tensor_tensor(g, g, ps(use)[:, :], ALU.add), use)
                    return
                ins = dve.tensor_tensor(modc[:, 4 * p:4 * p + 4], ps(use)[:, 0:4], b[:, 4 * p:4 * p + 4], ALU.add)
                free(ins, use)
                if p < 4:
                    use = ("spread_ctx", p)
                    ready(dve, use)
                    free(dve.tensor_tensor(modx[:, 4 * p:4 * p + 4], ps(use)[:, 0:4], b[:, 4 * p:4 * p + 4], ALU.add),
                         use)

            def gain_column(n, scale, g, uses):
                for use in uses:
                    emptied(dve, use)
                settle()
                step(dve.scalar_tensor_tensor(acol[:, n, :], scale, 1.0, vec(g), ALU.add, ALU.mult))

            for p in range(4):
                feed(f"ada{p}")
                if p:
                    spread(p - 1)
            spread(3)
            gain_column(0, modc[:, 8:16], "g_norm1", [("spread", p) for p in range(4)])
            gain_column(2, modx[:, 8:16], "g_norm1", [("spread_ctx", p) for p in range(4)])
            settle()
            turn("ctx")
            ready(dve, ("turn", "ctx", 3))
            scale_rows("x1", [res[:, t, :] for t in range(T)], [row[:, t, :] for t in range(T)])
            turn("x1")

            def turn_pairs(dst0, dst1, a0, a1, b0, b1):
                step(dve.tensor_tensor(dst0, a0, b1, ALU.subtract))
                return dve.tensor_tensor(dst1, a1, b0, ALU.add)

            feed("cqkv")
            for name in ("cq", "ckv", "ckvc"):
                variance(name)
            scale_rows("cq", [cq_row[:, t, :] for t in range(T)], [cq_row[:, t, :] for t in range(T)])
            scale_rows("ckv", [ckv_row[:, t, :] for t in range(T)], [ckv_row[:, t, :] for t in range(T)])
            scale_rows("ckvc", [ckv_row[:, T + t, :] for t in range(T)], [ckv_row[:, T + t, :] for t in range(T)])
            feed("kpe")
            dve.wait_ge(in_k1, 16)

            def mla_table(c, t):
                return k1[:, c - C_RCOS + t * ROPE:c - C_RCOS + (t + 1) * ROPE]

            def halves(x, h):
                v = x.rearrange("p h (a b c) -> p h a b c", a=2, b=2)
                return v[:, :, :, h, :]

            def rope_mla(x, t, heads):
                tmp = []
                for i, c in enumerate((C_MCOS, C_MSIN)):
                    o = rtmp[:, i, 0:heads * ROPE].rearrange("p (h d) -> p h d", h=heads)
                    step(dve.tensor_tensor(o, x, mla_table(c, t).unsqueeze(1).broadcast_to([P, heads, ROPE]), ALU.mult))
                    tmp.append(o)
                settle()
                A, B = tmp
                return turn_pairs(halves(x, 0), halves(x, 1), halves(A, 0), halves(A, 1), halves(B, 0), halves(B, 1))

            for t in range(T):
                emptied(dve, ("kpe", t))
                step(rope_mla(kpe_row[:, t:t + 1, :], t, 1))
                settle()
            feed("rk")

            def rope_ret(use, t, dst):
                ready(dve, use)
                x = ps(use)[:, :].rearrange("p (g d) -> p g d", d=64)
                tmp = []
                for i, c in enumerate((C_RCOS, C_RSIN)):
                    c += t * 64 - C_RCOS
                    o = rtmp[:, i, :].rearrange("p (g d) -> p g d", d=64)
                    ins = dve.tensor_tensor(o, x, k1[:, c:c + 64].unsqueeze(1).broadcast_to([P, 2 * RH, 64]), ALU.mult)
                    if i == 0:
                        step(ins)
                    else:
                        free(ins, use)
                    tmp.append(rtmp[:, i, :].rearrange("p (h b d) -> p h b d", b=2, d=64))
                settle()
                emptied(dve, use)
                A, B = tmp
                o = dst[:, t, :].rearrange("p (h b d) -> p h b d", b=2, d=64)
                turn_pairs(o[:, :, 0, :], o[:, :, 1, :], A[:, :, 0, :], A[:, :, 1, :], B[:, :, 0, :],
                           B[:, :, 1, :]).then_inc(ret_row_ready, 1)
                dve.wait_ge(ret_row_ready, rope_count[0] + 1)
                rope_count[0] += 1

            rope_count = [0]
            for t in range(T):
                rope_ret(("rk", t), t, rk_row)
            dve.wait_ge(wctx_ready, 8)
            for t in range(T):
                use = ("rk", T + t)
                ready(dve, use)
                for d, dst in enumerate((rkf, rkb)):
                    for h in range(RH):
                        ins = dve.tensor_scalar(dst[:, t, h * P:(h + 1) * P], ps(use)[:, h * P:(h + 1) * P],
                                                wctx[:, d, h, t:t + 1], RET_SCALE, ALU.mult, ALU.mult)
                free(ins, use)
            feed("rv")
            feed("rq")
            for t in range(T):
                rope_ret(("rq", t), t, rq_row)
            for h in range(RH):
                dst = decay[:, h, :, :].rearrange("p a b -> p (a b)")
                step(dve.tensor_scalar(dst, k1[:, C_PF - C_RCOS:C_PB - C_RCOS], lgam[:, h:h + 1], None, ALU.mult))
            settle()
            for h in range(RH):
                dst = decay[:, h, :, :].rearrange("p a b -> p (a b)")
                dve.scalar_tensor_tensor(dst, k1[:, C_PB - C_RCOS:C_XF - C_RCOS], lgam[:, RH + h:RH + h + 1], dst,
                                         ALU.mult, ALU.add).then_inc(decay_ready, 1)
            feed("rg")
            dve.wait_ge(in_gains, 16)
            for t in range(T):
                emptied(dve, ("rg", t))
                step(dve.tensor_tensor(sgate[:, t, :], sgate[:, t, :], g_ret[:, :], ALU.mult))
            for p in range(4, 12):
                feed(f"ada{p}")
                if p > 4:
                    spread(p - 1)
                if p == 10:
                    gain_column(1, modc[:, 32:40], "g_norm2", [("spread", 8), ("spread", 9)])
            spread(11)
            for d in range(2):
                use = ("rstate", d)
                ready(dve, use)
                free(dve.tensor_copy(rstate[:, d, :], ps(use)[:, :]), use)
            dve.wait_ge(decay_exp_ready, RH)
            for h in range(RH):
                use = ("ratt", h)
                ready(dve, use)
                dst = decay[:, h, :, :].rearrange("p a b -> p (a b)")
                free(dve.scalar_tensor_tensor(dst, ps(use)[:, :], RET_SCALE, dst, ALU.mult, ALU.mult), use)
            dve.wait_ge(xi_ready, 2 * RH)
            for t in range(T):
                emptied(dve, ("rT", "rq", t))
            for d in range(2):
                dve.tensor_tensor(xi[:, :, d, :], xi[:, :, d, :], rqT[:, :, :], ALU.mult).then_inc(qx_ready, 1)
            for t in range(T):
                ready(dve, ("ret", t))
                for h in range(RH):
                    step(dve.bn_stats(bn[:, t, h, :], ps(("ret", t))[:, h * P:(h + 1) * P]))
            settle()
            for t in range(T):
                for h in range(RH):
                    step(dve.bn_aggr(mv[:, t, h, :], bn[:, t, h, :]))
            settle()
            dve.tensor_scalar(var[:, POW["ret"], :].rearrange("p (t h) -> p t h", t=T), mv[:, :, :, 1], 1.0, EPS,
                              ALU.mult, ALU.add).then_inc(var_ready, 1)
            dve.wait_ge(rstd_ready, POW["ret"] + 1)
            for t in range(T):
                use = ("ret", t)
                for h in range(RH):
                    ins = dve.tensor_scalar(row[:, t, 512 + h * P:512 + (h + 1) * P], ps(use)[:, h * P:(h + 1) * P],
                                            mv[:, t, h, 0:1], rstd[:, POW["ret"], RH * t + h:RH * t + h + 1],
                                            ALU.subtract, ALU.mult)
                free(ins, use)
            for t in range(T):
                emptied(dve, ("ret", t))
                dve.tensor_tensor(row[:, t, 512:], row[:, t, 512:], sgate[:, t, :], ALU.mult).then_inc(ret_out_ready, 1)
            dve.wait_ge(ret_out_ready, T)
            for t in range(2 * T):
                emptied(dve, ("kpe", t))
                dve.tensor_copy(k_row[:, t, :, NOPE:], kpe_row[:, t, :].unsqueeze(1).broadcast_to([P, MLA_H // 2, ROPE])
                                ).then_inc(kpe_ready, 1)
            for name in ("cq", "ckv", "ckvc"):
                turn(name)
            feed("uq0")
            feed("uq1")
            for t in range(T):
                for p in range(2):
                    emptied(dve, (f"uq{p}", t))
                rope_mla(q_row[:, t, :, NOPE:], t, MLA_H).then_inc(q_row_ready, 1)
                dve.wait_ge(q_row_ready, t + 1)
            feed("ukv0")
            feed("ukv1")

            def attend(kind):
                for r in [r for r in ROUNDS if r[0] == kind]:
                    i = ROUND[r]
                    _, t, h = r
                    n = key_tiles(kind, t) * P
                    use = ("score",) + r
                    ready(dve, use)
                    if kind == "swa":
                        if i - 2 >= ROUND["swa", 0, 0]:
                            dve.wait_ge(exp_ready, i - 2 - ROUND["swa", 0, 0] + 1)
                        c = C_SWA - C_E1 + t * P
                        s = fbuf[:, i % 2, 0, 0:n]
                        free(dve.scalar_tensor_tensor(s, ps(use)[:, 0:n], SWA_SCALE, k3[:, c:c + n], ALU.mult, ALU.add), use)
                        emptied(dve, use)
                        step(dve.tensor_reduce(nmax[:, i, 0:1], s, AX_X, ALU.max))
                        settle()
                        dve.tensor_scalar(nmax[:, i, 1:2], nmax[:, i, 0:1], sinks[:, h:h + 1], -1.0,
                                          ALU.max, ALU.mult).then_inc(nmax_ready, 1)
                    else:
                        step(dve.tensor_reduce(nmax[:, i, 0:1], ps(use)[:, 0:n], AX_X, ALU.max))
                        settle()
                        dve.tensor_scalar(nmax[:, i, 1:2], nmax[:, i, 0:1], -(MLA_SCALE if kind == "mla" else X_SCALE),
                                          None, ALU.mult).then_inc(nmax_ready, 1)
                    if i - 1 >= ROUND[kind, 0, 0] and group_of(ROUNDS[i - 1])[2]:
                        divide(ROUNDS[i - 1])
                divide(r)

            def divide(r):
                kind, t, _ = r
                group, n, _ = group_of(r)
                n += 1
                i0 = ROUND[r] - n + 1
                use = ("o",) + group
                ready(dve, use)
                total = rowsum
                if kind == "swa":
                    step(dve.tensor_tensor(denom[:, i0:i0 + n], rowsum[:, i0:i0 + n], expsink[:, i0:i0 + n], ALU.add))
                    settle()
                    total = denom
                step(dve.reciprocal(rinv[:, i0:i0 + n], total[:, i0:i0 + n]))
                settle()
                c = 512 * group[2]
                free(dve.tensor_tensor(row[:, t, c:c + 512].rearrange("p (h d) -> p h d", h=n),
                                       ps(use)[:, :].rearrange("p (h d) -> p h d", h=n),
                                       rinv[:, i0:i0 + n].unsqueeze(2).broadcast_to([P, n, 512 // n]), ALU.mult), use)

            attend("mla")
            turn("o")

            tmp = fbuf[:, :, :, :].rearrange("p a b c -> p (a b c)")

            def gated(name, g):
                for p in range(2):
                    feed(f"{name}{p}")
                    for t in range(T):
                        use = (f"{name}{p}", t)
                        ready(dve, use)
                        c = slice(512 * p, 512 * p + 512)
                        o = tmp[:, 512 * (t % 2):512 * (t % 2) + 512]
                        free(dve.tensor_tensor(o, ps(use)[:, :], gate[:, g, c], ALU.mult), use)
                        emptied(dve, use)
                        dve.tensor_tensor(res[:, t, c], res[:, t, c], o, ALU.add).then_inc(res_ready, 1)

            def prenorm(name, after):
                variance(name)
                dve.wait_ge(res_ready, RES[after])
                scale_rows(name, [res[:, t, :] for t in range(T)], [row[:, t, :] for t in range(T)])
                turn(name)

            emptied(dve, ("spread", 5))
            gated("wout", 0)
            prenorm("x2", "wout")
            for p in range(NFF):
                feed(f"up{p}")
                for s in range(2):
                    use = (f"up{p}", s)
                    ready(dve, use)
                    dve.wait_ge(conv_ready, 4 * p + 2 * s + 2)
                    for j in range(2):
                        u = ps(use)[:, j * TOK:(j + 1) * TOK]
                        o = conv[:, p % 2, s, j, :]
                        ch = KF * s + 2 * p + j
                        step(dve.scalar_tensor_tensor(o[:, 1:TOK], u[:, 0:TOK - 1], vec("conv_w0", ch), o[:, 1:TOK],
                                                      ALU.mult, ALU.add))
                    settle()
                    for j in range(2):
                        u = ps(use)[:, j * TOK:(j + 1) * TOK]
                        o = conv[:, p % 2, s, j, :]
                        ch = KF * s + 2 * p + j
                        ins = dve.scalar_tensor_tensor(o[:, 0:TOK - 1], u[:, 1:TOK], vec("conv_w2", ch), o[:, 0:TOK - 1],
                                                       ALU.mult, ALU.add)
                    free(ins, use)
                emptied(dve, (f"up{p}", 0))
                dve.wait_ge(sg_ready, p + 1)
                dve.tensor_tensor(prod[:, p % 2, :, :], conv[:, p % 2, 0, :, :], sg[:, p % 2, :, :],
                                  ALU.mult).then_inc(prod_ready, 1)
                dve.wait_ge(act_hi_ready, p + 1)
                dve.tensor_tensor(act_lo[:, 2 * p:2 * p + 2, :], prod[:, p % 2, :, :],
                                  act_hi[:, 2 * p:2 * p + 2, :].bitcast(F32), ALU.subtract).then_inc(act_lo_ready, 1)
            gated("down", 1)
            variance("final")
            dve.wait_ge(res_ready, RES["down"])
            dve.wait_ge(rstd_ready, POW["final"] + 1)
            dve.wait_ge(in_gains, 32)
            for t in range(T):
                dve.scalar_tensor_tensor(res[:, t, :], res[:, t, :], rstd[:, POW["final"], t:t + 1], g_final[:, :],
                                         ALU.mult, ALU.mult).then_inc(res_ready, 1)
            prenorm("mix", "final")
            dve.memset(AT[:, :, :], 0.0).then_inc(dve_step, 1)
            steps[0] += 1
            feed("qh")
            feed("fh")
            for j in range(2):
                emptied(dve, ("fh", j))
            for h in range(HH):
                step(dve.tensor_scalar(logf[:, h, :], kk_[:, h, :], lbc[:, 5, h:h + 1], lbc[:, 4, h:h + 1],
                                       ALU.mult, ALU.add))
            settle()
            dve.tensor_scalar(kk_[:, :, :], logf[:, :, :], -1.0, 1.0, ALU.mult, ALU.add).then_inc(f_ready, 1)
            feed("ih")
            dve.wait_ge(in_k3, 16 * 6)
            dve.wait_ge(log_ready, 1)
            for h in range(HH):
                c = C_SCAN - C_E1
                step(dve.tensor_tensor_scan(cum[:, h, :], k3[:, c:c + TOK], logf[:, h, :], 0.0, ALU.mult, ALU.add))
            settle()

            def by_chunk(x):
                return x[:, :, :].rearrange("p h (c j) -> p (h c) j", j=CH)

            def at_position(j):
                return by_chunk(cum)[:, :, j:j + 1].broadcast_to([P, HH * 4, CH])

            dve.tensor_tensor(by_chunk(bmid), by_chunk(cum), at_position(CH // 2 - 1), ALU.subtract).then_inc(cum_ready, 1)
            dve.tensor_tensor(by_chunk(logf), at_position(CH - 1), by_chunk(cum), ALU.subtract).then_inc(cum_ready, 1)
            for j in range(2):
                emptied(dve, ("qh", j))
            dve.wait_ge(hexp_ready, 2)
            dve.scalar_tensor_tensor(qd[:, :, :], qs[:, :, :], HG_SCALE, qd[:, :, :], ALU.mult, ALU.mult).then_inc(hd_ready, 1)
            dve.wait_ge(f_ready, 1)
            dve.tensor_tensor(bmid[:, :, :], kk_[:, :, :], e_b[:, :, :], ALU.mult).then_inc(hd_ready, 1)
            dve.wait_ge(hexp_ready, 3)
            dve.tensor_tensor(kk_[:, :, :], kk_[:, :, :], logf[:, :, :], ALU.mult).then_inc(hd_ready, 1)
            dve.wait_ge(hexp_ready, 4)
            dve.wait_ge(hd_ready, 3)
            dve.scalar_tensor_tensor(logf[:, :, :], qs[:, :, :], HG_SCALE, e_b[:, :, :], ALU.mult, ALU.mult).then_inc(hd_ready, 1)
            feed("gh")
            for t in range(T):
                emptied(dve, ("gh", t))
                v = hg[:, t, :].rearrange("p (h d) -> p h d", h=HH)
                step(dve.tensor_tensor(v, v, onorm[:, :].unsqueeze(1).broadcast_to([P, HH, P]), ALU.mult))
            feed("qa")
            feed("kva")
            attend("swa")
            for t in range(T):
                use = ("A", t)
                ready(dve, use)
                c = C_CAUS - C_E1
                free(dve.copy_predicated(AT[:, t, :], k3[:, c:c + 512].bitcast(U32), ps(use)[:, :]), use)
            for c in range(3):
                use = ("kv", c)
                ready(dve, use)
                if c == 0:
                    ins = dve.tensor_copy(state[:, 0, :], ps(use)[:, :])
                else:
                    emptied(dve, ("kv", c - 1))
                    for h in range(HH):
                        f = slice(h * P, (h + 1) * P)
                        d = e_b[:, h, c * CH + CH - 1:c * CH + CH]
                        ins = dve.scalar_tensor_tensor(state[:, c, f], state[:, c - 1, f], d, ps(use)[:, f],
                                                       ALU.mult, ALU.add)
                free(ins, use)
            dve.wait_ge(hsq_ready, T * HH)
            dve.tensor_scalar(var[:, POW["hgrn"], :], hsq[:, :, :].rearrange("p t h -> p (t h)"), 1.0 / P, EPS,
                              ALU.mult, ALU.add).then_inc(var_ready, 1)
            dve.wait_ge(rstd_ready, POW["hgrn"] + 1)
            for t in range(T):
                use = ("ho", t)
                free(dve.tensor_tensor(row[:, t, 512:].rearrange("p (h d) -> p h d", h=HH),
                                       ps(use)[:, :].rearrange("p (h d) -> p h d", h=HH),
                                       rstd[:, POW["hgrn"], HH * t:HH * t + HH].unsqueeze(2).broadcast_to([P, HH, P]),
                                       ALU.mult), use)
            for t in range(T):
                emptied(dve, ("ho", t))
                dve.tensor_tensor(row[:, t, 512:], row[:, t, 512:], hg[:, t, :], ALU.mult).then_inc(hgrn_out_ready, 1)
            turn("o2")

            def postnorm(name, panel_name, n):
                for p in range(2):
                    feed(f"{panel_name}{p}")
                variance(name)
                for t in range(T):
                    emptied(dve, (f"{panel_name}0", t))
                    emptied(dve, (f"{panel_name}1", t))
                dve.wait_ge(rstd_ready, POW[name] + 1)
                for t in range(T):
                    step(dve.scalar_tensor_tensor(row[:, t, :], row[:, t, :], rstd[:, POW[name], t:t + 1],
                                                  g_post[:, n, :], ALU.mult, ALU.mult))
                settle()
                for t in range(T):
                    dve.tensor_tensor(res[:, t, :], res[:, t, :], row[:, t, :], ALU.add).then_inc(res_ready, 1)

            postnorm("mixpost", "wout2_", 0)
            prenorm("xpre", "mixpost")
            for p in range(2):
                feed(f"wq{p}")
            attend("x")
            turn("xo")
            postnorm("xpost", "wo", 1)
            prenorm("ffnpre", "xpost")
            for p in range(NFF):
                feed(f"gu{p}")
                use = (f"gu{p}", 1)
                ready(dve, use)
                emptied(dve, (f"gu{p}", 0))
                free(dve.tensor_tensor(prod[:, p % 2, :, :], ps(use)[:, :].rearrange("p (k t) -> p k t", k=2),
                                       sg[:, p % 2, :, :], ALU.mult), use)
                dve.wait_ge(act_hi_ready, NFF + p + 1)
                dve.tensor_tensor(act_lo[:, 2 * p:2 * p + 2, :], prod[:, p % 2, :, :],
                                  act_hi[:, 2 * p:2 * p + 2, :].bitcast(F32), ALU.subtract).then_inc(act_lo_ready, 1)
            postnorm("ffnpost", "dn", 2)


def kernel(**inputs):
    import numpy as _np
    import concourse.bacc as _bacc
    from concourse import mybir as _mybir
    from concourse.bass_utils import run_bass_kernel_spmd as _run

    nc = _bacc.Bacc("TRN2", target_bir_lowering=False, num_devices=1)
    arrays, aps = {}, {}
    for name, value in list(inputs.items()) + [("shape_constants", constants())]:
        v = _np.ascontiguousarray(value)
        if v.ndim > 1 and v.shape[0] == 1:
            v = v.reshape(v.shape[1:])
        arrays[name + "_dram"] = v
        aps[name] = nc.dram_tensor(name + "_dram", v.shape, _mybir.dt.from_np(v.dtype), kind="ExternalInput").ap()
    aps["ret_decay"] = aps["ret_decay"].rearrange("a b -> (a b)")
    out = nc.dram_tensor("out_dram", (1, TOK, D), F32, kind="ExternalOutput").ap()
    build(nc, aps, aps["shape_constants"], out)
    r = _run(nc, [arrays], core_ids=[0])
    return r.results[0]["out_dram"]
```

```python
import math
from contextlib import ExitStack

import concourse.bass as bass
import numpy as np
from concourse import mybir

F32 = mybir.dt.float32
F32R = mybir.dt.float32r
U32 = mybir.dt.uint32
ALU = mybir.AluOpType
ACT = mybir.ActivationFunctionType
AX_X = mybir.AxisListType.X

P = 128
D = 1024
KD = D // P
T = 2
TOK = T * P
FF = 2816
KF = FF // P
NFF = KF // 2
EPS = 1e-6
MLA_H, NOPE, ROPE = 8, 64, 32
DQ = NOPE + ROPE
MLA_SCALE = DQ ** -0.5
RH, RD = 4, 128
RET_SCALE = RD ** -0.5
CH = 64
HH = 4
HG_SCALE = 128 ** -0.5
SWA_H = 8
SWA_SCALE = 64 ** -0.5
XH = 4
XD = 256
X_SCALE = XD ** -0.5

UNIT = 1024
NRAW = 6
NSPLIT = 3

C_ID = 0
C_SEL = C_ID + 128
C_SELG = C_SEL + 2
C_RCOS = C_SELG + 128
C_RSIN = C_RCOS + T * 64
C_MCOS = C_RSIN + T * 64
C_MSIN = C_MCOS + T * ROPE
C_WEXP = C_MSIN + T * ROPE
C_PF = C_WEXP + 4
C_PB = C_PF + 512
C_XF = C_PB + 512
C_XB = C_XF + 256
C_E1 = C_XB + 256
C_SWA = C_E1
C_SCAN = C_SWA + 384
C_CAUS = C_SCAN + 256
C_END = C_CAUS + 512


def constants():
    c = np.zeros((P, C_END), np.float32)
    c[:, C_ID:C_ID + P] = np.eye(P)
    c[[0, 32], C_SEL] = 1
    c[[64, 96], C_SEL + 1] = 1
    c[[0, 32], C_SELG:C_SELG + P] = 1
    pos = np.arange(TOK)
    f32 = np.float32

    def angles(p, dim):
        inv = f32(10000.0) ** (-np.arange(0, dim, 2, dtype=f32) / f32(dim))
        return p.astype(f32)[:, None] * inv[None, :]

    a = angles(pos, RD)
    c[:, C_RCOS:C_RSIN] = np.cos(a).reshape(T, P, 64).transpose(1, 0, 2).reshape(P, -1)
    c[:, C_RSIN:C_MCOS] = np.sin(a).reshape(T, P, 64).transpose(1, 0, 2).reshape(P, -1)
    r, q = angles(pos // 64, 16), angles(pos % 64, 16)
    full = np.concatenate([r, r, q, q], axis=1)
    c[:, C_MCOS:C_MSIN] = np.cos(full).reshape(T, P, ROPE).transpose(1, 0, 2).reshape(P, -1)
    c[:, C_MSIN:C_WEXP] = np.sin(full).reshape(T, P, ROPE).transpose(1, 0, 2).reshape(P, -1)
    row = np.arange(P)
    for t in range(T):
        c[:, C_WEXP + t] = TOK - 1 - (t * P + row)
        c[:, C_WEXP + 2 + t] = t * P + row
        diff = pos[None, :] - (t * P + row)[:, None]
        c[:, C_PF + t * TOK:C_PF + (t + 1) * TOK] = np.maximum(diff, 0)
        c[:, C_PB + t * TOK:C_PB + (t + 1) * TOK] = np.maximum(-diff, 0)
    c[:, C_XF:C_XF + TOK] = pos + 1
    c[:, C_XB:C_XB + TOK] = TOK - pos
    chunk = row // CH
    for t in range(T):
        q_chunk = chunk + 2 * t
        k_chunk = np.arange((t + 1) * P) // CH
        seen = (k_chunk[None, :] <= q_chunk[:, None]) & (k_chunk[None, :] >= q_chunk[:, None] - 2)
        at = C_SWA + t * P
        c[:, at:at + (t + 1) * P] = np.where(seen, 0.0, -1e30)
    c[:, C_SCAN:C_SCAN + TOK] = (pos % CH != 0)
    causal = (row[None, :] >= row[:, None]) & (chunk[None, :] == chunk[:, None])
    c[:, C_CAUS:C_END] = np.tile(causal, (1, 4))
    return c


VEC = {}
VEC_GROUPS = (
    [("g_norm1", 8), ("g_norm2", 8), ("g_mix_pre_2", 8), ("g_mem_2", 8), ("g_x_pre_2", 8),
     ("g_ffn_pre_2", 8), ("g_q", 2), ("g_kv", 2), ("hgrn_lb_2", 8), ("c", 8), ("c_ctx", 8), ("b_ada", 48)],
    [("conv_b", 44), ("conv_w0", 44)],
    [("conv_w1", 44), ("conv_w2", 44)],
)
for _g, _vs in enumerate(VEC_GROUPS):
    _at = 0
    for _name, _n in _vs:
        VEC[_name] = (_g, _at, _n)
        _at += _n


def plan_panels(a):
    out = []

    def add(name, kind, matrix, c0, cols, kt=KD, nk=2):
        out.append((name, kind, kt, nk, cols, [(0, cols, matrix, c0)]))

    def ada(ps):
        for p in ps:
            add(f"ada{p}", "ada", a["w_ada"], 512 * p, 512)

    ada(range(4))
    add("cq", "rows", a["w_in"], 0, 256, nk=4)
    add("ckvpe", "rows", a["w_in"], 256, 256 + ROPE)
    add("rk", "rows", a["w_in"], 544 + 512, 512)
    add("rv", "rows", a["w_in"], 544 + 1024, 512)
    add("rq", "rows", a["w_in"], 544, 512)
    add("rg", "rows", a["w_in"], 544 + 1536, 512)
    for p in range(2):
        add(f"uq{p}", "rows", a["w_uq"], 384 * p, 384, kt=2)
    ada((4, 5))
    for p in range(2):
        add(f"ukv{p}", "rows", a["w_ukv"], 512 * p, 512, kt=2)
        ada((10 + p,))
    ada((6, 7, 8, 9))
    for p in range(2):
        add(f"wout{p}", "rows", a["w_out"], 512 * p, 512)
    add("wk0", "cols", a["wk_x_2"], 0, 512)
    for p in range(NFF):
        w = a["w_up"]
        out.append((f"up{p}", "cols", KD, 2, 512, [(0, 256, w, 256 * p), (256, 256, w, FF + 256 * p)]))
    for p in range(2):
        add(f"down{p}", "rows", a["w_down"], 512 * p, 512, kt=KF)
    w = a["w_in_2"]
    add("wk1", "cols", a["wk_x_2"], 512, 512)
    add("fh", "cols", w, 1280, 512)
    add("qa", "cols", w, 0, 512)
    add("qh", "cols", w, 768, 512)
    add("kva", "kva", w, 512, 256, nk=4)
    add("ih", "rows", w, 1792, 512)
    add("gh", "rows", w, 2304, 512)
    add("wv0", "rows", a["wv_x_2"], 0, 512)
    for p in range(2):
        add(f"wout2_{p}", "rows", a["w_out_2"], 512 * p, 512)
    add("wv1", "rows", a["wv_x_2"], 512, 512)
    for p in range(2):
        add(f"wq{p}", "cols", a["wq_x_2"], 512 * p, 512)
    for p in range(2):
        add(f"wo{p}", "rows", a["wo_x_2"], 512 * p, 512)
    for p in range(NFF):
        out.append((f"gu{p}", "cols", KD, 2, 512,
                    [(0, 256, a["w_gate_2"], 256 * p), (256, 256, a["w_up_2"], 256 * p)]))
    for p in range(2):
        add(f"dn{p}", "rows", a["w_down_2"], 512 * p, 512, kt=KF)
    return out


NORMS = [("ctx", D, 1), ("x1", D, 1), ("cq", 256, 1), ("ckv", 256, 1), ("ckvc", 256, 1), ("mem", D, 1),
         ("x2", D, 2), ("final", D, 4), ("mixpost", D, 2), ("xpre", D, 1), ("xpost", D, 2), ("ffnpre", D, 1),
         ("ffnpost", D, 2)]
WIDTH = {name: w for name, w, _ in NORMS}
PARTS = {name: n for name, _, n in NORMS}
SUMS_BEFORE, _sums = {}, 0
for _name, _, _n in NORMS:
    SUMS_BEFORE[_name] = _sums
    _sums += T * _n
POWS = ["ctx", "x1", "cq", "ckv", "ckvc", "mem", "ret", "x2", "final", "hgrn",
        "mixpost", "xpre", "xpost", "ffnpre", "ffnpost"]
POW = {name: n for n, name in enumerate(POWS)}
POW_COLS = {"ret": 8, "hgrn": 8, "final": 4}

ROUNDS = ([("mla", t, h) for t in range(T) for h in range(MLA_H)]
          + [("swa", t, h) for t in range(T) for h in range(SWA_H)]
          + [("x", t, h) for t in range(T) for h in range(XH)])
ROUND = {r: n for n, r in enumerate(ROUNDS)}


ADA_ORDER = [0, 1, 2, 3, 4, 5, 10, 11, 6, 7, 8, 9]


def key_tiles(kind, t):
    return {"mla": 4, "swa": t + 1, "x": 2}[kind]


MLA_PANELS = (6, 7, 8, 9)
FILLERS = {"mla": tuple(f"ada{p}" for p in MLA_PANELS), "swa": ("ih", "gh", "wv0"), "x": ()}
LEAD = {"mla": 0, "swa": 2, "x": 0}
SCORE_BANKS = {"mla": (4, 5, 3), "swa": (4, 5), "x": (4, 5, 2, 3)}
TURN_BANKS = {"mla": (6,), "swa": (6,), "x": (6, 1)}
AHEAD = {"mla": 2, "swa": 1, "x": 2}
PROBS = {"mla": 2, "swa": 4, "x": 4}


def group_of(r):
    kind, t, h = r
    per = 2 if kind == "x" else 8
    return (kind, t, h // per), h % per, h % per == per - 1


def build(nc, a, const, out):
    panels = plan_panels(a)
    units = []
    first_unit, last_unit = {}, {}
    for n, (name, kind, kt, nk, cols, sources) in enumerate(panels):
        first_unit[name] = len(units)
        for k0 in range(0, kt, nk):
            units.append((name, k0, nk, cols, sources))
        last_unit[name] = len(units) - 1
    ends = set(last_unit.values())
    inner = np.cumsum([u not in ends for u in range(len(units))]).tolist()

    with ExitStack() as ctx:
        base = (nc.sbuf_base + 63) // 64 * 64
        at = [base]
        top = [0]

        def sb(name, shape, dt=F32):
            nbytes = (int(np.prod(shape[1:])) * 4 + 31) // 32 * 32
            t = nc.alloc_sbuf_tensor_at(name, shape, dt, offset=at[0])
            at[0] += nbytes
            top[0] = max(top[0], at[0])
            return t

        raw = [sb(f"raw{i}", [P, UNIT]) for i in range(NRAW)]
        w_hi = [sb(f"w_hi{i}", [P, UNIT], F32R) for i in range(NSPLIT)]
        w_lo = [sb(f"w_lo{i}", [P, UNIT], F32R) for i in range(NSPLIT)]
        res = sb("res", [P, T, D])
        row = sb("row", [P, T, D])
        h_at = at[0]
        hT_hi = sb("hT_hi", [P, KD, TOK], F32R)
        hT_lo = sb("hT_lo", [P, KD, TOK], F32R)
        memT_hi = sb("memT_hi", [P, KD, TOK], F32R)
        memT_lo = sb("memT_lo", [P, KD, TOK], F32R)
        junk = sb("junk", [P, D])
        fbuf = sb("fbuf", [P, 2, 2, TOK])
        k0 = sb("k0", [P, C_RCOS])
        ident = k0[:, C_ID:C_ID + P]
        sel_col = k0[:, C_SEL:C_SEL + 2]
        sel_all = k0[:, C_SELG:C_SELG + P]
        vcol = [sb(f"vcol{g}", [P, sum(n for _, n in vs)]) for g, vs in enumerate(VEC_GROUPS)]
        NPOW = 8
        ssq = sb("ssq", [P, _sums])
        var = sb("var", [P, len(POWS), NPOW])
        rstd = sb("rstd", [P, len(POWS), NPOW])
        mhalf = sb("mhalf", [P, NPOW])
        sums = sb("sums", [P, 8])
        rs12 = sb("rs12", [P, T])
        modc = sb("modc", [P, 6 * 8])
        modx = sb("modx", [P, 2 * 8])
        acol = sb("acol", [P, 3, 8])
        lbc = sb("lbc", [P, 6, HH])
        rowsum = sb("rowsum", [P, len(ROUNDS)])
        expsink = sb("expsink", [P, len(ROUNDS)])
        nmax = sb("nmax", [P, len(ROUNDS), 2])
        denom = sb("denom", [P, len(ROUNDS)])
        rinv = sb("rinv", [P, len(ROUNDS)])
        prob_at = at[0]
        prob = sb("prob", [P, 2, 512])
        probT = sb("probT", [P, 2, 512])
        epoch = at[0]
        at[0] = prob_at
        rstate = sb("rstate", [P, 2, 512])
        rtmp = sb("rtmp", [P, 2, 512])
        at[0] = epoch

        gate = sb("gate", [P, 2, D])
        c_parts = sb("c_parts", [P, KD, P], F32R)
        csilu = sb("csilu", [P, 2, KD])
        modrow = sb("modrow", [P, 2, 512])
        k1 = sb("k1", [P, C_E1 - C_RCOS])
        g_ret = sb("g_ret", [P, 512])
        lgam = sb("lgam", [P, 8])
        wctx = sb("wctx", [P, 2, RH, T])
        cq_row = sb("cq_row", [P, T, 256])
        ckv_row = sb("ckv_row", [P, 2 * T, 256])
        kpe_row = sb("kpe_row", [P, 2 * T, ROPE])
        shared = at[0]
        hcT_hi = sb("hcT_hi", [P, KD, TOK], F32R)
        hcT_lo = sb("hcT_lo", [P, KD, TOK], F32R)
        after_hc = at[0]
        vrow = [sb(f"vrow{g}", [P, P]) for g in range(3)]
        in_ctx = sb("in_ctx", [P, T, D])
        at[0] = shared
        cqT_hi = sb("cqT_hi", [P, 2, TOK], F32R)
        cqT_lo = sb("cqT_lo", [P, 2, TOK], F32R)
        ckvT_hi = sb("ckvT_hi", [P, 2, 2 * TOK], F32R)
        ckvT_lo = sb("ckvT_lo", [P, 2, 2 * TOK], F32R)
        xi_f = sb("xi_f", [P, RH, TOK])
        assert at[0] <= after_hc
        at[0] = after_hc
        rk_row = sb("rk_row", [P, T, 512])
        rq_row = sb("rq_row", [P, T, 512])
        rkf = sb("rkf", [P, T, 512])
        rkb = sb("rkb", [P, T, 512])
        rvc_row = sb("rvc_row", [P, T, 512])
        after_rows = at[0]
        at[0] = after_hc
        q_row = sb("q_row", [P, T, MLA_H, DQ])
        k_row = sb("k_row", [P, 2 * T, MLA_H // 2, DQ])
        V = sb("V", [P, 2 * T, MLA_H, 64])
        assert at[0] <= after_rows
        at[0] = after_rows
        rv_row = sb("rv_row", [P, T, 512])
        sgate = sb("sgate", [P, T, 512])
        decay = sb("decay", [P, RH, T, TOK])
        after_ret = at[0]
        at[0] = after_rows
        kT = sb("kT", [P, MLA_H, 2 * TOK])
        assert at[0] <= after_ret
        at[0] = after_ret
        xi_b = sb("xi_b", [P, RH, TOK])
        xi = (xi_f, xi_b)
        bn = sb("bn", [P, T, RH, 6])
        mv = sb("mv", [P, T, RH, 2])
        at[0] = h_at
        rqT = sb("rqT", [P, RH, TOK])
        rkT = sb("rkT", [P, RH, TOK])
        qT = sb("qT", [P, MLA_H, TOK])

        at[0] = epoch + 4 * (C_END - C_E1 + 3 * D)
        act_hi = sb("act_hi", [P, KF, TOK], F32R)
        act_lo = sb("act_lo", [P, KF, TOK], F32R)
        conv = sb("conv", [P, 2, 2, 2, TOK])
        sg = sb("sg", [P, 2, 2, TOK])
        prod = sb("prod", [P, 2, 2, TOK])
        g_final = sb("g_final", [P, D])
        ffn_end = at[0]
        at[0] = epoch
        k3 = sb("k3", [P, C_END - C_E1])
        g_post = sb("g_post", [P, 3, D])
        hsq = sb("hsq", [P, T, HH])
        sinks = sb("sinks", [P, SWA_H])
        onorm = sb("onorm", [P, P])
        aqT = sb("aqT", [P, 4, TOK])
        akT = sb("akT", [P, 2, TOK])
        av = sb("av", [P, T, P])
        avT = sb("avT", [P, TOK])
        qs_at = at[0]
        qs = sb("qs", [P, HH, TOK])
        kk_ = sb("kk_", [P, HH, TOK])
        logf = sb("logf", [P, HH, TOK])
        cum = sb("cum", [P, HH, TOK])
        bmid = sb("bmid", [P, HH, TOK])
        e_b = sb("e_b", [P, HH, TOK])
        qd = sb("qd", [P, HH, TOK])
        kz_row = sb("kz_row", [P, T, 512])
        hi_row = sb("hi_row", [P, T, 512])
        hg = sb("hg", [P, T, 512])
        AT = sb("AT", [P, T, 512])
        state = sb("state", [P, 3, 512])
        end = at[0]
        at[0] = qs_at
        sxqT = sb("sxqT", [P, KD, TOK])
        at[0] = qs_at
        mix_row = sb("mix_row", [P, T, D])
        at[0] = end
        Vx = sb("Vx", [P, T, D])
        assert at[0] >= ffn_end
        KxT = sb("KxT", [P, KD, TOK])
        assert top[0] <= nc.sbuf_usable_end, (top[0], nc.sbuf_usable_end)

        bank = [ctx.enter_context(nc.psum_tensor(f"bank{i}", [P, 512], F32)) for i in range(8)]

        def sem(name):
            return ctx.enter_context(nc.semaphore(name))

        raw_landed = [sem(f"raw_landed{i}") for i in range(NRAW)]
        w_hi_ready = sem("w_hi_ready")
        w_lo_ready = sem("w_lo_ready")
        w_used = sem("w_used")
        filled = [sem(f"filled{i}") for i in range(8)]
        freed = [sem(f"freed{i}") for i in range(8)]
        act_step = sem("act_step")
        dve_step = sem("dve_step")
        in_vec = sem("in_vec")
        in_conv = sem("in_conv")
        in_ident = sem("in_ident")
        in_k1 = sem("in_k1")
        in_decay = sem("in_decay")
        in_mem = sem("in_mem")
        in_ctxx = sem("in_ctxx")
        in_x = sem("in_x")
        in_gate = sem("in_gate")
        in_gains = sem("in_gains")
        in_k3 = sem("in_k3")
        mhalf_ready = sem("mhalf_ready")
        rs12_ready = sem("rs12_ready")
        csilu_ready = sem("csilu_ready")
        c_hi_ready = sem("c_hi_ready")
        c_lo_ready = sem("c_lo_ready")
        row_ready_act = sem("row_ready_act")
        xg_ready = sem("xg_ready")
        lb_in_ready = sem("lb_in_ready")
        lb_exp_ready = sem("lb_exp_ready")
        ssq_ready = sem("ssq_ready")
        var_ready = sem("var_ready")
        rstd_ready = sem("rstd_ready")
        row_ready = sem("row_ready")
        turn_hi = sem("turn_hi")
        turn_lo = sem("turn_lo")
        ret_row_ready = sem("ret_row_ready")
        wctx_ready = sem("wctx_ready")
        decay_ready = sem("decay_ready")
        decay_exp_ready = sem("decay_exp_ready")
        xi_ready = sem("xi_ready")
        qx_ready = sem("qx_ready")
        ret_out_ready = sem("ret_out_ready")
        q_row_ready = sem("q_row_ready")
        kpe_ready = sem("kpe_ready")
        nmax_ready = sem("nmax_ready")
        exp_ready = sem("exp_ready")
        pv_done = sem("pv_done")
        res_ready = sem("res_ready")
        conv_ready = sem("conv_ready")
        sg_ready = sem("sg_ready")
        prod_ready = sem("prod_ready")
        act_hi_ready = sem("act_hi_ready")
        act_lo_ready = sem("act_lo_ready")
        f_ready = sem("f_ready")
        log_ready = sem("log_ready")
        cum_ready = sem("cum_ready")
        hexp_ready = sem("hexp_ready")
        hd_ready = sem("hd_ready")
        hsq_ready = sem("hsq_ready")
        hgrn_out_ready = sem("hgrn_out_ready")
        hg_ready = sem("hg_ready")
        stored = sem("stored")

        place, uses = {}, [0] * 8

        def ready(eng, name):
            b, n = place[name]
            eng.wait_ge(filled[b], n + 1)

        def emptied(eng, name):
            b, n = place[name]
            eng.wait_ge(freed[b], n + 1)

        def ps(name):
            return bank[place[name][0]]

        def free(ins, name):
            ins.then_inc(freed[place[name][0]], 1)

        def vec(name, k=None):
            g, c, n = VEC[name]
            return vcol[g][:, c:c + n] if k is None else vcol[g][:, c + k:c + k + 1]

        def multiplied(eng, i):
            group, _, last = group_of(ROUNDS[i])
            if last:
                ready(eng, ("o",) + group)
            else:
                eng.wait_ge(pv_done, sum(not group_of(r)[2] for r in ROUNDS[:i + 1]))

        vec_src = {}
        for vs in VEC_GROUPS:
            for name, n in vs:
                if name.startswith("conv_w"):
                    v = a["conv_w"][int(name[-1]), :]
                elif name == "hgrn_lb_2":
                    v = a[name].rearrange("l n -> (l n)")
                else:
                    v = a[name]
                vec_src[name] = v.rearrange("(r p) -> r p", p=P)

        def unit_view(t, u):
            _, _, nk, cols, _ = units[u]
            return t[:, 0:nk * cols]

        def released(eng, u):
            if u in ends:
                ready(eng, ("end", units[u][0]))
            else:
                eng.wait_ge(w_used, inner[u])

        TURNS = [("x1", KD, True), ("ctx", KD, True), ("mem", KD, True), ("cq", 2, True), ("ckv", 2, True),
                 ("ckvc", 2, True), ("o", KD, False), ("x2", KD, True), ("mix", KD, True),
                 ("o2", KD, False), ("xpre", KD, True), ("xo", KD, False), ("ffnpre", KD, True)]
        turn_hi_at, turn_lo_at = {}, {}
        nh = nl = 0
        for name, kt, scaled in TURNS:
            for p in range(kt // 2):
                nh += 1
                turn_hi_at[name, p] = nh
                nl += scaled
                turn_lo_at[name, p] = nl if scaled else None

        def turned(eng, name, p):
            if turn_lo_at[name, p] is None:
                emptied(eng, ("turn", name, p))
            else:
                eng.wait_ge(turn_lo, turn_lo_at[name, p])

        def prob_of(i):
            n = PROBS[ROUNDS[i][0]]
            return prob[:, :, :].rearrange("p a b -> p (a b)")[:, (i % n) * (UNIT // n):(i % n + 1) * (UNIT // n)]

        def square_column(name, part, t):
            c = SUMS_BEFORE[name] + T * part + t
            return ssq[:, c:c + 1]

        TURN_SRC = {"ctx": lambda t, k: in_ctx[:, t, k * P:(k + 1) * P],
                    "mix": lambda t, k: mix_row[:, t, k * P:(k + 1) * P],
                    "cq": lambda t, k: cq_row[:, t, k * P:(k + 1) * P],
                    "ckv": lambda t, k: ckv_row[:, t, k * P:(k + 1) * P],
                    "ckvc": lambda t, k: ckv_row[:, T + t, k * P:(k + 1) * P]}

        def turn_src(name):
            return TURN_SRC.get(name, lambda t, k: row[:, t, k * P:(k + 1) * P])

        def turn_dst(name):
            if name == "mem":
                return memT_hi, memT_lo, 0
            if name == "ctx":
                return hcT_hi, hcT_lo, 0
            if name == "cq":
                return cqT_hi, cqT_lo, 0
            if name in ("ckv", "ckvc"):
                return ckvT_hi, ckvT_lo, TOK * (name == "ckvc")
            return hT_hi, hT_lo, 0

        def turn_gain(name, k):
            if name in ("x1", "x2", "ctx"):
                n = {"x1": 0, "x2": 1, "ctx": 2}[name]
                shift = modx[:, k:k + 1] if name == "ctx" else modc[:, 24 * n + k:24 * n + k + 1]
                return acol[:, n, k:k + 1], shift
            gain = {"mem": "g_mem_2", "cq": "g_q", "ckv": "g_kv", "ckvc": "g_kv", "mix": "g_mix_pre_2",
                    "xpre": "g_x_pre_2", "ffnpre": "g_ffn_pre_2"}[name]
            return vec(gain, k), None

        NORM_ROWS = ["ctx", "x1", "cq", "ckv", "ckvc", "mem", "x2", "mix", "xpre", "ffnpre"]
        ROWS_BY_DVE = {name: sum(T if WIDTH.get(m, D) == 256 else 1 for m in NORM_ROWS[:n + 1])
                       for n, name in enumerate(NORM_ROWS)}
        ROWS_BY_ACT = {name: sum(WIDTH.get(m, D) == D for m in NORM_ROWS[:n + 1]) for n, name in enumerate(NORM_ROWS)}
        RES = {"wout": 4, "down": 8, "final": 10, "mixpost": 12, "xpost": 14, "ffnpost": 16}

        def rows_scaled(eng, name):
            eng.wait_ge(row_ready, ROWS_BY_DVE[name])
            if WIDTH.get(name, D) == D:
                eng.wait_ge(row_ready_act, ROWS_BY_ACT[name])

        landed = {}

        block = ctx.enter_context(nc.Block())

        @block.tensor
        def _(pe):
            def claim(name, b):
                if uses[b]:
                    pe.wait_ge(freed[b], uses[b])
                place[name] = (b, uses[b])
                uses[b] += 1
                return bank[b]

            def fill(ins, name):
                ins.then_inc(filled[place[name][0]], 1)

            small = [0]

            def next_small():
                small[0] += 1
                return 4 + small[0] % 4

            side = [0]

            def next_side():
                side[0] ^= 1
                return 2 * side[0]

            def three(o, xh, xl, yh, yl, first, last, skip=False):
                pe.matmul(o, xh, yh, start=first, stop=False, skip_group_check=skip)
                pe.matmul(o, xh, yl, start=False, stop=False, skip_group_check=skip)
                return pe.matmul(o, xl, yh, start=False, stop=last, skip_group_check=skip)

            def panel(name, outs, step, before=None):
                _, kind, kt, nk, cols, _ = next(x for x in panels if x[0] == name)
                place[("end", name)] = place[outs[-1]]
                for u in range(first_unit[name], last_unit[name] + 1):
                    first_k = units[u][1]
                    if before is not None:
                        for k in range(first_k, first_k + nk):
                            before(k)
                    pe.wait_ge(w_lo_ready, u + 1)
                    hi = unit_view(w_hi[u % NSPLIT], u).rearrange("p (k n) -> p k n", k=nk)
                    lo = unit_view(w_lo[u % NSPLIT], u).rearrange("p (k n) -> p k n", k=nk)
                    final = u == last_unit[name]
                    for use in outs:
                        for kk in range(nk):
                            k = first_k + kk
                            ins = step(k, use, hi[:, kk, :], lo[:, kk, :], k == 0, k == kt - 1)
                        if final:
                            fill(ins, use)
                    if not final:
                        ins.then_inc(w_used, 1)
                    yield

            def run(steps):
                for _ in steps:
                    pass

            def rows_steps(name, xh, xl, before=None, ctxT=None, b=None):
                outs = []
                if ctxT is not None:
                    b = 0 if b is None else b
                elif b is None:
                    b = next_side()
                for t in range(T):
                    outs.append((name, t))
                    claim(outs[-1], b + t)
                if ctxT is not None:
                    side[0] = 1
                    for t in range(T):
                        outs.append((name, T + t))
                        claim(outs[-1], b + 2 + t)

                def step(k, use, hi, lo, first, last):
                    t = use[1]
                    sh, sl = (xh, xl) if t < T else ctxT
                    s = slice((t % T) * P, (t % T + 1) * P)
                    return three(ps(use)[:, 0:hi.shape[1]], sh[:, k, s], sl[:, k, s], hi, lo, first, last)

                yield from panel(name, outs, step, before)

            def rows_panel(*args, **kwargs):
                run(rows_steps(*args, **kwargs))

            def cols_panel(*args):
                run(cols_steps(*args))

            def cols_steps(name, xh, xl, before=None):
                outs = [(name, 0), (name, 1)]
                b = next_side()
                for j in range(2):
                    claim(outs[j], b + j)

                def step(k, use, hi, lo, first, last):
                    for n in range(2):
                        c = (2 * use[1] + n) * P
                        o = ps(use)[:, n * TOK:(n + 1) * TOK]
                        f = first and n == 0
                        pe.matmul(o, hi[:, c:c + P], xh[:, k, :], start=f, stop=False, skip_group_check=True)
                        pe.matmul(o, hi[:, c:c + P], xl[:, k, :], start=False, stop=False, skip_group_check=True)
                        ins = pe.matmul(o, lo[:, c:c + P], xh[:, k, :], start=False, stop=last,
                                        skip_group_check=True)
                    return ins

                yield from panel(name, outs, step, before)

            def turn(name, wait_src=None, pairs=None):
                src = turn_src(name)
                kt = next(x[1] for x in TURNS if x[0] == name)
                if wait_src is None:
                    rows_scaled(pe, name)
                else:
                    wait_src()
                for p in pairs or range(kt // 2):
                    use = ("turn", name, p)
                    o = claim(use, next_small())
                    for kk in range(2):
                        for t in range(T):
                            c = (kk * T + t) * P
                            ins = pe.transpose(o[:, c:c + P], src(t, 2 * p + kk), ident)
                    fill(ins, use)

            def turn_before(name):
                done = set()

                def before(k):
                    if k // 2 not in done:
                        done.add(k // 2)
                        turned(pe, name, k // 2)
                return before

            pe.wait_ge(in_ident, 16)
            def turn_vectors(g):
                n = vcol[g].shape[1]
                o = claim(("vec", g), next_small())
                pe.wait_ge(in_conv if g else in_vec, 16 * (4 if g else 12))
                fill(pe.transpose(o[:, 0:n], vrow[g][0:n, :], ident[0:n, 0:n]), ("vec", g))

            turn_vectors(0)

            def ada_steps(p):
                name = f"ada{p}"
                use = (name, 0)
                if p >= 10:
                    claim(use, next_small())
                else:
                    claim(use, p % (2 if p in MLA_PANELS else 4))

                def step(k, use, hi, lo, first, last):
                    pe.matmul(ps(use)[:, :], c_parts[:, k, :], hi, start=first, stop=False)
                    return pe.matmul(ps(use)[:, :], c_parts[:, k, :], lo, start=False, stop=last)

                yield from panel(name, [use], step)

            def ada(p):
                run(ada_steps(p))

            def ada_spread(p, b=None):
                emptied(pe, (f"ada{p}", 0))
                use = ("spread", p)
                o = claim(use, next_small() if b is None else b)
                m = modrow[:, p % 2, :]
                if p in (4, 5, 10, 11):
                    fill(pe.matmul(o[:, :], sel_all, m, start=True, stop=True), use)
                    return
                for j in range(4):
                    ins = pe.matmul(o[:, 2 * j:2 * j + 2], m[:, j * P:(j + 1) * P], sel_col, start=True, stop=True)
                fill(ins, use)

            pe.wait_ge(c_lo_ready, 2)
            for p in range(4):
                ada(p)
                if p:
                    ada_spread(p - 1)
                else:
                    turn_vectors(1)
                    turn_vectors(2)
            ada_spread(3)
            turn("x1")

            cT = (hcT_hi, hcT_lo)
            cq = rows_steps("cq", hT_hi, hT_lo, turn_before("x1"), b=0)
            next(cq)
            turn("ctx")
            run(cq)
            rows_panel("ckvpe", hT_hi, hT_lo, turn_before("ctx"), cT, b=4)
            rk = rows_steps("rk", hT_hi, hT_lo, None, cT, b=0)
            for _ in range(3):
                next(rk)
            turn("mem")
            run(rk)
            rows_panel("rv", hT_hi, hT_lo, None, cT, b=4)
            rows_panel("rq", hT_hi, hT_lo, b=0)
            for name in ("cq", "ckv", "ckvc"):
                turn(name)
            rows_panel("rg", hT_hi, hT_lo, b=2)

            for what, src in (("rk", rk_row), ("rq", rq_row)):
                for t in range(T):
                    use = ("rT", what, t)
                    o = claim(use, next_small())
                    pe.wait_ge(ret_row_ready, 2 * (what == "rq") + t + 1)
                    for h in range(RH):
                        ins = pe.transpose(o[:, h * P:(h + 1) * P], src[:, t, h * P:(h + 1) * P], ident)
                    fill(ins, use)
            rows_panel("uq0", cqT_hi, cqT_lo, turn_before("cq"))
            for d, kd in enumerate((rkf, rkb)):
                use = ("rstate", d)
                o = claim(use, next_small())
                for t in range(T):
                    emptied(pe, ("rk", T + t))
                    emptied(pe, ("rv", T + t))
                for h in range(RH):
                    for j in range(T):
                        ins = pe.matmul(o[:, h * P:(h + 1) * P], kd[:, j, h * P:(h + 1) * P],
                                        rvc_row[:, j, h * P:(h + 1) * P], start=j == 0, stop=j == T - 1)
                fill(ins, use)
            for what in ("rk", "rq"):
                for t in range(T):
                    emptied(pe, ("rT", what, t))
            for h in range(RH):
                use = ("ratt", h)
                o = claim(use, next_small())
                for j in range(T):
                    ins = pe.matmul(o[:, j * TOK:(j + 1) * TOK], rkT[:, h, j * P:(j + 1) * P], rqT[:, h, :],
                                    start=True, stop=True)
                fill(ins, use)
            rows_panel("uq1", cqT_hi, cqT_lo)
            ada(4)
            ada(5)
            ada_spread(4)
            for t in range(T):
                use = ("ret", t)
                o = claim(use, next_small())
                for h in range(RH):
                    emptied(pe, ("ratt", h))
                for d in range(2):
                    emptied(pe, ("rstate", d))
                    emptied(pe, ("rv", d))
                pe.wait_ge(qx_ready, 2)
                s = slice(t * P, (t + 1) * P)
                for h in range(RH):
                    c = slice(h * P, (h + 1) * P)
                    pe.matmul(o[:, c], decay[:, h, 0, s], rv_row[:, 0, c], start=True, stop=False)
                    pe.matmul(o[:, c], decay[:, h, 1, s], rv_row[:, 1, c], start=False, stop=False)
                    pe.matmul(o[:, c], xi[0][:, h, s], rstate[:, 0, c], start=False, stop=False)
                    ins = pe.matmul(o[:, c], xi[1][:, h, s], rstate[:, 1, c], start=False, stop=True)
                fill(ins, use)

            for p in range(2):
                name = f"ukv{p}"
                b4 = turn_before("ckv")
                c4 = turn_before("ckvc")

                def both(k, b4=b4, c4=c4):
                    b4(k)
                    c4(k)
                rows_panel(name, ckvT_hi[:, :, 0:TOK], ckvT_lo[:, :, 0:TOK], both,
                           (ckvT_hi[:, :, TOK:], ckvT_lo[:, :, TOK:]))
                if p == 0:
                    two = [b for b in range(4, 8) if b not in (place[("ret", 0)][0], place[("ret", 1)][0])]
                    for t in range(T):
                        for g in range(2):
                            use = ("qT", t, g)
                            o = claim(use, two[g])
                            pe.wait_ge(q_row_ready, t + 1)
                            for h in range(4):
                                ins = pe.transpose(o[0:DQ, h * P:(h + 1) * P], q_row[:, t, 4 * g + h, :], ident)
                            fill(ins, use)
                    ada_spread(5)
                else:
                    ada_spread(10)
                ada(10 + p)
                for t in range(2 * T):
                    use = ("kT", p, t)
                    o = claim(use, next_small())
                    emptied(pe, (name, t))
                    pe.wait_ge(kpe_ready, 2 * T)
                    for h in range(4):
                        ins = pe.transpose(o[0:DQ, h * P:(h + 1) * P], k_row[:, t, h, :], ident)
                    fill(ins, use)
            ada_spread(11)

            def attend(kind, work=()):
                rounds = [r for r in ROUNDS if r[0] == kind]
                start = ROUND[rounds[0]]

                def score(r):
                    i = ROUND[r]
                    _, t, h = r
                    use = ("score",) + r
                    o = claim(use, SCORE_BANKS[kind][i % len(SCORE_BANKS[kind])])
                    s = slice(t * P, (t + 1) * P)
                    if kind == "mla":
                        ins = pe.matmul(o[:, :], qT[0:DQ, h, s], kT[0:DQ, h, :], start=True, stop=True)
                    elif kind == "swa":
                        b = slice(64 * (h % 2), 64 * (h % 2) + 64)
                        ins = pe.matmul(o[:, 0:(t + 1) * P], aqT[b, h // 2, s], akT[b, h // 4, 0:(t + 1) * P],
                                        start=True, stop=True)
                    else:
                        emptied(pe, (f"wq{h // 2}", h % 2))
                        pe.matmul(o[:, 0:TOK], sxqT[:, 2 * h, s], KxT[:, 2 * h, :], start=True, stop=False)
                        ins = pe.matmul(o[:, 0:TOK], sxqT[:, 2 * h + 1, s], KxT[:, 2 * h + 1, :],
                                        start=False, stop=True)
                    fill(ins, use)

                def turn_probs(r):
                    i = ROUND[r]
                    use = ("probT",) + r
                    o = claim(use, TURN_BANKS[kind][i % len(TURN_BANKS[kind])])
                    if kind == "swa":
                        pe.wait_ge(exp_ready, i - start + 1)
                    else:
                        emptied(pe, ("score",) + r)
                    for j in range(key_tiles(kind, r[1])):
                        ins = pe.transpose(o[:, j * P:(j + 1) * P], prob_of(i)[:, j * P:(j + 1) * P], ident)
                    fill(ins, use)

                def times_values(r):
                    i = ROUND[r]
                    _, t, h = r
                    group, at_, last = group_of(r)
                    if at_ == 0:
                        claim(("o",) + group, 7)
                    o = ps(("o",) + group)
                    w = XD if kind == "x" else 64
                    emptied(pe, ("probT",) + r)
                    nk = key_tiles(kind, t)
                    for j in range(nk):
                        v = {"mla": lambda: V[:, j, h, :], "swa": lambda: av[:, j, 64 * (h // 4):64 * (h // 4) + 64],
                             "x": lambda: Vx[:, j, h * XD:(h + 1) * XD]}[kind]()
                        ins = pe.matmul(o[:, at_ * w:(at_ + 1) * w], probT[:, i % 2, j * P:(j + 1) * P], v,
                                        start=j == 0, stop=j == nk - 1)
                    if last:
                        fill(ins, ("o",) + group)
                    else:
                        ins.then_inc(pv_done, 1)

                work = iter(work)
                for n in range(AHEAD[kind]):
                    score(rounds[n])
                for n, r in enumerate(rounds):
                    if n + AHEAD[kind] < len(rounds):
                        score(rounds[n + AHEAD[kind]])
                    turn_probs(r)
                    if n:
                        times_values(rounds[n - 1])
                    next(work, None)
                times_values(rounds[-1])
                run(work)

            for t in range(T):
                for p in range(2):
                    emptied(pe, ("qT", t, p))
            for p in range(2):
                for t in range(2 * T):
                    emptied(pe, ("kT", p, t))

            def mla_work():
                for n, p in enumerate(MLA_PANELS):
                    for u, _ in enumerate(ada_steps(p)):
                        if u == 1 and n:
                            ada_spread(p - 1, 2)
                        yield

            attend("mla", mla_work())
            ada_spread(9)

            def mixed(kind, sem_):
                for t in range(T):
                    emptied(pe, ("o", kind, t, 0))
                if sem_ is not None:
                    pe.wait_ge(sem_, T)

            turn("o", lambda: mixed("mla", ret_out_ready))
            for p in range(2):
                rows_panel(f"wout{p}", hT_hi, hT_lo, turn_before("o"))

            cols_panel("wk0", memT_hi, memT_lo)

            def ffn(up, down, pre, gen):
                turn(pre)
                for p in range(NFF):
                    cols_panel(f"{up}{p}", hT_hi, hT_lo, turn_before(pre) if p == 0 else None)

                def before(k):
                    if k % 2 == 0:
                        pe.wait_ge(act_lo_ready, NFF * gen + k // 2 + 1)
                rows_panel(f"{down}0", act_hi, act_lo, before)
                rows_panel(f"{down}1", act_hi, act_lo)

            ffn("up", "down", "x2", 0)

            cols_panel("wk1", memT_hi, memT_lo)
            turn("mix")
            cols_panel("fh", hT_hi, hT_lo, turn_before("mix"))
            cols_panel("qa", hT_hi, hT_lo)
            cols_panel("qh", hT_hi, hT_lo)
            b = next_side()
            claim(("kva", 0), b)
            claim(("kva", 1), b + 1)

            def step(k, use, hi, lo, first, last):
                c = slice(use[1] * P, (use[1] + 1) * P)
                o = ps(use)[:, 0:TOK]
                pe.matmul(o, hi[:, c], hT_hi[:, k, :], start=first, stop=False)
                pe.matmul(o, hi[:, c], hT_lo[:, k, :], start=False, stop=False)
                return pe.matmul(o, lo[:, c], hT_hi[:, k, :], start=False, stop=last)

            run(panel("kva", [("kva", 1), ("kva", 0)], step))

            def swa_work():
                ih = rows_steps("ih", hT_hi, hT_lo)
                next(ih)
                use = ("av",)
                o = claim(use, b)
                emptied(pe, ("kva", 1))
                for t in range(T):
                    ins = pe.transpose(o[:, t * P:(t + 1) * P], avT[:, t * P:(t + 1) * P], ident)
                fill(ins, use)
                yield
                for n, _ in enumerate(ih, 1):
                    if n == LEAD["swa"]:
                        emptied(pe, use)
                    yield
                yield from rows_steps("gh", hT_hi, hT_lo)
                yield from rows_steps("wv0", memT_hi, memT_lo)
                first, second = place[("gh", 0)][0], place[("wv0", 0)][0]
                pe.wait_ge(hd_ready, 3)
                for t in range(T):
                    use = ("kz", t)
                    o = claim(use, first + t)
                    for h in range(HH):
                        ins = pe.transpose(o[:, h * P:(h + 1) * P], kk_[:, h, t * P:(t + 1) * P], ident)
                    fill(ins, use)
                yield
                for t in range(T):
                    use = ("A", t)
                    o = claim(use, second + t)
                    for h in range(HH):
                        s = slice(t * P, (t + 1) * P)
                        ins = pe.matmul(o[:, h * P:(h + 1) * P], bmid[:, h, s], qd[:, h, s], start=True, stop=True)
                    fill(ins, use)
                yield
                for c in range(3):
                    use = ("kv", c)
                    o = claim(use, (first, first + 1, second)[c])
                    emptied(pe, ("kz", c // 2))
                    emptied(pe, ("ih", c // 2))
                    rows = slice((c % 2) * CH, (c % 2 + 1) * CH)
                    for h in range(HH):
                        f = slice(h * P, (h + 1) * P)
                        ins = pe.matmul(o[:, f], kz_row[rows, c // 2, f], hi_row[rows, c // 2, f], start=True, stop=True)
                    fill(ins, use)
                    if c:
                        yield

            swa = swa_work()
            for _ in range(LEAD["swa"]):
                next(swa)
            for j in range(2):
                emptied(pe, ("qa", j))
                emptied(pe, ("kva", j))
            attend("swa", swa)

            turn("o2", lambda: mixed("swa", None), range(2))
            for t in range(T):
                use = ("ho", t)
                o = claim(use, next_small())
                emptied(pe, ("A", t))
                emptied(pe, ("ih", t))
                for c in range(2 * t + 1):
                    emptied(pe, ("kv", c))
                pe.wait_ge(hd_ready, 4)
                for h in range(HH):
                    f = slice(h * P, (h + 1) * P)
                    ins = pe.matmul(o[:, f], AT[:, t, f], hi_row[:, t, f], start=True, stop=False,
                                    skip_group_check=True)
                    for half in range(2):
                        c = 2 * t + half
                        if c:
                            b = slice(half * CH, (half + 1) * CH)
                            ins = pe.matmul(o[b, f], logf[:, h, c * CH:(c + 1) * CH], state[:, c - 1, f],
                                            start=False, stop=True, skip_group_check=True)
                fill(ins, use)
            wout2_0 = rows_steps("wout2_0", hT_hi, hT_lo, turn_before("o2"))
            next(wout2_0)
            next(wout2_0)
            turn("o2", lambda: pe.wait_ge(hgrn_out_ready, T), range(2, 4))
            run(wout2_0)
            rows_panel("wout2_1", hT_hi, hT_lo)
            small[0] = 1
            rows_panel("wv1", memT_hi, memT_lo, b=4)
            turn("xpre")
            for p in range(2):
                cols_panel(f"wq{p}", hT_hi, hT_lo, turn_before("xpre"))
            for p in range(2):
                for j in range(2):
                    emptied(pe, (f"wk{p}", j))
                    emptied(pe, (f"wv{p}", j))
            attend("x")

            def crossed():
                for t in range(T):
                    for g in range(2):
                        emptied(pe, ("o", "x", t, g))

            turn("xo", crossed)
            for p in range(2):
                rows_panel(f"wo{p}", hT_hi, hT_lo, turn_before("xo"))
            ffn("gu", "dn", "ffnpre", 1)

        @block.sync
        def _(sp):
            count = [0] * NRAW
            for u, (name, k0, nk, cols, sources) in enumerate(units):
                slot = u % NRAW
                if u >= NRAW:
                    sp.wait_ge(w_lo_ready, u - NRAW + 1)
                dst = unit_view(raw[slot], u).rearrange("p (k n) -> p k n", k=nk)
                for c0, width, matrix, m0 in sources:
                    src = matrix[k0 * P:(k0 + nk) * P, m0:m0 + width].rearrange("(k p) n -> p k n", p=P)
                    sp.dma_start(dst[:, :, c0:c0 + width], src).then_inc(raw_landed[slot], 16)
                    count[slot] += 16
                landed[u] = count[slot]
            for t in range(T):
                sp.wait_ge(res_ready, RES["ffnpost"] - (T - 1 - t))
                sp.dma_start(out[0, t * P:(t + 1) * P, :], res[:, t, :]).then_inc(stored, 16)
            sp.wait_ge(stored, 16 * T)

        @block.gpsimd
        def _(pool):
            pool.memset(mhalf[:, :], -0.5).then_inc(mhalf_ready, 1)
            pool.wait_ge(mhalf_ready, 1)
            for n, name in enumerate(POWS):
                w = POW_COLS.get(name, T)
                pool.wait_ge(var_ready, n + 1)
                pool.tensor_tensor(rstd[:, n, 0:w], var[:, n, 0:w], mhalf[:, 0:w], ALU.pow).then_inc(rstd_ready, 1)

        @block.scalar
        def _(act):
            steps = [0]

            def step(ins):
                steps[0] += 1
                ins.then_inc(act_step, 1)

            def settle():
                act.wait_ge(act_step, steps[0])

            fed = [0]

            def feed(name):
                feed_units(last_unit[name] + 1 + NSPLIT if name else NSPLIT)

            def feed_units(stop):
                while fed[0] < min(stop, len(units)):
                    u = fed[0]
                    act.wait_ge(raw_landed[u % NRAW], landed[u])
                    if u >= NSPLIT:
                        released(act, u - NSPLIT)
                    act.activation(unit_view(w_hi[u % NSPLIT], u), unit_view(raw[u % NRAW], u),
                                   ACT.Copy).then_inc(w_hi_ready, 1)
                    fed[0] += 1

            act.dma_start(k0[:, :], const[:, 0:C_RCOS]).then_inc(in_ident, 16)
            for name, _ in VEC_GROUPS[0]:
                g, r, n = VEC[name]
                act.dma_start(vrow[g][r:r + n, :], vec_src[name]).then_inc(in_vec, 16)
            act.dma_start(in_ctx[:, :, :], a["ctx"].rearrange("(t p) d -> p t d", p=P)).then_inc(in_ctxx, 16)
            act.dma_start(res[:, :, :], a["x"].rearrange("(t p) d -> p t d", p=P)).then_inc(in_x, 16)
            for vs in VEC_GROUPS[1:]:
                for name, _ in vs:
                    g, r, n = VEC[name]
                    act.dma_start(vrow[g][r:r + n, :], vec_src[name]).then_inc(in_conv, 16)

            squares = [0]

            def square(name, part, t, src):
                if squares[0]:
                    act.wait_ge(ssq_ready, squares[0])
                act.activation(junk[:, 0:src.shape[1]], src, ACT.Square,
                               accum_out=square_column(name, part, t)).then_inc(ssq_ready, 1)
                squares[0] += 1

            def scale_row(name, src, dst):
                act.wait_ge(rstd_ready, POW[name] + 1)
                act.activation(dst, src, ACT.Copy, scale=rstd[:, POW[name], 1:2]).then_inc(row_ready_act, 1)

            def turn(name, after=None, pairs=None):
                kt, scaled = next(x[1:] for x in TURNS if x[0] == name)
                hi, _, c = turn_dst(name)
                limit = last_unit[after] + 1 + NSPLIT if after else 0
                for p in pairs or range(kt // 2):
                    if p != 1:
                        feed_units(min(fed[0] + 1, limit))
                    use = ("turn", name, p)
                    dst = hi[:, 2 * p:2 * p + 2, c:c + TOK]
                    if scaled:
                        emptied(act, use)
                        act.activation(dst, fbuf[:, p % 2, :, :], ACT.Copy).then_inc(turn_hi, 1)
                    else:
                        ready(act, use)
                        act.activation(dst, ps(use)[:, :].rearrange("p (k t) -> p k t", k=2),
                                       ACT.Copy).then_inc(turn_hi, 1)

            def halves_of(use, dst):
                ready(act, use)
                free(act.activation(dst, ps(use)[:, :].rearrange("p (k t) -> p k t", k=2), ACT.Copy), use)

            emptied(act, ("vec", 0))
            act.activation(csilu[:, 0, :], vec("c"), ACT.Silu).then_inc(csilu_ready, 1)
            act.activation(csilu[:, 1, :], vec("c_ctx"), ACT.Silu).then_inc(csilu_ready, 1)
            act.wait_ge(csilu_ready, 2)
            for i in range(2):
                act.activation(c_parts[:, :, 64 * i:64 * i + 32],
                               csilu[:, i, :].unsqueeze(2).broadcast_to([P, KD, 32]), ACT.Copy).then_inc(c_hi_ready, 1)
            feed(None)
            act.wait_ge(lb_in_ready, 2)
            act.activation(lbc[:, 1:3, :], lbc[:, 1:3, :], ACT.Exp).then_inc(lb_exp_ready, 1)

            def ada(p):
                use = (f"ada{p}", 0)
                ready(act, use)
                n = ADA_ORDER.index(p)
                if n >= 2:
                    ready(act, ("spread", ADA_ORDER[n - 2]))
                free(act.activation(modrow[:, p % 2, :], ps(use)[:, :], ACT.Copy), use)

            feed("ada0")
            ada(0)
            act.wait_ge(in_ctxx, 16)
            for t in range(T):
                square("ctx", 0, t, in_ctx[:, t, :])
            act.wait_ge(in_x, 16)
            for t in range(T):
                square("x1", 0, t, res[:, t, :])
            feed("ada1")
            ada(1)
            scale_row("ctx", in_ctx[:, 1, :], in_ctx[:, 1, :])
            scale_row("x1", res[:, 1, :], row[:, 1, :])
            for p in (2, 3):
                feed(f"ada{p}")
                ada(p)
            act.dma_start(k1[:, :], const[:, C_RCOS:C_E1]).then_inc(in_k1, 16)
            act.dma_start(lgam[:, :], a["ret_decay"].partition_broadcast(P)).then_inc(in_decay, 16)
            act.dma_start(g_ret[:, :], a["g_ret"].partition_broadcast(P)).then_inc(in_gains, 16)
            act.dma_start(gate[:, 0, :], a["b_ada"][2 * D:3 * D].partition_broadcast(P)).then_inc(in_gate, 16)
            act.dma_start(gate[:, 1, :], a["b_ada"][5 * D:6 * D].partition_broadcast(P)).then_inc(in_gate, 16)
            turn("x1")
            turn("ctx")
            ready(act, ("turn", "x1", 3))
            act.dma_start(row[:, :, :], a["mem_2"].rearrange("(t p) d -> p t d", p=P)).then_inc(in_mem, 16)

            feed("cq")
            for t in range(T):
                use = ("cq", t)
                ready(act, use)
                free(act.activation(cq_row[:, t, :], ps(use)[:, 0:256], ACT.Copy), use)
            for t in range(T):
                emptied(act, ("cq", t))
                square("cq", 0, t, cq_row[:, t, :])
            feed("ckvpe")
            for t in range(2 * T):
                use = ("ckvpe", t)
                ready(act, use)
                act.activation(ckv_row[:, t, :], ps(use)[:, 0:256], ACT.Copy)
                free(act.activation(kpe_row[:, t, :], ps(use)[:, 256:256 + ROPE], ACT.Copy), use)
            for t in range(2 * T):
                emptied(act, ("ckvpe", t))
                square(("ckv", "ckvc")[t // T], 0, t % T, ckv_row[:, t, :])
            act.wait_ge(in_mem, 16)
            for t in range(T):
                square("mem", 0, t, row[:, t, :])
            act.wait_ge(in_decay, 16)
            step(act.activation(lgam[:, :], lgam[:, :], ACT.Exp))
            settle()
            step(act.activation(lgam[:, :], lgam[:, :], ACT.Copy, scale=-1.0))
            settle()
            act.wait_ge(in_k1, 16)
            for d in range(2):
                for h in range(RH):
                    act.activation(wctx[:, d, h, :], k1[:, C_WEXP - C_RCOS + 2 * d:C_WEXP - C_RCOS + 2 * d + 2],
                                   ACT.Exp, scale=lgam[:, 4 * d + h:4 * d + h + 1]).then_inc(wctx_ready, 1)
            scale_row("mem", row[:, 1, :], row[:, 1, :])
            feed_units(fed[0] + 1)
            turn("mem")
            feed("rk")
            feed("rv")
            for t in range(2 * T):
                use = ("rv", t)
                ready(act, use)
                dst = rv_row if t < T else rvc_row
                free(act.activation(dst[:, t % T, :], ps(use)[:, :], ACT.Copy), use)
            for h in range(RH):
                act.wait_ge(decay_ready, h + 1)
                act.activation(decay[:, h, :, :], decay[:, h, :, :], ACT.Exp).then_inc(decay_exp_ready, 1)
            feed("rq")
            ready(act, ("end", "rv"))
            for h in range(RH):
                for d in range(2):
                    c = (C_XF, C_XB)[d] - C_RCOS
                    act.activation(xi[d][:, h, :], k1[:, c:c + TOK], ACT.Exp,
                                   scale=lgam[:, 4 * d + h:4 * d + h + 1]).then_inc(xi_ready, 1)
            for name in ("cq", "ckv", "ckvc"):
                feed_units(fed[0] + 1)
                turn(name)
            feed("rg")
            for t in range(T):
                use = ("rg", t)
                ready(act, use)
                free(act.activation(sgate[:, t, :], ps(use)[:, :], ACT.Silu), use)
            for what, dst in (("rk", rkT), ("rq", rqT)):
                for t in range(T):
                    use = ("rT", what, t)
                    ready(act, use)
                    free(act.activation(dst[:, :, t * P:(t + 1) * P],
                                        ps(use)[:, :].rearrange("p (h t) -> p h t", h=RH), ACT.Copy), use)
            for p in range(2):
                feed(f"uq{p}")
                for t in range(T):
                    use = (f"uq{p}", t)
                    ready(act, use)
                    free(act.activation(q_row[:, t, 4 * p:4 * p + 4, :],
                                        ps(use)[:, 0:384].rearrange("p (h d) -> p h d", h=4), ACT.Copy), use)
            feed("ada4")
            ada(4)
            feed("ada5")
            ada(5)
            for p in range(2):
                feed(f"ukv{p}")
                if p == 0:
                    for t in range(T):
                        for g in range(2):
                            use = ("qT", t, g)
                            ready(act, use)
                            free(act.activation(qT[0:DQ, 4 * g:4 * g + 4, t * P:(t + 1) * P],
                                                ps(use)[0:DQ, :].rearrange("p (h t) -> p h t", h=4), ACT.Copy), use)
                for t in range(T):
                    use = (f"ukv{p}", t)
                    ready(act, use)
                    v = ps(use)[:, :].rearrange("p (h d) -> p h d", h=4)
                    if p:
                        ready(act, ("kT", 0, t))
                    act.activation(V[:, t, 4 * p:4 * p + 4, :], v[:, :, NOPE:], ACT.Copy)
                    free(act.activation(k_row[:, t, :, 0:NOPE], v[:, :, 0:NOPE], ACT.Copy), use)
                feed(f"ada{10 + p}")
                ada(10 + p)
                act.wait_ge(ret_out_ready, T)
                for t in range(T):
                    use = ("kT", p, t)
                    ready(act, use)
                    free(act.activation(kT[0:DQ, 4 * p:4 * p + 4, t * P:(t + 1) * P],
                                        ps(use)[0:DQ, :].rearrange("p (h t) -> p h t", h=4), ACT.Copy), use)

            def attend(kind, events={}):
                scale = {"mla": MLA_SCALE, "swa": 1.0, "x": X_SCALE}[kind]
                rounds = [r for r in ROUNDS if r[0] == kind]
                start = ROUND[rounds[0]]
                base_unit = first_unit[FILLERS[kind][0]] if FILLERS[kind] else None

                def exponentials(r):
                    i = ROUND[r]
                    _, t, h = r
                    n = key_tiles(kind, t) * P
                    src = fbuf[:, i % 2, 0, 0:n] if kind == "swa" else ps(("score",) + r)[:, 0:n]
                    act.wait_ge(nmax_ready, i + 1)
                    before = i - PROBS[kind]
                    if i >= 2:
                        ready(act, ("probT",) + ROUNDS[before if before >= start else start - 1])
                    if kind == "swa":
                        act.activation(expsink[:, i:i + 1], sinks[:, h:h + 1], ACT.Exp, bias=nmax[:, i, 1:2])
                    ins = act.activation(prob_of(i)[:, 0:n], src, ACT.Exp, bias=nmax[:, i, 1:2], scale=scale,
                                         accum_out=rowsum[:, i:i + 1])
                    if kind == "swa":
                        ins.then_inc(exp_ready, 1)
                    else:
                        free(ins, ("score",) + r)

                def copy_turned(r):
                    i = ROUND[r]
                    n = key_tiles(kind, r[1]) * P
                    use = ("probT",) + r
                    ready(act, use)
                    if i >= 2:
                        multiplied(act, i - 2)
                    free(act.activation(probT[:, i % 2, 0:n], ps(use)[:, 0:n], ACT.Copy), use)

                for n, r in enumerate(rounds):
                    exponentials(r)
                    if n and (n - 1) % 2 == 0:
                        copy_turned(rounds[n - 1])
                    if base_unit is not None:
                        feed_units(min(base_unit + LEAD[kind] + n + NSPLIT, last_unit[FILLERS[kind][-1]] + 1 + NSPLIT))
                    for e in events.get(n, ()):
                        e()
                if base_unit is not None:
                    feed(FILLERS[kind][-1])

            attend("mla", {4: [lambda: ada(6)], 8: [lambda: ada(7)], 12: [lambda: ada(8)]})
            ada(9)
            turn("o")

            def square_gated(panel_name, name, extra=False):
                for p in range(2):
                    feed(f"{panel_name}{p}")
                    for t in range(T):
                        c = slice(512 * p, 512 * p + 512)
                        act.wait_ge(res_ready, RES[panel_name] - 2 * T + T * p + t + 1)
                        square(name, 2 * p if extra else p, t, res[:, t, c])
                        if extra:
                            act.wait_ge(xg_ready, T * p + t + 1)
                            square(name, 2 * p + 1, t, row[:, t, c])

            square_gated("wout", "x2")
            feed_units(last_unit["wk0"] + 1)
            scale_row("x2", res[:, 1, :], row[:, 1, :])
            turn("x2", "wk0")
            feed("wk0")
            for j in range(2):
                halves_of(("wk0", j), KxT[:, 2 * j:2 * j + 2, :])

            act.dma_start(g_final[:, :], a["g_final"].partition_broadcast(P)).then_inc(in_gains, 16)
            for p in range(NFF):
                feed(f"up{p}")
                ahead = "down0" if p == NFF - 1 else f"up{p + 1}"
                limit = last_unit[ahead] + 1 + NSPLIT
                for s in range(2):
                    use = (f"up{p}", s)
                    ready(act, use)
                    if p >= 2:
                        act.wait_ge(prod_ready, p - 1)
                    for j in range(2):
                        ch = KF * s + 2 * p + j
                        act.activation(conv[:, p % 2, s, j, :], ps(use)[:, j * TOK:(j + 1) * TOK], ACT.Identity,
                                       scale=vec("conv_w1", ch), bias=vec("conv_b", ch)).then_inc(conv_ready, 1)
                    if s:
                        feed_units(min(fed[0] + 1, limit))
                emptied(act, (f"up{p}", 1))
                act.activation(sg[:, p % 2, :, :], conv[:, p % 2, 1, :, :], ACT.Silu).then_inc(sg_ready, 1)
                feed_units(min(fed[0] + 1, limit))
                act.wait_ge(prod_ready, p + 1)
                act.activation(act_hi[:, 2 * p:2 * p + 2, :], prod[:, p % 2, :, :], ACT.Copy).then_inc(act_hi_ready, 1)
            square_gated("down", "final", True)
            feed_units(last_unit["wk1"] + 1)
            act.wait_ge(rs12_ready, 1)
            act.activation(mix_row[:, 1, :], row[:, 1, :], ACT.Copy, scale=rs12[:, 1:2]).then_inc(row_ready_act, 1)
            turn("mix", "wk1")
            act.wait_ge(res_ready, RES["down"])
            act.dma_start(k3[:, :], const[:, C_E1:C_END]).then_inc(in_k3, 16)
            act.dma_start(onorm[:, :], a["hgrn_onorm_2"].partition_broadcast(P)).then_inc(in_k3, 16)
            act.dma_start(sinks[:, :], a["sinks_2"].partition_broadcast(P)).then_inc(in_k3, 16)
            for n, g in enumerate(("g_mix_post_2", "g_x_post_2", "g_ffn_post_2")):
                act.dma_start(g_post[:, n, :], a[g].partition_broadcast(P)).then_inc(in_k3, 16)
            feed("wk1")
            for j in range(2):
                halves_of(("wk1", j), KxT[:, 4 + 2 * j:6 + 2 * j, :])

            feed("fh")
            for j in range(2):
                use = ("fh", j)
                ready(act, use)
                free(act.activation(kk_[:, 2 * j:2 * j + 2, :], ps(use)[:, :].rearrange("p (h t) -> p h t", h=2),
                                    ACT.Sigmoid), use)
            feed("qa")
            act.wait_ge(f_ready, 1)
            act.activation(logf[:, :, :], logf[:, :, :], ACT.Ln).then_inc(log_ready, 1)
            for j in range(2):
                halves_of(("qa", j), aqT[:, 2 * j:2 * j + 2, :])
            feed("qh")
            for j in range(2):
                use = ("qh", j)
                ready(act, use)
                free(act.activation(qs[:, 2 * j:2 * j + 2, :], ps(use)[:, :].rearrange("p (h t) -> p h t", h=2),
                                    ACT.Silu), use)
            feed("kva")
            use = ("kva", 1)
            ready(act, use)
            free(act.activation(avT[:, :], ps(use)[:, 0:TOK], ACT.Copy), use)
            use = ("kva", 0)
            ready(act, use)
            for g in range(2):
                for half in range(2):
                    ins = act.activation(akT[64 * half:64 * half + 64, g, :], ps(use)[64 * g:64 * g + 64, 0:TOK],
                                         ACT.Copy)
            free(ins, use)
            act.wait_ge(cum_ready, 1)
            act.activation(qd[:, :, :], bmid[:, :, :], ACT.Exp).then_inc(hexp_ready, 1)
            act.activation(e_b[:, :, :], bmid[:, :, :], ACT.Exp, scale=-1.0).then_inc(hexp_ready, 1)
            act.wait_ge(in_k3, 16 * 6)

            def copy_values():
                use = ("av",)
                ready(act, use)
                free(act.activation(av[:, :, :], ps(use)[:, 0:TOK].rearrange("p (t d) -> p t d", t=T), ACT.Copy), use)

            def decay_last():
                act.wait_ge(cum_ready, 2)
                act.activation(logf[:, :, :], logf[:, :, :], ACT.Exp).then_inc(hexp_ready, 1)

            def decay_first():
                act.wait_ge(hd_ready, 2)
                act.activation(e_b[:, :, :], cum[:, :, :], ACT.Exp).then_inc(hexp_ready, 1)

            def copy_row(name, dst):
                use = (name, 0)
                ready(act, use)
                free(act.activation(dst[:, 0, :], ps(use)[:, :], ACT.Copy), use)

            def copy_kz():
                for t in range(T):
                    use = ("kz", t)
                    ready(act, use)
                    free(act.activation(kz_row[:, t, :], ps(use)[:, :], ACT.Copy), use)

            attend("swa", {0: [copy_values], 1: [decay_last], 3: [decay_first], 4: [lambda: copy_row("ih", hi_row)], 7: [lambda: copy_row("gh", hg)],
                           11: [lambda: copy_row("wv0", Vx[:, :, 0:512]), copy_kz]})
            for t in range(T):
                emptied(act, ("gh", t))
            act.activation(hg[:, :, :], hg[:, :, :], ACT.Silu).then_inc(hg_ready, 1)
            turn("o2", None, range(2))
            for t in range(T):
                use = ("ho", t)
                ready(act, use)
                for h in range(HH):
                    if HH * t + h == 0:
                        act.wait_ge(ssq_ready, squares[0])
                    j = (HH * t + h) * P
                    act.activation(junk[:, j:j + P], ps(use)[:, h * P:(h + 1) * P], ACT.Square,
                                   accum_out=hsq[:, t, h:h + 1]).then_inc(hsq_ready, 1)
            act.wait_ge(hsq_ready, T * HH)
            turn("o2", None, range(2, 4))

            def square_out(panel_name, name):
                for p in range(2):
                    feed(f"{panel_name}{p}")
                    for t in range(T):
                        ready(act, (f"{panel_name}{p}", t))
                        square(name, p, t, ps((f"{panel_name}{p}", t))[:, :])

            def square_res(name, after):
                for t in range(T):
                    act.wait_ge(res_ready, RES[after] - (T - 1 - t))
                    square(name, 0, t, res[:, t, :])
                scale_row(name, res[:, 1, :], row[:, 1, :])

            square_out("wout2_", "mixpost")
            feed_units(last_unit["wv1"] + 1)
            square_res("xpre", "mixpost")
            copy_row("wv1", Vx[:, :, 512:])
            turn("xpre", "wv1")
            feed("wv1")
            for p in range(2):
                feed(f"wq{p}")
                for j in range(2):
                    halves_of((f"wq{p}", j), sxqT[:, 4 * p + 2 * j:4 * p + 2 * j + 2, :])
            attend("x")
            turn("xo")
            square_out("wo", "xpost")
            square_res("ffnpre", "xpost")
            turn("ffnpre")
            for p in range(NFF):
                feed(f"gu{p}")
                use = (f"gu{p}", 0)
                ready(act, use)
                if p >= 2:
                    emptied(act, (f"gu{p - 2}", 1))
                free(act.activation(sg[:, p % 2, :, :], ps(use)[:, :].rearrange("p (k t) -> p k t", k=2),
                                    ACT.Silu), use)
                emptied(act, (f"gu{p}", 1))
                act.activation(act_hi[:, 2 * p:2 * p + 2, :], prod[:, p % 2, :, :], ACT.Copy).then_inc(act_hi_ready, 1)
            square_out("dn", "ffnpost")

        @block.vector
        def _(dve):
            steps = [0]

            def step(ins):
                steps[0] += 1
                ins.then_inc(dve_step, 1)

            def settle():
                dve.wait_ge(dve_step, steps[0])

            fed = [0]

            def feed(name):
                feed_units(last_unit[name] + 1 + NSPLIT if name else NSPLIT)

            def feed_units(stop):
                while fed[0] < min(stop, len(units)):
                    u = fed[0]
                    dve.wait_ge(w_hi_ready, u + 1)
                    dve.tensor_tensor(unit_view(w_lo[u % NSPLIT], u), unit_view(raw[u % NRAW], u),
                                      unit_view(w_hi[u % NSPLIT], u).bitcast(F32), ALU.subtract).then_inc(w_lo_ready, 1)
                    fed[0] += 1

            def variance(name):
                c, w, parts = SUMS_BEFORE[name], WIDTH[name], PARTS[name]
                n = POW[name]
                dve.wait_ge(ssq_ready, c + T * parts)
                if parts == 1:
                    dve.tensor_scalar(var[:, n, 0:T], ssq[:, c:c + T], 1.0 / w, EPS, ALU.mult,
                                      ALU.add).then_inc(var_ready, 1)
                    return
                m = T * parts // 2
                step(dve.tensor_tensor(sums[:, 0:m], ssq[:, c:c + m], ssq[:, c + m:c + 2 * m], ALU.add))
                settle()
                ins = dve.tensor_scalar(var[:, n, 0:T], sums[:, 0:T], 1.0 / w, EPS, ALU.mult, ALU.add)
                if parts == 4:
                    step(ins)
                    settle()
                    step(dve.reciprocal(sums[:, 4:6], var[:, n, 0:T]))
                    settle()
                    step(dve.tensor_tensor(sums[:, 6:8], sums[:, 2:4], sums[:, 4:6], ALU.mult))
                    settle()
                    ins = dve.tensor_scalar(var[:, n, T:2 * T], sums[:, 6:8], 1.0 / w, EPS, ALU.mult, ALU.add)
                ins.then_inc(var_ready, 1)

            def scale_rows(name, srcs, dsts):
                dve.wait_ge(rstd_ready, POW[name] + 1)
                for t in range(len(srcs)):
                    dve.tensor_scalar(dsts[t], srcs[t], rstd[:, POW[name], t:t + 1], None, ALU.mult).then_inc(row_ready, 1)

            def turn(name, after=None, pairs=None):
                kt, scaled = next(x[1:] for x in TURNS if x[0] == name)
                hi, lo, c = turn_dst(name)
                limit = last_unit[after] + 1 + NSPLIT if after else 0

                def full(p):
                    use = ("turn", name, p)
                    ready(dve, use)
                    before = turn_lo_at[name, p] - 2 if p >= 2 else turn_lo_at[name, 0] - 1
                    if before:
                        dve.wait_ge(turn_lo, before)
                    for kk in range(2):
                        gain, shift = turn_gain(name, 2 * p + kk)
                        src = ps(use)[:, kk * TOK:(kk + 1) * TOK]
                        if shift is None:
                            ins = dve.tensor_scalar(fbuf[:, p % 2, kk, :], src, gain, None, ALU.mult)
                        else:
                            ins = dve.tensor_scalar(fbuf[:, p % 2, kk, :], src, gain, shift, ALU.mult, ALU.add)
                    free(ins, use)

                def rest(p):
                    use = ("turn", name, p)
                    h, l = hi[:, 2 * p:2 * p + 2, c:c + TOK], lo[:, 2 * p:2 * p + 2, c:c + TOK]
                    dve.wait_ge(turn_hi, turn_hi_at[name, p])
                    if scaled:
                        dve.tensor_tensor(l, fbuf[:, p % 2, :, :], h.bitcast(F32), ALU.subtract).then_inc(turn_lo, 1)
                    else:
                        free(dve.tensor_tensor(l, ps(use)[:, :].rearrange("p (k t) -> p k t", k=2), h.bitcast(F32),
                                               ALU.subtract), use)

                n = kt // 2
                feed_units(min(fed[0] + 1, limit))
                if scaled:
                    full(0)
                for p in pairs or range(n):
                    if scaled and p + 1 < n:
                        full(p + 1)
                    rest(p)
                    if p in (1, 2):
                        feed_units(min(fed[0] + 1, limit))

            def columns(g):
                ready(dve, ("vec", g))
                n = vcol[g].shape[1]
                free(dve.tensor_copy(vcol[g][:, :], ps(("vec", g))[:, 0:n]), ("vec", g))

            columns(0)
            emptied(dve, ("vec", 0))
            lb = vec("hgrn_lb_2")
            step(dve.tensor_tensor(lbc[:, 0, :], lb[:, 0:HH], lb[:, HH:2 * HH], ALU.max))
            settle()
            for i in range(2):
                dve.tensor_tensor(lbc[:, 1 + i, :], lb[:, i * HH:(i + 1) * HH], lbc[:, 0, :],
                                  ALU.subtract).then_inc(lb_in_ready, 1)
            dve.wait_ge(c_hi_ready, 2)
            for i in range(2):
                dve.tensor_tensor(c_parts[:, :, 64 * i + 32:64 * i + 64],
                                  csilu[:, i, :].unsqueeze(2).broadcast_to([P, KD, 32]),
                                  c_parts[:, :, 64 * i:64 * i + 32].bitcast(F32), ALU.subtract).then_inc(c_lo_ready, 1)
            feed(None)

            def spread(p):
                use = ("spread", p)
                ready(dve, use)
                b = vec("b_ada")
                if p in (4, 5, 10, 11):
                    g = gate[:, p // 8, 512 * (p % 2):512 * (p % 2) + 512]
                    if p == 4:
                        dve.wait_ge(in_gate, 32)
                    free(dve.tensor_tensor(g, g, ps(use)[:, :], ALU.add), use)
                    return
                o = ps(use)[:, 0:8].rearrange("p (j c) -> p j c", c=2)
                ins = dve.tensor_tensor(modc[:, 4 * p:4 * p + 4], o[:, :, 0], b[:, 4 * p:4 * p + 4], ALU.add)
                if p < 4:
                    step(ins)
                    ins = dve.tensor_tensor(modx[:, 4 * p:4 * p + 4], o[:, :, 1], b[:, 4 * p:4 * p + 4], ALU.add)
                free(ins, use)

            def gain_column(n, scale, g, uses):
                for use in uses:
                    emptied(dve, use)
                settle()
                step(dve.scalar_tensor_tensor(acol[:, n, :], scale, 1.0, vec(g), ALU.add, ALU.mult))

            feed("ada0")
            columns(1)
            columns(2)
            variance("ctx")
            variance("x1")
            feed("ada1")
            spread(0)
            scale_rows("ctx", [in_ctx[:, 0, :]], [in_ctx[:, 0, :]])
            scale_rows("x1", [res[:, 0, :]], [row[:, 0, :]])
            for p in (2, 3):
                feed(f"ada{p}")
                spread(p - 1)
            spread(3)
            gain_column(0, modc[:, 8:16], "g_norm1", [("spread", p) for p in range(4)])
            gain_column(2, modx[:, 8:16], "g_norm1", [])
            settle()
            turn("x1")
            turn("ctx")
            dve.wait_ge(lb_exp_ready, 1)
            step(dve.tensor_tensor(lbc[:, 3, :], lbc[:, 1, :], lbc[:, 2, :], ALU.add))
            settle()
            step(dve.reciprocal(lbc[:, 3, :], lbc[:, 3, :]))
            settle()
            step(dve.tensor_tensor(lbc[:, 4, :], lbc[:, 1, :], lbc[:, 3, :], ALU.mult))
            settle()
            step(dve.tensor_scalar(lbc[:, 5, :], lbc[:, 4, :], -1.0, 1.0, ALU.mult, ALU.add))

            def turn_pairs(dst0, dst1, a0, a1, b0, b1):
                step(dve.tensor_tensor(dst0, a0, b1, ALU.subtract))
                return dve.tensor_tensor(dst1, a1, b0, ALU.add)

            feed("cq")
            feed("ckvpe")
            for name in ("cq", "ckv", "ckvc"):
                variance(name)
            scale_rows("cq", [cq_row[:, t, :] for t in range(T)], [cq_row[:, t, :] for t in range(T)])
            scale_rows("ckv", [ckv_row[:, t, :] for t in range(T)], [ckv_row[:, t, :] for t in range(T)])
            scale_rows("ckvc", [ckv_row[:, T + t, :] for t in range(T)], [ckv_row[:, T + t, :] for t in range(T)])
            variance("mem")
            scale_rows("mem", [row[:, 0, :]], [row[:, 0, :]])
            dve.wait_ge(in_k1, 16)
            dve.wait_ge(wctx_ready, 8)
            for h in range(RH):
                dst = decay[:, h, :, :].rearrange("p a b -> p (a b)")
                step(dve.tensor_scalar(dst, k1[:, C_PF - C_RCOS:C_PB - C_RCOS], lgam[:, h:h + 1], None, ALU.mult))
            settle()
            for h in range(RH):
                dst = decay[:, h, :, :].rearrange("p a b -> p (a b)")
                dve.scalar_tensor_tensor(dst, k1[:, C_PB - C_RCOS:C_XF - C_RCOS], lgam[:, RH + h:RH + h + 1], dst,
                                         ALU.mult, ALU.add).then_inc(decay_ready, 1)

            def mla_table(c, t):
                return k1[:, c - C_RCOS + t * ROPE:c - C_RCOS + (t + 1) * ROPE]

            def halves(x, h):
                v = x.rearrange("p h (a b c) -> p h a b c", a=2, b=2)
                return v[:, :, :, h, :]

            def rope_mla(x, t, heads):
                tmp = []
                for i, c in enumerate((C_MCOS, C_MSIN)):
                    o = rtmp[:, i, 0:heads * ROPE].rearrange("p (h d) -> p h d", h=heads)
                    step(dve.tensor_tensor(o, x, mla_table(c, t).unsqueeze(1).broadcast_to([P, heads, ROPE]), ALU.mult))
                    tmp.append(o)
                settle()
                A, B = tmp
                return turn_pairs(halves(x, 0), halves(x, 1), halves(A, 0), halves(A, 1), halves(B, 0), halves(B, 1))

            for t in range(T):
                emptied(dve, ("ckvpe", t))
                step(rope_mla(kpe_row[:, t:t + 1, :], t, 1))
                settle()
            def rope_ret(use, t, dst):
                ready(dve, use)
                x = ps(use)[:, :].rearrange("p (g d) -> p g d", d=64)
                tmp = []
                for i, c in enumerate((C_RCOS, C_RSIN)):
                    c += t * 64 - C_RCOS
                    o = rtmp[:, i, :].rearrange("p (g d) -> p g d", d=64)
                    ins = dve.tensor_tensor(o, x, k1[:, c:c + 64].unsqueeze(1).broadcast_to([P, 2 * RH, 64]), ALU.mult)
                    if i == 0:
                        step(ins)
                    else:
                        free(ins, use)
                    tmp.append(rtmp[:, i, :].rearrange("p (h b d) -> p h b d", b=2, d=64))
                settle()
                emptied(dve, use)
                A, B = tmp
                o = dst[:, t, :].rearrange("p (h b d) -> p h b d", b=2, d=64)
                turn_pairs(o[:, :, 0, :], o[:, :, 1, :], A[:, :, 0, :], A[:, :, 1, :], B[:, :, 0, :],
                           B[:, :, 1, :]).then_inc(ret_row_ready, 1)
                dve.wait_ge(ret_row_ready, rope_count[0] + 1)
                rope_count[0] += 1

            rope_count = [0]
            feed_units(fed[0] + 1)
            turn("mem")
            feed("rk")
            for t in range(T):
                rope_ret(("rk", t), t, rk_row)
            feed_units(fed[0] + 1)
            dve.wait_ge(wctx_ready, 8)
            for t in range(T):
                use = ("rk", T + t)
                ready(dve, use)
                for d, dst in enumerate((rkf, rkb)):
                    for h in range(RH):
                        ins = dve.tensor_scalar(dst[:, t, h * P:(h + 1) * P], ps(use)[:, h * P:(h + 1) * P],
                                                wctx[:, d, h, t:t + 1], RET_SCALE, ALU.mult, ALU.mult)
                free(ins, use)
                feed_units(fed[0] + 1)
            feed("rv")
            feed("rq")
            for t in range(T):
                rope_ret(("rq", t), t, rq_row)
            for name in ("cq", "ckv", "ckvc"):
                feed_units(fed[0] + 1)
                turn(name)
            feed("rg")
            for d in range(2):
                use = ("rstate", d)
                ready(dve, use)
                free(dve.tensor_copy(rstate[:, d, :], ps(use)[:, :]), use)
            dve.wait_ge(decay_exp_ready, RH)
            for h in range(RH):
                use = ("ratt", h)
                ready(dve, use)
                dst = decay[:, h, :, :].rearrange("p a b -> p (a b)")
                free(dve.scalar_tensor_tensor(dst, ps(use)[:, :], RET_SCALE, dst, ALU.mult, ALU.mult), use)
            feed("uq0")
            dve.wait_ge(xi_ready, 2 * RH)
            for t in range(T):
                emptied(dve, ("rT", "rq", t))
            for d in range(2):
                dve.tensor_tensor(xi[d][:, :, :], xi[d][:, :, :], rqT[:, :, :], ALU.mult).then_inc(qx_ready, 1)
            feed("uq1")
            feed("ada4")
            feed("ada5")
            spread(4)
            for t in range(T):
                for p in range(2):
                    emptied(dve, (f"uq{p}", t))
                rope_mla(q_row[:, t, :, NOPE:], t, MLA_H).then_inc(q_row_ready, 1)
                dve.wait_ge(q_row_ready, t + 1)
            dve.wait_ge(in_gains, 16)
            for t in range(T):
                emptied(dve, ("rg", t))
                step(dve.tensor_tensor(sgate[:, t, :], sgate[:, t, :], g_ret[:, :], ALU.mult))
            for t in range(T):
                ready(dve, ("ret", t))
                for h in range(RH):
                    step(dve.bn_stats(bn[:, t, h, :], ps(("ret", t))[:, h * P:(h + 1) * P]))
            settle()
            for t in range(T):
                for h in range(RH):
                    step(dve.bn_aggr(mv[:, t, h, :], bn[:, t, h, :]))
            settle()
            dve.tensor_scalar(var[:, POW["ret"], :].rearrange("p (t h) -> p t h", t=T), mv[:, :, :, 1], 1.0, EPS,
                              ALU.mult, ALU.add).then_inc(var_ready, 1)
            feed_units(fed[0] + 1)
            dve.wait_ge(rstd_ready, POW["ret"] + 1)
            for t in range(T):
                use = ("ret", t)
                for h in range(RH):
                    ins = dve.tensor_scalar(row[:, t, 512 + h * P:512 + (h + 1) * P], ps(use)[:, h * P:(h + 1) * P],
                                            mv[:, t, h, 0:1], rstd[:, POW["ret"], RH * t + h:RH * t + h + 1],
                                            ALU.subtract, ALU.mult)
                free(ins, use)
            feed_units(fed[0] + 1)
            for t in range(T):
                emptied(dve, ("ret", t))
                dve.tensor_tensor(row[:, t, 512:], row[:, t, 512:], sgate[:, t, :], ALU.mult).then_inc(ret_out_ready, 1)
            dve.wait_ge(ret_out_ready, T)
            for t in range(2 * T):
                emptied(dve, ("ckvpe", t))
                dve.tensor_copy(k_row[:, t, :, NOPE:], kpe_row[:, t, :].unsqueeze(1).broadcast_to([P, MLA_H // 2, ROPE])
                                ).then_inc(kpe_ready, 1)
            for p in range(2):
                feed(f"ukv{p}")
                spread((5, 10)[p])
                for t in range(T, 2 * T):
                    use = (f"ukv{p}", t)
                    ready(dve, use)
                    v = ps(use)[:, :].rearrange("p (h d) -> p h d", h=4)
                    if p:
                        ready(dve, ("kT", 0, t))
                    dve.tensor_copy(V[:, t, 4 * p:4 * p + 4, :], v[:, :, NOPE:])
                    free(dve.tensor_copy(k_row[:, t, :, 0:NOPE], v[:, :, 0:NOPE]), use)
                    feed_units(min(fed[0] + 1, last_unit[f"ada{10 + p}"] + 1))
                feed(f"ada{10 + p}")
                for t in range(T, 2 * T):
                    use = ("kT", p, t)
                    ready(dve, use)
                    free(dve.tensor_copy(kT[0:DQ, 4 * p:4 * p + 4, t * P:(t + 1) * P],
                                         ps(use)[0:DQ, :].rearrange("p (h t) -> p h t", h=4)), use)

            def attend(kind, events={}):
                rounds = [r for r in ROUNDS if r[0] == kind]
                start = ROUND[rounds[0]]
                base_unit = first_unit[FILLERS[kind][0]] if FILLERS[kind] else None

                def maxima(r):
                    i = ROUND[r]
                    _, t, h = r
                    n = key_tiles(kind, t) * P
                    use = ("score",) + r
                    ready(dve, use)
                    if kind == "swa":
                        if i - 2 >= start:
                            dve.wait_ge(exp_ready, i - 2 - start + 1)
                        c = C_SWA - C_E1 + t * P
                        s = fbuf[:, i % 2, 0, 0:n]
                        free(dve.scalar_tensor_tensor(s, ps(use)[:, 0:n], SWA_SCALE, k3[:, c:c + n], ALU.mult, ALU.add), use)
                        emptied(dve, use)
                        step(dve.tensor_reduce(nmax[:, i, 0:1], s, AX_X, ALU.max))
                        settle()
                        dve.tensor_scalar(nmax[:, i, 1:2], nmax[:, i, 0:1], sinks[:, h:h + 1], -1.0,
                                          ALU.max, ALU.mult).then_inc(nmax_ready, 1)
                    else:
                        step(dve.tensor_reduce(nmax[:, i, 0:1], ps(use)[:, 0:n], AX_X, ALU.max))
                        settle()
                        dve.tensor_scalar(nmax[:, i, 1:2], nmax[:, i, 0:1], -(MLA_SCALE if kind == "mla" else X_SCALE),
                                          None, ALU.mult).then_inc(nmax_ready, 1)

                def copy_turned(r):
                    i = ROUND[r]
                    n = key_tiles(kind, r[1]) * P
                    use = ("probT",) + r
                    ready(dve, use)
                    if i >= 2:
                        multiplied(dve, i - 2)
                    free(dve.tensor_copy(probT[:, i % 2, 0:n], ps(use)[:, 0:n]), use)

                for n, r in enumerate(rounds):
                    maxima(r)
                    if n and (n - 1) % 2:
                        copy_turned(rounds[n - 1])
                    if n >= 2 and group_of(rounds[n - 2])[2]:
                        divide(rounds[n - 2])
                    if base_unit is not None:
                        feed_units(min(base_unit + LEAD[kind] + n + NSPLIT - 1, last_unit[FILLERS[kind][-1]] + 1 + NSPLIT))
                    for e in events.get(n, ()):
                        e()
                copy_turned(rounds[-1])
                if base_unit is not None:
                    feed(FILLERS[kind][-1])
                divide(rounds[-1])

            def divide(r):
                kind, t, _ = r
                group, n, _ = group_of(r)
                n += 1
                i0 = ROUND[r] - n + 1
                use = ("o",) + group
                ready(dve, use)
                total = rowsum
                if kind == "swa":
                    step(dve.tensor_tensor(denom[:, i0:i0 + n], rowsum[:, i0:i0 + n], expsink[:, i0:i0 + n], ALU.add))
                    settle()
                    total = denom
                step(dve.reciprocal(rinv[:, i0:i0 + n], total[:, i0:i0 + n]))
                settle()
                c = 512 * group[2]
                free(dve.tensor_tensor(row[:, t, c:c + 512].rearrange("p (h d) -> p h d", h=n),
                                       ps(use)[:, :].rearrange("p (h d) -> p h d", h=n),
                                       rinv[:, i0:i0 + n].unsqueeze(2).broadcast_to([P, n, 512 // n]), ALU.mult), use)

            spread(11)
            attend("mla", {6: [lambda: spread(6)], 10: [lambda: spread(7)], 14: [lambda: spread(8)]})
            spread(9)
            gain_column(1, modc[:, 32:40], "g_norm2", [("spread", 8), ("spread", 9)])
            turn("o")

            tmp = fbuf[:, :, :, :].rearrange("p a b c -> p (a b c)")

            def gated(name, g):
                for p in range(2):
                    feed(f"{name}{p}")
                    for t in range(T):
                        use = (f"{name}{p}", t)
                        ready(dve, use)
                        c = slice(512 * p, 512 * p + 512)
                        o = tmp[:, 512 * (t % 2):512 * (t % 2) + 512]
                        free(dve.tensor_tensor(o, ps(use)[:, :], gate[:, g, c], ALU.mult), use)
                        emptied(dve, use)
                        dve.tensor_tensor(res[:, t, c], res[:, t, c], o, ALU.add).then_inc(res_ready, 1)
                        if name == "down":
                            dve.wait_ge(res_ready, RES["down"] - 2 * T + T * p + t + 1)
                            dve.tensor_tensor(row[:, t, c], res[:, t, c], g_final[:, c], ALU.mult).then_inc(xg_ready, 1)

            def prenorm(name, after, ahead=None):
                variance(name)
                if ahead:
                    feed_units(last_unit[ahead] + 1)
                dve.wait_ge(res_ready, RES[after])
                scale_rows(name, [res[:, 0, :]], [row[:, 0, :]])

            emptied(dve, ("spread", 5))
            gated("wout", 0)
            prenorm("x2", "wout", "wk0")
            turn("x2", "wk0")
            feed("wk0")
            for p in range(NFF):
                feed(f"up{p}")
                ahead = "down0" if p == NFF - 1 else f"up{p + 1}"
                limit = last_unit[ahead] + 1 + NSPLIT
                for s in range(2):
                    use = (f"up{p}", s)
                    ready(dve, use)
                    dve.wait_ge(conv_ready, 4 * p + 2 * s + 2)
                    for j in range(2):
                        u = ps(use)[:, j * TOK:(j + 1) * TOK]
                        o = conv[:, p % 2, s, j, :]
                        ch = KF * s + 2 * p + j
                        step(dve.scalar_tensor_tensor(o[:, 1:TOK], u[:, 0:TOK - 1], vec("conv_w0", ch), o[:, 1:TOK],
                                                      ALU.mult, ALU.add))
                    settle()
                    for j in range(2):
                        u = ps(use)[:, j * TOK:(j + 1) * TOK]
                        o = conv[:, p % 2, s, j, :]
                        ch = KF * s + 2 * p + j
                        ins = dve.scalar_tensor_tensor(o[:, 0:TOK - 1], u[:, 1:TOK], vec("conv_w2", ch), o[:, 0:TOK - 1],
                                                       ALU.mult, ALU.add)
                    free(ins, use)
                feed_units(min(fed[0] + 1, limit))
                emptied(dve, (f"up{p}", 0))
                dve.wait_ge(sg_ready, p + 1)
                dve.tensor_tensor(prod[:, p % 2, :, :], conv[:, p % 2, 0, :, :], sg[:, p % 2, :, :],
                                  ALU.mult).then_inc(prod_ready, 1)
                feed_units(min(fed[0] + 1, limit))
                dve.wait_ge(act_hi_ready, p + 1)
                dve.tensor_tensor(act_lo[:, 2 * p:2 * p + 2, :], prod[:, p % 2, :, :],
                                  act_hi[:, 2 * p:2 * p + 2, :].bitcast(F32), ALU.subtract).then_inc(act_lo_ready, 1)
            dve.wait_ge(in_gains, 32)
            gated("down", 1)
            variance("final")
            feed_units(last_unit["wk1"] + 1)
            dve.wait_ge(rstd_ready, POW["final"] + 1)
            dve.tensor_tensor(rs12[:, :], rstd[:, POW["final"], 0:T], rstd[:, POW["final"], T:2 * T],
                              ALU.mult).then_inc(rs12_ready, 1)
            dve.wait_ge(rs12_ready, 1)
            dve.wait_ge(xg_ready, 4)
            dve.tensor_scalar(mix_row[:, 0, :], row[:, 0, :], rs12[:, 0:1], None, ALU.mult).then_inc(row_ready, 1)
            turn("mix", "wk1")
            for t in range(T):
                dve.tensor_scalar(res[:, t, :], row[:, t, :], rstd[:, POW["final"], t:t + 1], None,
                                  ALU.mult).then_inc(res_ready, 1)
            feed("wk1")
            dve.memset(AT[:, :, :], 0.0).then_inc(dve_step, 1)
            steps[0] += 1
            feed("fh")
            for j in range(2):
                emptied(dve, ("fh", j))
            for h in range(HH):
                step(dve.tensor_scalar(logf[:, h, :], kk_[:, h, :], lbc[:, 5, h:h + 1], lbc[:, 4, h:h + 1],
                                       ALU.mult, ALU.add))
            settle()
            dve.tensor_scalar(kk_[:, :, :], logf[:, :, :], -1.0, 1.0, ALU.mult, ALU.add).then_inc(f_ready, 1)
            feed("qa")
            dve.wait_ge(in_k3, 16 * 6)
            dve.wait_ge(log_ready, 1)
            for h in range(HH):
                c = C_SCAN - C_E1
                step(dve.tensor_tensor_scan(cum[:, h, :], k3[:, c:c + TOK], logf[:, h, :], 0.0, ALU.mult, ALU.add))
            settle()

            def by_chunk(x):
                return x[:, :, :].rearrange("p h (c j) -> p (h c) j", j=CH)

            def at_position(j):
                return by_chunk(cum)[:, :, j:j + 1].broadcast_to([P, HH * 4, CH])

            dve.tensor_tensor(by_chunk(bmid), by_chunk(cum), at_position(CH // 2 - 1), ALU.subtract).then_inc(cum_ready, 1)
            dve.tensor_tensor(by_chunk(logf), at_position(CH - 1), by_chunk(cum), ALU.subtract).then_inc(cum_ready, 1)
            feed("qh")
            feed("kva")
            for j in range(2):
                emptied(dve, ("qh", j))
            dve.wait_ge(hexp_ready, 2)

            def q_mid():
                dve.scalar_tensor_tensor(qd[:, :, :], qs[:, :, :], HG_SCALE, qd[:, :, :], ALU.mult,
                                         ALU.mult).then_inc(hd_ready, 1)

            def k_mid():
                dve.wait_ge(f_ready, 1)
                dve.tensor_tensor(bmid[:, :, :], kk_[:, :, :], e_b[:, :, :], ALU.mult).then_inc(hd_ready, 1)

            def k_last():
                dve.wait_ge(hexp_ready, 3)
                dve.tensor_tensor(kk_[:, :, :], kk_[:, :, :], logf[:, :, :], ALU.mult).then_inc(hd_ready, 1)

            def q_first():
                dve.wait_ge(hexp_ready, 4)
                dve.wait_ge(hd_ready, 3)
                dve.scalar_tensor_tensor(logf[:, :, :], qs[:, :, :], HG_SCALE, e_b[:, :, :], ALU.mult,
                                         ALU.mult).then_inc(hd_ready, 1)

            def copy_row(name, dst):
                use = (name, 1)
                ready(dve, use)
                free(dve.tensor_copy(dst[:, 1, :], ps(use)[:, :]), use)

            def mask_scores():
                for t in range(T):
                    use = ("A", t)
                    ready(dve, use)
                    c = C_CAUS - C_E1
                    free(dve.copy_predicated(AT[:, t, :], k3[:, c:c + 512].bitcast(U32), ps(use)[:, :]), use)

            def states(chunks):
                for c in chunks:
                    use = ("kv", c)
                    ready(dve, use)
                    if c == 0:
                        ins = dve.tensor_copy(state[:, 0, :], ps(use)[:, :])
                    else:
                        emptied(dve, ("kv", c - 1))
                        for h in range(HH):
                            f = slice(h * P, (h + 1) * P)
                            d = e_b[:, h, c * CH + CH - 1:c * CH + CH]
                            ins = dve.scalar_tensor_tensor(state[:, c, f], state[:, c - 1, f], d, ps(use)[:, f],
                                                           ALU.mult, ALU.add)
                    free(ins, use)

            attend("swa", {0: [q_mid], 1: [k_mid], 2: [k_last], 3: [lambda: copy_row("ih", hi_row)], 4: [q_first],
                           7: [lambda: copy_row("gh", hg)], 11: [lambda: copy_row("wv0", Vx[:, :, 0:512])],
                           12: [mask_scores], 13: [lambda: states((0, 1))], 14: [lambda: states((2,))]})
            dve.wait_ge(hg_ready, 1)
            v = hg[:, :, :].rearrange("p t (h d) -> p (t h) d", h=HH)
            step(dve.tensor_tensor(v, v, onorm[:, :].unsqueeze(1).broadcast_to([P, T * HH, P]), ALU.mult))
            turn("o2", None, range(2))
            dve.wait_ge(hsq_ready, T * HH)
            dve.tensor_scalar(var[:, POW["hgrn"], :], hsq[:, :, :].rearrange("p t h -> p (t h)"), 1.0 / P, EPS,
                              ALU.mult, ALU.add).then_inc(var_ready, 1)
            dve.wait_ge(rstd_ready, POW["hgrn"] + 1)
            for t in range(T):
                use = ("ho", t)
                free(dve.tensor_tensor(row[:, t, 512:].rearrange("p (h d) -> p h d", h=HH),
                                       ps(use)[:, :].rearrange("p (h d) -> p h d", h=HH),
                                       rstd[:, POW["hgrn"], HH * t:HH * t + HH].unsqueeze(2).broadcast_to([P, HH, P]),
                                       ALU.mult), use)
            settle()
            for t in range(T):
                emptied(dve, ("ho", t))
                dve.tensor_tensor(row[:, t, 512:], row[:, t, 512:], hg[:, t, :], ALU.mult).then_inc(hgrn_out_ready, 1)
            turn("o2", None, range(2, 4))

            def postnorm(name, panel_name, n, ahead=None):
                def times_gain(p, t):
                    use = (f"{panel_name}{p}", t)
                    c = slice(512 * p, 512 * p + 512)
                    dve.wait_ge(ssq_ready, SUMS_BEFORE[name] + T * p + t + 1)
                    free(dve.tensor_tensor(row[:, t, c], ps(use)[:, :], g_post[:, n, c], ALU.mult), use)

                for p in range(2):
                    feed(f"{panel_name}{p}")
                    for t in range(T - p):
                        times_gain(p, t)
                variance(name)
                times_gain(1, 1)
                if ahead:
                    feed_units(last_unit[ahead] + 1)
                dve.wait_ge(rstd_ready, POW[name] + 1)
                for t in range(T):
                    for p in range(2):
                        emptied(dve, (f"{panel_name}{p}", t))
                    dve.scalar_tensor_tensor(res[:, t, :], row[:, t, :], rstd[:, POW[name], t:t + 1], res[:, t, :],
                                             ALU.mult, ALU.add).then_inc(res_ready, 1)

            postnorm("mixpost", "wout2_", 0, "wv1")
            prenorm("xpre", "mixpost")
            copy_row("wv1", Vx[:, :, 512:])
            turn("xpre", "wv1")
            feed("wv1")
            for p in range(2):
                feed(f"wq{p}")
            attend("x")
            turn("xo")
            postnorm("xpost", "wo", 1)
            prenorm("ffnpre", "xpost")
            turn("ffnpre")
            for p in range(NFF):
                feed(f"gu{p}")
                use = (f"gu{p}", 1)
                ready(dve, use)
                emptied(dve, (f"gu{p}", 0))
                free(dve.tensor_tensor(prod[:, p % 2, :, :], ps(use)[:, :].rearrange("p (k t) -> p k t", k=2),
                                       sg[:, p % 2, :, :], ALU.mult), use)
                dve.wait_ge(act_hi_ready, NFF + p + 1)
                dve.tensor_tensor(act_lo[:, 2 * p:2 * p + 2, :], prod[:, p % 2, :, :],
                                  act_hi[:, 2 * p:2 * p + 2, :].bitcast(F32), ALU.subtract).then_inc(act_lo_ready, 1)
            postnorm("ffnpost", "dn", 2)


def kernel(**inputs):
    import numpy as _np
    import concourse.bacc as _bacc
    from concourse import mybir as _mybir
    from concourse.bass_utils import run_bass_kernel_spmd as _run

    nc = _bacc.Bacc("TRN2", target_bir_lowering=False, num_devices=1)
    arrays, aps = {}, {}
    for name, value in list(inputs.items()) + [("shape_constants", constants())]:
        v = _np.ascontiguousarray(value)
        if v.ndim > 1 and v.shape[0] == 1:
            v = v.reshape(v.shape[1:])
        arrays[name + "_dram"] = v
        aps[name] = nc.dram_tensor(name + "_dram", v.shape, _mybir.dt.from_np(v.dtype), kind="ExternalInput").ap()
    aps["ret_decay"] = aps["ret_decay"].rearrange("a b -> (a b)")
    out = nc.dram_tensor("out_dram", (1, TOK, D), F32, kind="ExternalOutput").ap()
    build(nc, aps, aps["shape_constants"], out)
    r = _run(nc, [arrays], core_ids=[0])
    return r.results[0]["out_dram"]
```
